# Optimizing a Trainium2 kernel written in Bass

```python
import math
import jax
import jax.numpy as jnp
from jax import lax
import numpy as np

D_MODEL = 1024
BATCH = 1
SEQ = 256
DEPTH = 1
DEC_BATCH = 8
DEC_SEQ = 8
PAST_LEN = 2048
PAGE_SIZE = 128

HEAD_DIM = 64
MIX_WIDTH = D_MODEL
CONV_CH = MIX_WIDTH // 4
CONV_K = 31
NSA_HEADS = MIX_WIDTH // 2 // HEAD_DIM
NSA_KV_HEADS = max(1, NSA_HEADS // 4)
GQA_GROUP = NSA_HEADS // NSA_KV_HEADS
CMP_BLOCK = 64
SEL_BLOCK = 64
N_SEL = 16
WINDOW = 512
Q_BLOCK = 64
FORCE_SCORE = 1e4
RET_HEADS = MIX_WIDTH // 4 // HEAD_DIM
RET_CHUNK = 128
N_EXPERTS = 32
TOP_K = 4
D_FF = D_MODEL
SWIGLU_LIMIT = 7.0
SWIGLU_ALPHA = 1.702
MOE_BLOCK = 128
PLE_DIM = 256
DEEPNORM_ALPHA = (2 * DEPTH) ** 0.25
DEEPNORM_BETA = (8 * DEPTH) ** -0.25
LN_EPS = 1e-5
NEG_INF = -1e30
TINY = 1e-30
COL_CONV = 2 * CONV_CH
COL_Q = NSA_HEADS * HEAD_DIM
COL_KV = 6 * NSA_KV_HEADS * HEAD_DIM
COL_GATE = 3 * NSA_HEADS
COL_RET = 4 * RET_HEADS * HEAD_DIM
IN_COLS = COL_CONV + COL_Q + COL_KV + COL_GATE + COL_RET

kernel_name = 'hybrid_conv_nsa_retention_moe_decoder_step'

def layer_norm(x, g, b):
    xf = x.astype(jnp.float32)
    mu = xf.mean(-1, keepdims=True)
    var = jnp.square(xf - mu).mean(-1, keepdims=True)
    return ((xf - mu) * lax.rsqrt(var + LN_EPS) * g + b).astype(x.dtype)

def masked_softmax(s, mask):
    s = jnp.where(mask, s, NEG_INF)
    s = s - s.max(axis=-1, keepdims=True)
    p = jnp.where(mask, jnp.exp(s), 0.0)
    return p / jnp.maximum(p.sum(-1, keepdims=True), TINY)

def alibi_slopes(n):
    return jnp.exp2(-8.0 * jnp.arange(1, n + 1, dtype=jnp.float32) / n)

def conformer_conv(u, s0, conv_w, conv_b, ln_g, ln_b):
    a, g = jnp.split(u, 2, axis=-1)
    h = a * jax.nn.sigmoid(g)
    full = jnp.concatenate([s0.astype(h.dtype), h], axis=1)
    y = lax.conv_general_dilated(full, conv_w[:, None, :].astype(h.dtype), window_strides=(1,), padding='VALID',
                                 dimension_numbers=('NWC', 'WIO', 'NWC'), feature_group_count=CONV_CH)
    y = layer_norm(y + conv_b, ln_g, ln_b)
    return jax.nn.silu(y.astype(jnp.float32)).astype(u.dtype), full[:, -(CONV_K - 1):]

def retention(q, k, v, s0):
    B, T = q.shape[:2]
    C = math.gcd(T, RET_CHUNK)
    n = T // C
    log_g = jnp.log1p(-jnp.exp2(-5.0 - jnp.arange(RET_HEADS, dtype=jnp.float32)))
    i = jnp.arange(C, dtype=jnp.float32)
    diff = i[:, None] - i[None, :]
    dmask = jnp.exp(jnp.where(diff >= 0, log_g[:, None, None] * diff, -jnp.inf))
    q_dec = jnp.exp(log_g[None, :] * (i[:, None] + 1.0))
    k_dec = jnp.exp(log_g[None, :] * (C - 1.0 - i[:, None]))
    c_dec = jnp.exp(log_g * C)

    def step(S, inp):
        qc, kc, vc = inp
        att = jnp.einsum('bihd,bjhd->bhij', qc, kc) * dmask
        o = (jnp.einsum('bhij,bjhe->bihe', att, vc)
             + jnp.einsum('bihd,bhde->bihe', qc, S) * q_dec[None, :, :, None])
        S = S * c_dec[None, :, None, None] + jnp.einsum('bjhd,bjhe->bhde', kc * k_dec[None, :, :, None], vc)
        return S, o

    xs = tuple(a.reshape(B, n, C, RET_HEADS, HEAD_DIM).swapaxes(0, 1) for a in (q, k, v))
    S, o = lax.scan(step, s0, xs)
    return o.swapaxes(0, 1).reshape(B, T, RET_HEADS, HEAD_DIM), S

def nsa_attention(q, kv_full, win_full, gate_logits, q_start):
    f32 = jnp.float32
    B, T = q.shape[:2]
    L = kv_full.shape[1]
    KV, G, HD = NSA_KV_HEADS, GQA_GROUP, HEAD_DIM
    n_cmp = L // CMP_BLOCK
    n_blk = -(-L // SEL_BLOCK)
    k_sel = min(N_SEL, n_blk)
    qc = math.gcd(T, Q_BLOCK)
    n_qc = T // qc
    slopes = alibi_slopes(NSA_HEADS).reshape(KV, G)[None, :, :, None, None]
    cmp = kv_full[:, :n_cmp * CMP_BLOCK, :2].astype(f32).reshape(B, n_cmp, CMP_BLOCK, 2, KV, HD).mean(axis=2)
    k_cmp, v_cmp = cmp[:, :, 0], cmp[:, :, 1]
    cmp_end = (jnp.arange(n_cmp) + 1) * CMP_BLOCK - 1
    sel = jnp.pad(kv_full[:, :, 2:], ((0, 0), (0, n_blk * SEL_BLOCK - L), (0, 0), (0, 0), (0, 0)))
    sel = sel.reshape(B, n_blk, SEL_BLOCK, 2, KV, HD).transpose(3, 0, 4, 1, 2, 5)
    k_blk, v_blk = sel[0], sel[1]
    gather = jax.vmap(jax.vmap(lambda blocks, idx: blocks[idx]))

    def chunk(args):
        q_c, g_c, c = args
        t = q_start + c * qc + jnp.arange(qc)
        qg = (q_c.astype(f32) * HD ** -0.5).reshape(B, qc, KV, G, HD)
        s = jnp.einsum('bqkgd,bnkd->bkgqn', qg, k_cmp) - slopes * (t[:, None] - cmp_end[None, :]).astype(f32)
        p_cmp = masked_softmax(s, cmp_end[None, :] <= t[:, None])
        o_cmp = jnp.einsum('bkgqn,bnkd->bqkgd', p_cmp, v_cmp)
        imp = jnp.pad(p_cmp.sum(axis=2), ((0, 0), (0, 0), (0, 0), (0, n_blk - n_cmp)))
        blk = jnp.arange(n_blk)[None, :]
        cur = (t // SEL_BLOCK)[:, None]
        forced = (blk == 0) | (blk == cur) | (blk == cur - 1)
        score = jnp.where(blk <= cur, jnp.where(forced, FORCE_SCORE, imp), -1.0)
        top_s, top_i = lax.top_k(score, k_sel)
        kg = gather(k_blk, top_i).astype(f32)
        vg = gather(v_blk, top_i).astype(f32)
        pos = top_i[..., None] * SEL_BLOCK + jnp.arange(SEL_BLOCK)
        m_sel = (top_s[..., None] >= 0) & (pos <= t[:, None, None])
        dist = (t[:, None, None] - pos).astype(f32)[:, :, None]
        s = jnp.einsum('bqkgd,bkqnsd->bkgqns', qg, kg) - slopes[..., None] * dist
        p = masked_softmax(s.reshape(B, KV, G, qc, k_sel * SEL_BLOCK),
                           m_sel.reshape(B, KV, 1, qc, k_sel * SEL_BLOCK))
        o_sel = jnp.einsum('bkgqns,bkqnsd->bqkgd', p.reshape(B, KV, G, qc, k_sel, SEL_BLOCK), vg)
        wk = lax.dynamic_slice_in_dim(win_full, c * qc, qc + WINDOW, axis=1).astype(f32)
        pw = q_start - WINDOW + c * qc + jnp.arange(qc + WINDOW)
        dw = t[:, None] - pw[None, :]
        m_win = (dw >= 0) & (dw < WINDOW) & (pw[None, :] >= 0)
        s = jnp.einsum('bqkgd,bskd->bkgqs', qg, wk[:, :, 0]) - slopes * dw.astype(f32)
        p = masked_softmax(s, m_win)
        o_win = jnp.einsum('bkgqs,bskd->bqkgd', p, wk[:, :, 1])
        g = jax.nn.sigmoid(g_c.astype(f32)).reshape(B, qc, KV, G, 3)
        o = g[..., 0:1] * o_cmp + g[..., 1:2] * o_sel + g[..., 2:3] * o_win
        return o.reshape(B, qc, NSA_HEADS * HD)

    q_chunks = q.reshape(B, n_qc, qc, NSA_HEADS, HD).swapaxes(0, 1)
    g_chunks = gate_logits.reshape(B, n_qc, qc, NSA_HEADS, 3).swapaxes(0, 1)
    out = lax.map(chunk, (q_chunks, g_chunks, jnp.arange(n_qc)))
    return out.swapaxes(0, 1).reshape(B, T, NSA_HEADS * HD).astype(q.dtype)

def moe_ffn(h2d, w_router, b_router, w_up, b_up, w_down, b_down):
    N, D = h2d.shape
    logits = jnp.dot(h2d.astype(jnp.float32), w_router.astype(jnp.float32)) + b_router
    top_v, top_e = lax.top_k(logits, TOP_K)
    gate = jax.nn.softmax(top_v, axis=-1)
    NK = N * TOP_K
    flat_e = top_e.reshape(NK)
    order = jnp.argsort(flat_e)
    se = flat_e[order]
    stok = order // TOP_K
    sgate = gate.reshape(NK)[order]
    counts = jnp.bincount(flat_e, length=N_EXPERTS)
    starts = jnp.cumsum(counts) - counts
    padded = (counts + MOE_BLOCK - 1) // MOE_BLOCK * MOE_BLOCK
    pend = jnp.cumsum(padded)
    pstart = pend - padded
    dest = pstart[se] + jnp.arange(NK) - starts[se]
    n_blocks = -(-(NK + N_EXPERTS * (MOE_BLOCK - 1)) // MOE_BLOCK)
    R = n_blocks * MOE_BLOCK
    row_tok = jnp.full((R,), N, jnp.int32).at[dest].set(stok)
    row_gate = jnp.zeros((R,), jnp.float32).at[dest].set(sgate)
    block_e = jnp.minimum(jnp.searchsorted(pend, jnp.arange(n_blocks) * MOE_BLOCK, side='right'), N_EXPERTS - 1)
    xpad = jnp.concatenate([h2d, jnp.zeros((1, D), h2d.dtype)], axis=0)
    xb = xpad[row_tok].reshape(n_blocks, MOE_BLOCK, D)

    def expert_block(args):
        xblk, e = args
        hu = jnp.dot(xblk, w_up[e]) + b_up[e]
        g = jnp.minimum(hu[:, 0::2], SWIGLU_LIMIT)
        u = jnp.clip(hu[:, 1::2], -SWIGLU_LIMIT, SWIGLU_LIMIT)
        act = (u + 1.0) * g * jax.nn.sigmoid(SWIGLU_ALPHA * g)
        return jnp.dot(act, w_down[e]) + b_down[e]

    yb = lax.map(expert_block, (xb, block_e)).reshape(R, D)
    out = jnp.zeros((N + 1, D), jnp.float32).at[row_tok].add(yb.astype(jnp.float32) * row_gate[:, None])
    return out[:N].astype(h2d.dtype)

def decoder_layer(x, p, past_kv, win_prefix, ret_s0, conv_s0, q_start, n_win_keep,
                  w_in, w_out, conv_w, conv_b, conv_ln_g, conv_ln_b, ret_norm_g, ln1_g, ln1_b,
                  w_router, b_router, w_up, b_up, w_down, b_down, w_ple, w_plg, ln2_g, ln2_b):
    B, T, _ = x.shape
    u = jnp.einsum('btd,dc->btc', x, w_in)
    cuts = [COL_CONV, COL_CONV + COL_Q, COL_CONV + COL_Q + COL_KV, COL_CONV + COL_Q + COL_KV + COL_GATE]
    u_conv, u_q, u_kv, u_gate, u_ret = jnp.split(u, cuts, axis=-1)
    conv_out, conv_state = conformer_conv(u_conv, conv_s0, conv_w, conv_b, conv_ln_g, conv_ln_b)
    q = u_q.reshape(B, T, NSA_HEADS, HEAD_DIM)
    kv_new = u_kv.reshape(B, T, 6, NSA_KV_HEADS, HEAD_DIM)
    paged_new = kv_new[:, :, :4]
    kv_full = jnp.concatenate([past_kv.astype(kv_new.dtype), paged_new], axis=1)
    win_full = jnp.concatenate([win_prefix.astype(kv_new.dtype), kv_new[:, :, 4:]], axis=1)
    nsa_out = nsa_attention(q, kv_full, win_full, u_gate.reshape(B, T, NSA_HEADS, 3), q_start)
    rq, rk, rv, rg = jnp.split(u_ret.astype(jnp.float32), 4, axis=-1)
    rs = (B, T, RET_HEADS, HEAD_DIM)
    ret_o, ret_state = retention(rq.reshape(rs), rk.reshape(rs) * HEAD_DIM ** -0.5, rv.reshape(rs),
                                 ret_s0.astype(jnp.float32))
    mu = ret_o.mean(-1, keepdims=True)
    var = jnp.square(ret_o - mu).mean(-1, keepdims=True)
    ret_o = ((ret_o - mu) * lax.rsqrt(var + LN_EPS)).reshape(B, T, RET_HEADS * HEAD_DIM) * ret_norm_g
    ret_out = (jax.nn.silu(rg) * ret_o).astype(x.dtype)
    mixed = jnp.concatenate([conv_out, nsa_out, ret_out], axis=-1)
    h = layer_norm(DEEPNORM_ALPHA * x + jnp.einsum('btc,cd->btd', mixed, w_out), ln1_g, ln1_b)
    ffn = moe_ffn(h.reshape(B * T, D_MODEL), w_router, b_router, w_up, b_up, w_down, b_down).reshape(B, T, D_MODEL)
    ple = jnp.einsum('btp,pd->btd', p, w_ple) * jax.nn.sigmoid(jnp.einsum('btd,de->bte', h, w_plg))
    y = layer_norm(DEEPNORM_ALPHA * h + ffn + ple, ln2_g, ln2_b)
    return y, paged_new, win_full[:, -n_win_keep:], ret_state, conv_state

def setup_inputs(seed: int = 0) -> dict:
    key = jax.random.key(seed)
    ks = jax.random.split(key, 32)
    f32 = jnp.float32
    n_pages = PAST_LEN // PAGE_SIZE
    n_pool = (DEC_BATCH * n_pages * 5 + 3) // 4
    wbuf = min(WINDOW, PAST_LEN)

    def nrm(k, shape, scale):
        return jax.random.normal(k, shape, f32) * scale

    page_table = jax.random.permutation(ks[8], n_pool)[:DEC_BATCH * n_pages].reshape(DEC_BATCH, n_pages).astype(jnp.int32)
    return {
        'x_prompt': nrm(ks[0], (BATCH, SEQ, D_MODEL), 1.0),
        'x_sample': nrm(ks[1], (DEC_BATCH, DEC_SEQ, D_MODEL), 1.0),
        'p_prompt': nrm(ks[2], (DEPTH, BATCH, SEQ, PLE_DIM), 1.0),
        'p_sample': nrm(ks[3], (DEPTH, DEC_BATCH, DEC_SEQ, PLE_DIM), 1.0),
        'cache_nsa_kv': nrm(ks[4], (DEPTH, n_pool, PAGE_SIZE, 4, NSA_KV_HEADS, HEAD_DIM), 1.0),
        'cache_win_kv': nrm(ks[5], (DEPTH, DEC_BATCH, wbuf, 2, NSA_KV_HEADS, HEAD_DIM), 1.0),
        'state_ret': nrm(ks[6], (DEPTH, DEC_BATCH, RET_HEADS, HEAD_DIM, HEAD_DIM), 1.0),
        'state_conv': nrm(ks[7], (DEPTH, DEC_BATCH, CONV_K - 1, CONV_CH), 0.5),
        'page_table': page_table,
        'w_in': nrm(ks[9], (DEPTH, D_MODEL, IN_COLS), D_MODEL ** -0.5),
        'w_out': nrm(ks[10], (DEPTH, MIX_WIDTH, D_MODEL), MIX_WIDTH ** -0.5 * DEEPNORM_BETA),
        'conv_w': nrm(ks[11], (DEPTH, CONV_K, CONV_CH), CONV_K ** -0.5),
        'conv_b': nrm(ks[12], (DEPTH, CONV_CH), 0.02),
        'conv_ln_g': 1.0 + nrm(ks[13], (DEPTH, CONV_CH), 0.02),
        'conv_ln_b': nrm(ks[14], (DEPTH, CONV_CH), 0.02),
        'ret_norm_g': 1.0 + nrm(ks[15], (DEPTH, RET_HEADS * HEAD_DIM), 0.02),
        'ln1_g': 1.0 + nrm(ks[16], (DEPTH, D_MODEL), 0.02),
        'ln1_b': nrm(ks[17], (DEPTH, D_MODEL), 0.02),
        'w_router': nrm(ks[18], (DEPTH, D_MODEL, N_EXPERTS), D_MODEL ** -0.5),
        'b_router': nrm(ks[19], (DEPTH, N_EXPERTS), 0.01),
        'w_up': nrm(ks[20], (DEPTH, N_EXPERTS, D_MODEL, 2 * D_FF), D_MODEL ** -0.5),
        'b_up': nrm(ks[21], (DEPTH, N_EXPERTS, 2 * D_FF), 0.02),
        'w_down': nrm(ks[22], (DEPTH, N_EXPERTS, D_FF, D_MODEL), D_FF ** -0.5 * DEEPNORM_BETA),
        'b_down': nrm(ks[23], (DEPTH, N_EXPERTS, D_MODEL), 0.02),
        'w_ple': nrm(ks[24], (DEPTH, PLE_DIM, D_MODEL), PLE_DIM ** -0.5 * DEEPNORM_BETA),
        'w_plg': nrm(ks[25], (DEPTH, D_MODEL, D_MODEL), D_MODEL ** -0.5),
        'ln2_g': 1.0 + nrm(ks[26], (DEPTH, D_MODEL), 0.02),
        'ln2_b': nrm(ks[27], (DEPTH, D_MODEL), 0.02),
    }

def reference(x_prompt, x_sample, p_prompt, p_sample, cache_nsa_kv, cache_win_kv, state_ret, state_conv, page_table,
              w_in, w_out, conv_w, conv_b, conv_ln_g, conv_ln_b, ret_norm_g, ln1_g, ln1_b,
              w_router, b_router, w_up, b_up, w_down, b_down, w_ple, w_plg, ln2_g, ln2_b):
    bp, seq = x_prompt.shape[:2]
    dec_b, n_pages = page_table.shape
    past_len = n_pages * PAGE_SIZE
    wbuf = cache_win_kv.shape[2]
    dt = x_prompt.dtype
    zeros_kv = jnp.zeros((bp, 0, 4, NSA_KV_HEADS, HEAD_DIM), dt)
    zeros_win = jnp.zeros((bp, WINDOW, 2, NSA_KV_HEADS, HEAD_DIM), dt)
    zeros_ret = jnp.zeros((bp, RET_HEADS, HEAD_DIM, HEAD_DIM), jnp.float32)
    zeros_conv = jnp.zeros((bp, CONV_K - 1, CONV_CH), dt)
    hp, hs = x_prompt, x_sample
    kvp, kvs, wp, ws, rp, rs, cp, cs = [], [], [], [], [], [], [], []
    for i in range(DEPTH):
        lw = (w_in[i], w_out[i], conv_w[i], conv_b[i], conv_ln_g[i], conv_ln_b[i], ret_norm_g[i], ln1_g[i], ln1_b[i],
              w_router[i], b_router[i], w_up[i], b_up[i], w_down[i], b_down[i], w_ple[i], w_plg[i], ln2_g[i], ln2_b[i])
        hp, a_kv, a_win, a_ret, a_conv = decoder_layer(hp, p_prompt[i], zeros_kv, zeros_win, zeros_ret, zeros_conv,
                                                       0, min(WINDOW, seq), *lw)
        past = cache_nsa_kv[i, page_table].reshape(dec_b, past_len, 4, NSA_KV_HEADS, HEAD_DIM)
        win_prefix = jnp.pad(cache_win_kv[i], ((0, 0), (WINDOW - wbuf, 0), (0, 0), (0, 0), (0, 0)))
        hs, b_kv, b_win, b_ret, b_conv = decoder_layer(hs, p_sample[i], past, win_prefix, state_ret[i], state_conv[i],
                                                       past_len, wbuf, *lw)
        kvp.append(a_kv); kvs.append(b_kv); wp.append(a_win); ws.append(b_win)
        rp.append(a_ret); rs.append(b_ret); cp.append(a_conv); cs.append(b_conv)
    return (hp, hs, jnp.stack(kvp), jnp.stack(kvs), jnp.stack(wp), jnp.stack(ws),
            jnp.stack(rp), jnp.stack(rs), jnp.stack(cp), jnp.stack(cs))


_drawn_inputs = setup_inputs


def setup_inputs(seed=0):
    import zlib

    import numpy as np

    out = dict(_drawn_inputs(seed))
    spreads = {}
    factors = {'conv_b': 3.744,
     'conv_ln_g': 6.146,
     'conv_ln_b': 4.22,
     'ret_norm_g': 7.411,
     'b_router': 3.173,
     'b_up': 8.0,
     'b_down': 6.57,
     'ln2_g': 2.78,
     'ln2_b': 3.118}
    for name, (base, spread) in spreads.items():
        noise = np.random.default_rng([zlib.crc32(name.encode()), seed]).standard_normal(out[name].shape)
        drawn = base * np.exp(spread * noise) if base else spread * noise
        out[name] = jnp.asarray(drawn.astype(out[name].dtype))
    for name, factor in factors.items():
        out[name] = (out[name] * factor).astype(out[name].dtype)
    return out
```

```python
import math

F = 4
D, NPR, NB, TS = 1024, 256, 8, 8
NSM = NB * TS
NT = NPR + NSM
KT = D // 128
HD, HEADS, KV, GQ = 64, 8, 2, 4
PAST, PAGE = 2048, 128
NPG = PAST // PAGE
WIN = 512
RH, CC, CK = 4, 256, 31
NE, TOPK, FF, PLE = 32, 4, 1024, 256
CAP = 128
ROUNDS = -(-NT // CAP)
ALPHA = 2 ** 0.25
EPS, TINY, NEG = 1e-5, 1e-30, -1e30
LIMIT, SALPHA = 7.0, 1.702
MT = [128, 128, 64]
TQ, TCK, TSK, TWK, TRQ, TRK, TA, TG, TCV, TSV, TWV, TGATE, TRV, TRG = 0, 4, 5, 6, 7, 9, 11, 13, 15, 16, 17, 18, 19, 21
NTILE = 23


def const_layout():
    sizes = dict(ident=128, lower=128, ones=128, headsum=128, iota=128, kdec=RH, kdec_s=RH,
                 cdec=2, cdec_s=2, bmask=NB, tabwin=WIN, tabsel=WIN, chunkbase=4, tabnew=4 * 128,
                 tabcmp=32, pick=4 * 128, headmask=24, distp=384, distcmp=2 * 4)
    late = dict(dmask=RH * 128, dmask_s=RH * 64, qdec=2 * 128, qmask=2 * NB * 64)
    out, ends = {}, []
    for group in (sizes, late):
        at = 0
        for k, n in group.items():
            out[k] = (at, n)
            at += n
        ends.append(at)
    return out, ends[0], ends[1], set(late)


def constants():
    import numpy as np
    lay, n, n_late, late = const_layout()
    early, retention = np.zeros((128, n), np.float32), np.zeros((128, n_late), np.float32)

    def put(name, a):
        a = np.asarray(a, np.float64).reshape(a.shape[0], -1)
        o, w = lay[name]
        c = retention if name in late else early
        assert a.shape[1] == w, (name, a.shape, w)
        c[:a.shape[0], o:o + w] = a.astype(np.float32)

    p = np.arange(128)
    put("ident", np.eye(128))
    put("lower", (p[:, None] < p[None, :]) * 1.0)
    put("ones", np.ones((128, 128)))
    r = p
    b2, g, i, t = r // 64, r // 32 % 2, r // 8 % 4, r % 8
    put("headsum", ((b2[:, None] == b2) & (g[:, None] == g) & (t[:, None] == t)) * 1.0)
    put("iota", np.tile(np.arange(128.0), (128, 1)))
    lg = np.log1p(-np.exp2(-5.0 - np.arange(RH)))
    d = p[None, :] - p[:, None]
    put("dmask", np.stack([np.where(d >= 0, np.exp(lg[h] * np.maximum(d, 0)), 0) for h in range(RH)], 1))
    q = np.arange(64)
    ds = q[None, :] - q[:, None]
    same = (q[None, :] // 8 == q[:, None] // 8) & (ds >= 0)
    put("dmask_s", np.stack([np.where(same, np.exp(lg[h] * np.maximum(ds, 0)), 0) for h in range(RH)], 1))
    hp = p // 64
    put("qdec", np.stack([np.exp(lg[2 * k + hp][:, None] * (np.arange(128) + 1.0)) for k in range(2)], 1))
    put("kdec", np.exp(lg[None, :] * (127.0 - p[:, None])))
    put("kdec_s", np.exp(lg[None, :] * (7.0 - (q % 8)[:, None])))
    put("cdec", np.stack([np.exp(lg[2 * k + hp] * 128) for k in range(2)], 1))
    put("cdec_s", np.stack([np.exp(lg[2 * k + hp] * 8) for k in range(2)], 1))
    put("bmask", (q[:, None] // 8 == np.arange(8)) * 1.0)
    qm = np.stack([np.exp(lg[2 * k + hp][:, None] * (q % 8 + 1.0)) for k in range(2)], 1)
    put("qmask", qm[:, :, None, :] * (np.arange(8)[:, None] == q // 8)[None, None])
    slope = np.exp2(-1.0 * (g * 4 + i + 1))
    ts = PAST + t
    near = ts[:, None] - (PAST - WIN + np.arange(WIN))[None, :]
    put("tabwin", np.where(near < WIN, -slope[:, None] * near, NEG))
    put("tabsel", -slope[:, None] * near)
    put("chunkbase", slope[:, None] * 512.0 * (np.arange(4) - 3)[None, :])
    new = []
    for k in range(4):
        ok = (q[None, :] // 8 == (2 * k + b2)[:, None]) & ((q % 8)[None, :] <= t[:, None])
        new.append(np.tile(np.where(ok, -slope[:, None] * (t[:, None] - (q % 8)[None, :]), NEG), (1, 2)))
    put("tabnew", np.stack(new, 1))
    put("tabcmp", -slope[:, None] * (ts[:, None] - ((np.arange(32) + 1) * 64 - 1)[None, :]))
    put("pick", np.stack([(q[:, None] == ((2 * k + b2) * 8 + t)[None, :]) * 1.0 for k in range(4)], 1))
    put("headmask", np.repeat((np.arange(8)[None, :] == (g * 4 + i)[:, None]) * 1.0, 3, 1))
    far = 1e33
    k0, k1 = p[None, :], np.arange(256)[None, :]
    d0, d1 = p[:, None] - k0, 128 + p[:, None] - k1
    put("distp", np.concatenate([np.where(d0 >= 0, d0, far), np.where(d1 >= 0, d1, far)], 1))
    ce = (np.arange(4) + 1) * 64 - 1
    dc = np.arange(256)[:, None] - ce[None, :]
    dc = np.where(dc >= 0, dc, far)
    put("distcmp", np.stack([dc[:128], dc[128:]], 1))
    return early, retention


def jobs():
    out = [("proj", j) for j in range(NTILE)]
    out += [(w, m) for m in range(3) for w in ("rowsA", "rowsB", "rowsC", "rowsD")]
    out += [("gates",)]
    for p in range(4):
        out += [("vc", p), ("sc", p), ("imp", p)] + [("sw", p, c) for c in range(6)]
        out += [("pt", p, q) for q in range(6)] + [("o", p)]
    out += [("pcv",)]
    for qi in range(2):
        out += [("pc", qi, 0), ("pc", qi, 1), ("ps", qi, 0), ("ps", qi, 4), ("pct", qi, 0), ("pct", qi, 1)]
        for i in range(4):
            if i < 3:
                out += [("ps", qi, i + 1), ("ps", qi, i + 5)]
            out += [("ppt", qi, i), ("ppt", qi, i + 4), ("po", qi, i)]
    for c in range(3):
        out += [("att", c, 0), ("att", c, 1), ("ro", c, 0), ("ro", c, 1)]
        out += [("rS", c)] if c < 2 else [("ri", 0), ("ri", 1), ("rS_s", 0), ("rS_s", 1)]
    out += [("cv", m) for m in range(3)] + [("mx", m) for m in range(3)]
    out += [("wo", m, c) for m in range(3) for c in range(2)]
    out += [("hT", m, c) for m in range(3) for c in range(2)]
    out += [("router", m) for m in range(3)]
    out += [(w, m, c) for m in range(3) for c in range(2) for w in ("plg", "ple")]
    out += [("rank", m) for m in range(3)] + [("count",), ("GT",)]
    out += [("bd", m, c) for m in range(3) for c in range(2)]
    return {n: k for k, n in enumerate(out)}


def build(nc, A, O):
    from contextlib import ExitStack
    import concourse.bass as bass
    from concourse import mybir

    f32, i32, u32 = mybir.dt.float32, mybir.dt.int32, mybir.dt.uint32
    ALU, ACT, AX = mybir.AluOpType, mybir.ActivationFunctionType, mybir.AxisListType.X
    MUL, ADD, SUB, MAXOP = ALU.mult, ALU.add, ALU.subtract, ALU.max
    JOB = jobs()
    LAY, NCONST, NLATE, LATE = const_layout()
    TE, VE, SE, GE = nc.tensor, nc.vector, nc.scalar, nc.gpsimd
    ctx = ExitStack()
    with ctx:
        def sem(name):
            return ctx.enter_context(nc.semaphore(name))

        def many(name, n):
            return [sem(f"{name}{k}") for k in range(n)]

        SIZE = 52960
        arena = ctx.enter_context(nc.sbuf_tensor("arena", [128, SIZE], f32))
        page_ids = ctx.enter_context(nc.sbuf_tensor("page_ids", [1, NB * NPG], i32))
        items_i = ctx.enter_context(nc.sbuf_tensor("items_i", [1, 1], i32))
        top_i = ctx.enter_context(nc.sbuf_tensor("top_i", [128, 3, 8], u32))
        conv_w = ctx.enter_context(nc.sbuf_tensor("conv_w", [128, 2, CK + 1], f32))
        psum = ctx.enter_context(nc.psum_tensor("psum", [128, 8, 512], f32))

        def split(a, dims):
            if len(dims) == 1:
                return a
            names = "abcd"[:len(dims)]
            return a.rearrange(f"p ({' '.join(names)}) -> p {' '.join(names)}",
                               **{x: d for x, d in zip(names, dims)})

        class Cut:

            def __init__(self, at, end):
                self.at, self.end = at, end

            def take(self, *dims):
                a = arena[:, self.at:self.at + math.prod(dims)]
                self.at += math.prod(dims)
                assert self.at <= self.end, (dims, self.at, self.end)
                return split(a, dims)

        SLOT = 2048
        U0 = 12 * SLOT
        C0 = U0 + NTILE * NT
        R0 = C0 + NCONST
        M0 = R0 + 3 * (768 + 24 + 768)
        X0 = M0 + KT * NT
        wslot = Cut(0, U0).take(12, SLOT)
        kvslot = Cut(0, U0).take(3, NPG, 4, 128)
        w_out = Cut(0, 4 * SLOT).take(KT, D)
        w_plg = Cut(4 * SLOT, 8 * SLOT).take(KT, D)
        w_ple = Cut(8 * SLOT, 9 * SLOT).take(2, D)
        late_sb = arena[:, 9 * SLOT:9 * SLOT + NLATE]
        retc = Cut(10 * SLOT, 12 * SLOT)
        s_in, v_wide, q_wide = retc.take(2, NB, 64), retc.take(RH, NB, 64), retc.take(2, NB, 64)
        uT = Cut(U0, C0).take(NTILE, NT)
        early_sb = arena[:, C0:C0 + NCONST]

        def const(name, *dims):
            o, n = LAY[name]
            return split((late_sb if name in LATE else early_sb)[:, o:o + n], dims or (n,))

        ident, ones = const("ident"), const("ones")
        rc = Cut(R0, M0)
        kvR = rc.take(3, 6, 128)
        gateR = rc.take(3, 24)
        rvR, rgR, rkR = rc.take(3, 256), rc.take(3, 256), rc.take(3, 256)
        xT = Cut(M0, X0).take(KT, NT)
        mixT = Cut(M0, X0).take(KT, NT)
        hT = mixT
        xc = Cut(X0, SIZE)
        win = xc.take(3, 2, 512)
        w_in = Cut(xc.at, SIZE).take(4, KT, 128)
        PT = xc.take(22, 128)
        xc.at = max(xc.at, X0 + 3072 + 4096)
        convP, convS, convY = xc.take(2, CK - 1 + NPR), xc.take(2, NB, CK - 1 + TS), xc.take(2, NT)
        vecs = xc.take(3, CC)
        cm, vcr = xc.take(2, 2, 32), xc.take(2, 128)
        pc2 = Cut(X0, X0 + 3072 + 4096)
        Sp, PTp = pc2.take(4, 2, 256), pc2.take(4, 4, 128)
        pcT, vcp = pc2.take(8, 128), pc2.take(128)
        pcs = pc2.take(8, 4)
        sm = xc
        cmp_p = sm.take(2, 4)
        pcm, pgc, score, score2, score3 = sm.take(32), sm.take(32), sm.take(40), sm.take(40), sm.take(40)
        selb, st = sm.take(32), sm.take(32)
        gsig, gs, gtmp = sm.take(3, 24), sm.take(4, 3), split(PT[:, 0, 0:96], (4, 24))
        mx, nmx, sums, fac = sm.take(4), sm.take(4), sm.take(4), sm.take(4)
        t8a, t8b = sm.take(8), sm.take(8)
        mxp, nmxp, sump, facp = sm.take(4, 2), sm.take(4, 2), sm.take(4, 2), sm.take(4, 2)
        mc8, sc8 = sm.take(8), sm.take(8)
        stats, mv, rstd = sm.take(4, 6), sm.take(4, 2), sm.take(4)
        su = Cut(U0 + 11 * NT, C0)
        S, Qbd, Vnew = su.take(2688), su.take(NB, 64), su.take(128)
        ru = Cut(U0 + 11 * NT, C0)
        attT, q_dec, kd = ru.take(RH, 128), ru.take(2, 128), ru.take(256)
        S1, S2 = ru.take(2, 64), ru.take(2, 64)
        retR, convR, sig = ru.take(3, 256), ru.take(3, 256), ru.take(3, 256)
        conv_t = Cut(C0 - NPR, C0).take(NPR)
        assert ru.at <= C0 - NPR and su.at <= C0 - NPR
        acc = Cut(U0, C0).take(3, D)
        h = Cut(U0 + 3 * D, C0).take(3, D)
        ln = Cut(R0, M0).take(4, D)
        ec = Cut(X0, SIZE)
        wr, br, pT = ec.take(KT, NE), ec.take(NE), ec.take(2, NT)
        bup = ec.take(NE, 16)
        NI = ROUNDS * NE
        rank_all, gate_all = ec.take(3, NI + 8), ec.take(3, NI + 8)
        Mk, G = ec.take(3, NE), ec.take(3, NE)
        lg, etmp, top8, idxf, g4 = ec.take(NE), ec.take(NE), ec.take(8), ec.take(8), ec.take(8)
        r1 = ec.take(8)
        stats2, mv2, rstd2 = ec.take(2, 6), ec.take(2), ec.take(1)
        P, PG, PGT = ec.take(3, CAP), ec.take(3, CAP), ec.take(384)
        xg, hu, y = ec.take(KT, CAP), ec.take(2 * FF), ec.take(D)
        gg, uu = ec.take(8, CAP), ec.take(8, CAP)
        act_sb = Cut(U0 + 6 * D, C0).take(8, CAP)
        bdn = hu[:, 0:D]
        sg = hu[:, D:2 * D]
        GTs = y[:, 0:NT]
        assert ec.at <= SIZE

        bank_full, bank_free = many("bank_full", 8), many("bank_free", 8)
        const_in, late_in, x_in, ids_in = sem("const_in"), sem("late_in"), sem("x_in"), sem("ids_in")
        w_in_here, kv_here = many("w_in_here", 4), many("kv_here", 3)
        conv_in, vec_in, wout_in, plg_in, ple_in = sem("conv_in"), sem("vec_in"), sem("wout_in"), sem("plg_in"), sem("ple_in")
        sin_in, xrow_in, ln1_in, ln2_in, moe_in = sem("sin_in"), sem("xrow_in"), sem("ln1_in"), sem("ln2_in"), sem("moe_in")
        vnew_in = sem("vnew_in")
        conv_e, conv_ready = sem("conv_e"), sem("conv_ready")
        gsig_ready, qbd_ready = sem("gsig_ready"), sem("qbd_ready")
        means_ready, cmp_max, cmp_exp, pcm_ready = sem("means_ready"), sem("cmp_max"), sem("cmp_exp"), sem("pcm_ready")
        pgc_ready = sem("pgc_ready")
        s_max, s_exp, s_fac, s_scaled = sem("s_max"), sem("s_exp"), sem("s_fac"), sem("s_scaled")
        pmean_ready, pc_max, pc_exp, pc_ready = sem("pmean_ready"), sem("pc_max"), sem("pc_exp"), sem("pc_ready")
        p_max, p_exp, p_fac, p_scaled = sem("p_max"), sem("p_exp"), sem("p_fac"), sem("p_scaled")
        kd_ready, qd_ready, rets_ready = sem("kd_ready"), sem("qd_ready"), sem("rets_ready")
        ret_e, ret_done, convn_in, conv_sig, mix_ready = sem("ret_e"), sem("ret_done"), sem("convn_in"), sem("conv_sig"), sem("mix_ready")
        states_ready = sem("states_ready")
        h_ready, top_ready, top_exp, sig_e = sem("h_ready"), sem("top_ready"), sem("top_exp"), sem("sig_e")
        mask_ready, G_ready, items_ready, rank_ready = sem("mask_ready"), sem("G_ready"), sem("items_ready"), sem("rank_ready")
        w_here, w_used = many("w_here", 12), many("w_used", 12)
        P_ready, PG_ready, gathered, xg_ready = sem("P_ready"), sem("PG_ready"), sem("gathered"), sem("xg_ready")
        up_done, hu_ready, PG_turned, PGT_ready = sem("up_done"), sem("hu_ready"), sem("PG_turned"), sem("PGT_ready")
        hu_turned, g_ready, e_ready, act_ready = sem("hu_turned"), sem("g_ready"), sem("e_ready"), sem("act_ready")
        y_stored, var_ready, std_ready = sem("y_stored"), sem("var_ready"), sem("std_ready")
        y_ready, scattered, added, y_out = sem("y_ready"), sem("scattered"), sem("added"), sem("y_out")
        rows_out, states_out, wincopy_out, conv_out = sem("rows_out"), sem("states_out"), sem("wincopy_out"), sem("conv_out")
        dve_step, act_step, pool_step, dve_loop, dve_tail = sem("dve_step"), sem("act_step"), sem("pool_step"), sem("dve_loop"), sem("dve_tail")

        def bank(job):
            return JOB[job] % 8

        def ps(job):
            return psum[:, bank(job), :]

        def full(eng, job):
            eng.wait_ge(bank_full[bank(job)], JOB[job] // 8 + 1)

        def freed(eng, job):
            eng.wait_ge(bank_free[bank(job)], JOB[job] // 8 + 1)

        def open_bank(pe, job):
            if JOB[job] >= 8:
                pe.wait_ge(bank_free[bank(job)], JOB[job] // 8)

        def steps(eng, s, start=0):
            n = [0]

            def seen(ins):
                n[0] += 1
                ins.then_inc(s, 1)
                eng.wait_ge(s, start + n[0])
            seen.count = n
            return seen

        CONV_STEPS = 2 * 2 * (1 + 2 * (CK - 1))
        NSLOPE = [-(2.0 ** -(hh + 1)) for hh in range(HEADS)]
        block = ctx.enter_context(nc.Block())

        @block.sync
        def _(sp):
            sp.dma_start(xT, A["xT"]).then_inc(x_in, 16)
            sp.dma_start(page_ids[:, :], A["page_table"]).then_inc(ids_in, 16)

            def tile_load(j):
                if j >= 4:
                    full(sp, ("proj", j - 4))
                sp.dma_start(w_in[:, j % 4], A["w_in"][j]).then_inc(w_in_here[j % 4], 16)

            def batch_load(b):
                if b >= 3:
                    full(sp, ("o", (b - 3) // 2))
                with sp.Fori(0, NPG) as k:
                    page = sp.value_load(page_ids[0:1, bass.ds(k + b * NPG, 1)], min_val=0, max_val=A["pages"].shape[0] - 1)
                    dst = wslot[:, (b % 3) * 4:(b % 3) * 4 + 4, :].rearrange("p a b -> p (a b)")
                    sp.dma_start(dst[:, bass.ds(k * 512, 512)],
                                 A["pages"][bass.ds(page, 1), :, :].rearrange("a p n -> (a p) n")).then_inc(kv_here[b % 3], 16)
                sp.dma_start(win[:, b % 3], A["windows"][b]).then_inc(kv_here[b % 3], 16)

            for j in range(4):
                tile_load(j)
            sp.dma_start(early_sb, A["early"]).then_inc(const_in, 16)
            for j in range(4, NTILE):
                tile_load(j)
                if j == 4:
                    sp.wait_ge(ids_in, 16)
                if j in (6, 11, 16):
                    batch_load((j - 6) // 5)
            for b in range(3, NB):
                batch_load(b)
            full(sp, ("o", 2))
            sp.dma_start(late_sb, A["late"]).then_inc(late_in, 16)
            sp.dma_start(s_in, A["state_ret"]).then_inc(sin_in, 16)
            sp.dma_start(w_ple, A["w_ple"]).then_inc(ple_in, 16)
            full(sp, ("o", 3))
            sp.dma_start(w_out, A["w_out"]).then_inc(wout_in, 16)
            sp.dma_start(w_plg, A["w_plg"]).then_inc(plg_in, 16)
            freed(sp, ("rS_s", 1))
            sp.dma_start(acc[:, 0:2], A["x_rows"][0:256].rearrange("(m p) d -> p m d", p=128)).then_inc(xrow_in, 16)
            sp.dma_start(acc[0:64, 2], A["x_rows"][256:320]).then_inc(xrow_in, 16)
            sp.wait_ge(rows_out, 16 * 13)
            sp.wait_ge(conv_out, 48)
            full(sp, ("mx", 2))
            sp.dma_start(ln, A["ln"]).then_inc(ln1_in, 16)
            sp.dma_start(wr, A["w_router"]).then_inc(moe_in, 16)
            sp.dma_start(br, A["b_router"]).then_inc(moe_in, 16)
            sp.dma_start(pT, A["pT"]).then_inc(moe_in, 16)
            sp.dma_start(bup, A["b_up"]).then_inc(moe_in, 16)
            sp.dma_start(bdn[0:NE, :], A["b_down"]).then_inc(moe_in, 16)

            up = A["w_up"].rearrange("e (k p) n -> e k p n", p=128)
            down = A["w_down"].rearrange("e (k a p) n -> e k p a n", p=128, a=2)

            def weights(e, c):
                if c < 8:
                    src = up[e, c] if isinstance(e, int) else up[bass.ds(e, 1), c].rearrange("e p n -> (e p) n")
                    return sp.dma_start(wslot[:, c], src).then_inc(w_here[c], 16)
                dst = wslot[:, c].rearrange("p (a n) -> p a n", a=2)
                src = down[e, c - 8] if isinstance(e, int) else down[bass.ds(e, 1), c - 8].rearrange("e p a n -> (e p) a n")
                return sp.dma_start(dst, src).then_inc(w_here[c], 16)

            full(sp, ("wo", 2, 1))
            for c in range(4):
                weights(0, c)
            full(sp, ("plg", 2, 1))
            for c in range(4, 8):
                weights(0, c)
            sp.wait_ge(states_out, 16 * 2)
            full(sp, ("ple", 2, 1))
            for c in range(8, 12):
                weights(0, c)

            def item_loads(i, e):
                for c in range(12):
                    if c == 7:
                        sp.wait_ge(up_done, i * 4)
                    else:
                        sp.wait_ge(w_used[c], i)
                    weights(e, c)

            sp.wait_ge(items_ready, 1)
            n_items = sp.value_load(items_i[0:1, 0:1], min_val=NE, max_val=NI)
            with sp.Fori(1, NE) as e:
                item_loads(e, e)
            with sp.Fori(1, ROUNDS) as r:
                with sp.If(n_items > r * NE):
                    with sp.Fori(0, NE) as e:
                        item_loads(r * NE + e, e)

        @block.tensor
        def _(pe):
            def mm(out, lhsT, rhs, start, stop):
                return TE.matmul(out, lhsT, rhs, start=start, stop=stop, skip_group_check=True)

            def turn(out, in_):
                return TE.transpose(out, in_, ident[0:in_.shape[0], 0:in_.shape[0]])

            def close(ins, job):
                ins.then_inc(bank_full[bank(job)], 1)

            def tok(m):
                return slice(m * 128, m * 128 + MT[m])

            pe.wait_ge(x_in, 16)
            for j in range(NTILE):
                job = ("proj", j)
                open_bank(pe, job)
                pe.wait_ge(w_in_here[j % 4], 16 * (j // 4 + 1))
                for k in range(KT):
                    last = mm(ps(job)[:, 0:NT], w_in[:, j % 4, k], xT[:, k], k == 0, k == KT - 1)
                close(last, job)
            pe.wait_ge(const_in, 16)
            for j in range(NTILE):
                freed(pe, ("proj", j))
            for m in range(3):
                for what, tiles in (("rowsA", (TCK, TCV, TSK, TSV)), ("rowsB", (TWK, TWV, TGATE)),
                                    ("rowsC", (TRV, TRV + 1, TRG, TRG + 1)), ("rowsD", (TRK, TRK + 1))):
                    job = (what, m)
                    open_bank(pe, job)
                    for n, t in enumerate(tiles):
                        K = 24 if t == TGATE else 128
                        last = turn(ps(job)[0:MT[m], n * 128:n * 128 + K], uT[0:K, t, tok(m)])
                    close(last, job)
            open_bank(pe, ("gates",))
            pe.wait_ge(gsig_ready, 3)
            for p in range(4):
                last = mm(ps(("gates",))[:, 24 * p:24 * p + 24], const("pick", 4, 128)[0:64, p], gsig[0:64, 2], True, True)
            close(last, ("gates",))

            pe.wait_ge(qbd_ready, 1)
            for p in range(4):
                slot = [(2 * p + b2) % 3 for b2 in range(2)]
                half = [slice(b2 * 64, b2 * 64 + 64) for b2 in range(2)]
                job = ("vc", p)
                open_bank(pe, job)
                pe.wait_ge(means_ready, p + 1)
                for b2 in range(2):
                    last = turn(ps(job)[0:32, b2 * 128:b2 * 128 + 128], cm[:, b2, 1])
                close(last, job)
                job = ("sc", p)
                open_bank(pe, job)
                for b2 in range(2):
                    last = mm(ps(job)[half[b2], 0:32], Qbd[:, 2 * p + b2], cm[:, b2, 0], True, True)
                close(last, job)
                job = ("imp", p)
                open_bank(pe, job)
                pe.wait_ge(pcm_ready, p + 1)
                close(mm(ps(job)[:, 0:32], const("headsum"), pcm, True, True), job)
                for c in range(6):
                    job = ("sw", p, c)
                    open_bank(pe, job)
                    for b2 in range(2):
                        b = 2 * p + b2
                        pe.wait_ge(kv_here[slot[b2]], 16 * 17 * (b // 3 + 1))
                        if c == 0:
                            last = mm(ps(job)[half[b2], :], Qbd[:, b], win[:, slot[b2], 0], True, True)
                        elif c == 1:
                            mm(ps(job)[half[b2], 0:64], Qbd[:, b], uT[:, TWK, NPR:NT], True, True)
                            last = mm(ps(job)[half[b2], 64:128], Qbd[:, b], uT[:, TSK, NPR:NT], True, True)
                        else:
                            q = 4 * (c - 2)
                            last = mm(ps(job)[half[b2], :], Qbd[:, b], kvslot[:, slot[b2], q:q + 4, 2], True, True)
                    close(last, job)
                for q in range(6):
                    job = ("pt", p, q)
                    open_bank(pe, job)
                    pe.wait_ge(s_scaled, 2 * p + (1 if q == 0 else 2))
                    if q < 5:
                        for k in range(4):
                            last = turn(ps(job)[:, k * 128:k * 128 + 128], S[:, (4 * q + k) * 128:(4 * q + k) * 128 + 128])
                    else:
                        turn(ps(job)[:, 0:128], S[:, 2560:2688])
                        pe.wait_ge(pgc_ready, p + 1)
                        last = turn(ps(job)[0:32, 128:256], pgc)
                    close(last, job)
                job = ("o", p)
                open_bank(pe, job)
                freed(pe, ("vc", p))
                pe.wait_ge(vnew_in, 32)
                for b2 in range(2):
                    cols = half[b2]
                    out = ps(job)[:, cols]
                    freed(pe, ("pt", p, 5))
                    mm(out, vcr[0:32, b2], PT[0:32, 21, cols], True, False)
                    for t in range(21):
                        if t % 4 == 0:
                            freed(pe, ("pt", p, t // 4))
                        v = (win[:, slot[b2], 1, t * 128:t * 128 + 128] if t < 4 else
                             Vnew if t == 4 else kvslot[:, slot[b2], t - 5, 3])
                        last = mm(out, v, PT[:, t, cols], False, t == 20)
                close(last, job)

            job = ("pcv",)
            open_bank(pe, job)
            pe.wait_ge(pmean_ready, 1)
            close(turn(ps(job)[0:4, 0:128], cmp_p[:, 1]), job)

            def prompt_scores(qi, hh):
                i, g = hh % 4, hh // 4
                gp = slice(g * 64, g * 64 + 64)
                Kq = 128 * (qi + 1)
                job = ("ps", qi, hh)
                open_bank(pe, job)
                q = uT[gp, TQ + i, qi * 128:qi * 128 + 128]
                mm(ps(job)[:, 0:Kq], q, uT[gp, TSK, 0:Kq], True, True)
                close(mm(ps(job)[:, 256:256 + Kq], q, uT[gp, TWK, 0:Kq], True, True), job)

            for qi in range(2):
                for g in range(2):
                    job = ("pc", qi, g)
                    open_bank(pe, job)
                    gp = slice(g * 64, g * 64 + 64)
                    for i in range(4):
                        last = mm(ps(job)[:, 4 * i:4 * i + 4], uT[gp, TQ + i, qi * 128:qi * 128 + 128], cmp_p[gp, 0], True, True)
                    close(last, job)
                prompt_scores(qi, 0)
                prompt_scores(qi, 4)
                for half_ in range(2):
                    job = ("pct", qi, half_)
                    open_bank(pe, job)
                    pe.wait_ge(pc_ready, qi + 1)
                    for k in range(4):
                        last = turn(ps(job)[0:4, k * 128:k * 128 + 128], pcs[:, 4 * half_ + k])
                    close(last, job)
                for i in range(4):
                    if i < 3:
                        prompt_scores(qi, i + 1)
                        prompt_scores(qi, i + 5)
                    nk = qi + 1
                    for g in range(2):
                        n = qi * 8 + 2 * i + g
                        job = ("ppt", qi, i + 4 * g)
                        open_bank(pe, job)
                        pe.wait_ge(p_scaled, n + 1)
                        for b2 in range(2):
                            for k in range(nk):
                                c = (b2 * nk + k) * 128
                                last = turn(ps(job)[:, c:c + 128], Sp[:, n % 4, b2, k * 128:k * 128 + 128])
                        close(last, job)
                    job = ("po", qi, i)
                    open_bank(pe, job)
                    freed(pe, ("pcv",))
                    freed(pe, ("pct", qi, 0))
                    freed(pe, ("pct", qi, 1))
                    for g in range(2):
                        n = qi * 8 + 2 * i + g
                        gp = slice(g * 64, g * 64 + 64)
                        freed(pe, ("ppt", qi, i + 4 * g))
                        out = ps(job)[gp, 0:128]
                        mm(out, vcp[0:4, gp], pcT[0:4, i + 4 * g], True, False)
                        for b2 in range(2):
                            for k in range(nk):
                                last = mm(out, kvR[:, k, 3 + 2 * b2, gp], PTp[:, n % 4, b2 * nk + k], False,
                                          b2 == 1 and k == nk - 1)
                    close(last, job)

            def head(hh):
                return slice((hh % 2) * 64, (hh % 2) * 64 + 64)

            for c in range(3):
                M = MT[c]
                for z in range(2):
                    job = ("att", c, z)
                    open_bank(pe, job)
                    for hh in (z, z + 2):
                        last = mm(ps(job)[0:M, hh * 128:hh * 128 + M], uT[head(hh), TRK + hh // 2, tok(c)],
                                  uT[head(hh), TRQ + hh // 2, tok(c)], True, True)
                    close(last, job)
                if c == 1:
                    freed(pe, ("rS", 0))
                    pe.wait_ge(qd_ready, 1)
                if c == 2:
                    pe.wait_ge(rets_ready, 1)
                    pe.wait_ge(sin_in, 16)
                for z in range(2):
                    job = ("ro", c, z)
                    open_bank(pe, job)
                    freed(pe, ("att", c, z))
                    for hh in (z, z + 2):
                        out = ps(job)[0:M, hh * 64:hh * 64 + 64]
                        last = mm(out, attT[0:M, hh, 0:M], rvR[0:M, c, hh * 64:hh * 64 + 64], True, c != 1)
                        if c == 1:
                            last = mm(out, q_dec[head(hh), hh // 2], S1[head(hh), hh // 2], False, True)
                    close(last, job)
                if c < 2:
                    job = ("rS", c)
                    open_bank(pe, job)
                    pe.wait_ge(kd_ready, c + 1)
                    for hh in range(RH):
                        last = mm(ps(job)[head(hh), (hh // 2) * 64:(hh // 2) * 64 + 64], kd[:, hh * 64:hh * 64 + 64],
                                  rvR[:, c, hh * 64:hh * 64 + 64], True, True)
                    close(last, job)
            for z in range(2):
                job = ("ri", z)
                open_bank(pe, job)
                for hh in (z, z + 2):
                    for b in range(NB):
                        last = mm(ps(job)[0:64, hh * 64:hh * 64 + 64], q_wide[head(hh), hh // 2, b],
                                  s_in[head(hh), hh // 2, b], b == 0, b == NB - 1)
                close(last, job)
            for hp in range(2):
                job = ("rS_s", hp)
                open_bank(pe, job)
                for hh in (2 * hp, 2 * hp + 1):
                    last = mm(ps(job)[head(hh), :], kd[0:64, hh * 64:hh * 64 + 64], v_wide[0:64, hh], True, True)
                close(last, job)
            pe.wait_ge(pool_step, CONV_STEPS)
            for m in range(3):
                job = ("cv", m)
                open_bank(pe, job)
                for k in range(2):
                    last = turn(ps(job)[0:MT[m], k * 128:k * 128 + 128], convY[:, k, tok(m)])
                close(last, job)
            for m in range(3):
                job = ("mx", m)
                open_bank(pe, job)
                pe.wait_ge(mix_ready, m + 1)
                for k in range(4):
                    src = (convR if k < 2 else retR)[0:MT[m], m, (k % 2) * 128:(k % 2) * 128 + 128]
                    last = turn(ps(job)[:, k * 128:k * 128 + MT[m]], src)
                close(last, job)
            pe.wait_ge(wout_in, 16)
            for p in range(4):
                freed(pe, ("o", p))
            for qi in range(2):
                for i in range(4):
                    freed(pe, ("po", qi, i))
            for m in range(3):
                freed(pe, ("mx", m))
                for c in range(2):
                    job = ("wo", m, c)
                    open_bank(pe, job)
                    for k in range(KT):
                        last = mm(ps(job)[0:MT[m], :], mixT[:, k, tok(m)], w_out[:, k, c * 512:c * 512 + 512], k == 0, k == KT - 1)
                    close(last, job)
            for m in range(3):
                for c in range(2):
                    job = ("hT", m, c)
                    open_bank(pe, job)
                    pe.wait_ge(h_ready, m + 1)
                    for k in range(4):
                        d = (4 * c + k) * 128
                        last = turn(ps(job)[:, k * 128:k * 128 + MT[m]], h[0:MT[m], m, d:d + 128])
                    close(last, job)
            pe.wait_ge(moe_in, 16 * 5)
            for m in range(3):
                job = ("router", m)
                open_bank(pe, job)
                freed(pe, ("hT", m, 0))
                freed(pe, ("hT", m, 1))
                for k in range(KT):
                    last = mm(ps(job)[0:MT[m], 0:NE], hT[:, k, tok(m)], wr[:, k], k == 0, k == KT - 1)
                close(last, job)
            pe.wait_ge(plg_in, 16)
            pe.wait_ge(ple_in, 16)
            for m in range(3):
                for c in range(2):
                    for what, w, x, K in (("plg", w_plg, hT, KT), ("ple", w_ple, pT, 2)):
                        job = (what, m, c)
                        open_bank(pe, job)
                        for k in range(K):
                            last = mm(ps(job)[0:MT[m], :], x[:, k, tok(m)], w[:, k, c * 512:c * 512 + 512], k == 0, k == K - 1)
                        close(last, job)
            pe.wait_ge(mask_ready, 3)
            for m in range(3):
                job = ("rank", m)
                open_bank(pe, job)
                for j in range(m + 1):
                    w = const("lower") if j == m else ones
                    last = mm(ps(job)[0:MT[m], 0:NE], w[0:MT[j], 0:MT[m]], Mk[0:MT[j], j], j == 0, j == m)
                close(last, job)
            job = ("count",)
            open_bank(pe, job)
            for j in range(3):
                last = mm(ps(job)[:, 0:NE], ones[0:MT[j], :], Mk[0:MT[j], j], j == 0, j == 2)
            close(last, job)
            job = ("GT",)
            open_bank(pe, job)
            for m in range(3):
                last = turn(ps(job)[0:NE, tok(m)], G[0:MT[m], m])
            close(last, job)
            freed(pe, ("GT",))
            for m in range(3):
                for c in range(2):
                    job = ("bd", m, c)
                    open_bank(pe, job)
                    close(mm(ps(job)[0:MT[m], :], GTs[0:NE, tok(m)], bdn[0:NE, c * 512:c * 512 + 512], True, True), job)

            for job in list(JOB)[-8:]:
                freed(pe, job)

            def gather(i1):
                pe.wait_ge(P_ready, i1)
                for k in range(KT):
                    if k == 4:
                        pe.wait_ge(PGT_ready, i1)
                    for m in range(3):
                        last = mm(psum[:, 6 + k // 4, (k % 4) * CAP:(k % 4 + 1) * CAP], h[0:MT[m], m, k * 128:k * 128 + 128],
                                  P[0:MT[m], m], m == 0, m == 2)
                last.then_inc(gathered, 1)

            def scatter(i):
                pe.wait_ge(y_ready, i + 1)
                pe.wait_ge(PGT_ready, i + 1)
                for n in range(6):
                    m, c = n // 2, n % 2
                    if n >= 2:
                        pe.wait_ge(added, i * 6 + (n - 1))
                    mm(psum[:, 6 + c, :], PGT[0:CAP, m * 128:m * 128 + 128], y[0:CAP, c * 512:c * 512 + 512], True, True)\
                        .then_inc(scattered, 1)

            gather(1)
            n_ready = items_ready
            pe.wait_ge(n_ready, 1)
            n_items = pe.value_load(items_i[0:1, 0:1], min_val=NE, max_val=NI)
            with pe.Fori(0, ROUNDS) as r:
                with pe.If(n_items > r * NE):
                    with pe.Fori(0, NE) as e:
                        i = r * NE + e
                        pe.wait_ge(xg_ready, i + 1)
                        for k in range(KT):
                            pe.wait_ge(w_here[k], i * 16 + 16)
                            for n in range(4):
                                last = mm(psum[0:CAP, n, :], xg[:, k], wslot[:, k, n * 512:n * 512 + 512], k == 0, k == KT - 1)
                                if k == KT - 1:
                                    last.then_inc(up_done, 1)
                            if k < KT - 1:
                                last.then_inc(w_used[k], 1)
                        scatter(i)
                        pe.wait_ge(added, i * 6 + 6)
                        pe.wait_ge(PG_ready, i + 1)
                        for m in range(3):
                            last = turn(psum[:, 7, tok(m)], PG[0:MT[m], m])
                        last.then_inc(PG_turned, 1)
                        pe.wait_ge(hu_ready, i * 4 + 4)
                        for half_ in range(2):
                            for s in range(2):
                                for j in range(4 * half_, 4 * half_ + 4):
                                    cols = hu[:, 2 * j * 128 + s:2 * (j + 1) * 128:2]
                                    last = turn(psum[:, 2 * half_ + s, (j % 4) * CAP:(j % 4 + 1) * CAP], cols)
                            last.then_inc(hu_turned, 1)
                        gather(i + 2)
                        for j in range(8):
                            if j % 4 == 0:
                                pe.wait_ge(act_ready, i * 2 + (j // 4 + 1))
                            if j % 2 == 0:
                                pe.wait_ge(w_here[8 + j // 2], i * 16 + 16)
                            for c in range(2):
                                at = (j % 2) * D + c * 512
                                last = mm(psum[0:CAP, 4 + c, :], act_sb[:, j], wslot[:, 8 + j // 2, at:at + 512], j == 0, j == 7)
                            if j % 2:
                                last.then_inc(w_used[8 + j // 2], 1)
            scatter(n_items)

        @block.scalar
        def _(act):
            seen = steps(act, act_step)

            def root(n, v):
                act.wait_ge(var_ready, n + 1)
                SE.activation(v, v, ACT.Sqrt).then_inc(std_ready, 1)

            def take(job, *pairs):
                full(act, job)
                for dst, src in pairs:
                    last = SE.activation(dst, src, ACT.Copy)
                last.then_inc(bank_free[bank(job)], 1)

            act.dma_start(convS[:, 0, :, 0:CK - 1], A["state_conv"][:, 0]).then_inc(conv_in, 16)
            act.dma_start(convS[:, 1, :, 0:CK - 1], A["state_conv"][:, 1]).then_inc(conv_in, 16)
            act.dma_start(conv_w[:, :, :], A["conv_w"]).then_inc(conv_in, 16)
            act.dma_start(vecs, A["vecs"]).then_inc(vec_in, 16)
            for j in range(0, NTILE, 2):
                full(act, ("proj", j))
                scale = 0.125 if j in (TQ, TQ + 1, TQ + 2, TQ + 3, TRK, TRK + 1) else 1.0
                SE.activation(uT[:, j], ps(("proj", j))[:, 0:NT], ACT.Copy, scale=scale).then_inc(bank_free[bank(("proj", j))], 1)
            freed(act, ("proj", TG))
            freed(act, ("proj", TG + 1))
            SE.activation(uT[:, TG:TG + 2], uT[:, TG:TG + 2], ACT.Sigmoid).then_inc(conv_e, 1)
            for m in range(3):
                M = MT[m]
                b = ps(("rowsB", m))
                take(("rowsB", m), (kvR[0:M, m, 4:6], b[0:M, 0:256].rearrange("p (a b) -> p a b", a=2)),
                     (gateR[0:M, m], b[0:M, 256:280]))
                freed(act, ("rowsB", m))
                SE.activation(gsig[0:M, m], gateR[0:M, m], ACT.Sigmoid).then_inc(gsig_ready, 1)
                take(("rowsD", m), (rkR[0:M, m], ps(("rowsD", m))[0:M, 0:256]))
            freed(act, ("rowsA", 2))
            full(act, ("rowsD", 2))
            act.wait_ge(conv_ready, 1)
            act.dma_start(Vnew[0:64], kvR[0:64, 2, 5]).then_inc(vnew_in, 16)
            act.dma_start(Vnew[64:128], kvR[0:64, 2, 3]).then_inc(vnew_in, 16)

            for p in range(4):
                if p:
                    full(act, ("o", p - 1))
                take(("vc", p), (vcr[0:32], ps(("vc", p))[0:32, 0:256].rearrange("p (a b) -> p a b", a=2)))
                act.wait_ge(cmp_max, p + 1)
                SE.activation(st, st, ACT.Exp, bias=nmx[:, 0:1], accum_out=sums[:, 0:1]).then_inc(cmp_exp, 1)
                for n, (a, b) in enumerate(((0, 576), (576, 2688))):
                    act.wait_ge(s_max, 2 * p + n + 1)
                    SE.activation(S[:, a:b], S[:, a:b], ACT.Exp, bias=nmx[:, n + 1:n + 2],
                                  accum_out=sums[:, n + 1:n + 2]).then_inc(s_exp, 1)
                    act.wait_ge(s_fac, 2 * p + n + 1)
                    SE.activation(S[:, a:b], S[:, a:b], ACT.Copy, scale=fac[:, n + 1:n + 2]).then_inc(s_scaled, 1)
                for q in (0, 2, 4):
                    take(("pt", p, q), (PT[:, 4 * q:4 * q + 4], ps(("pt", p, q)).rearrange("p (a b) -> p a b", a=4)))

            full(act, ("o", 3))
            take(("pcv",), (vcp[0:4], ps(("pcv",))[0:4, 0:128]))
            for qi in range(2):
                act.wait_ge(pc_max, qi + 1)
                SE.activation(pcs, pcs, ACT.Exp).then_inc(pc_exp, 1)

                def soften(n):
                    for b2 in range(2):
                        act.wait_ge(p_max, 2 * n + b2 + 1)
                        Kq = 128 * (n // 8 + 1)
                        SE.activation(Sp[:, n % 4, b2, 0:Kq], Sp[:, n % 4, b2, 0:Kq], ACT.Exp, bias=nmxp[:, n % 4, b2:b2 + 1],
                                      accum_out=sump[:, n % 4, b2:b2 + 1]).then_inc(p_exp, 1)

                def scale_p(n):
                    act.wait_ge(p_fac, n + 1)
                    Kq = 128 * (n // 8 + 1)
                    seen(SE.activation(Sp[:, n % 4, 0, 0:Kq], Sp[:, n % 4, 0, 0:Kq], ACT.Copy, scale=facp[:, n % 4, 0:1]))
                    SE.activation(Sp[:, n % 4, 1, 0:Kq], Sp[:, n % 4, 1, 0:Kq], ACT.Copy, scale=facp[:, n % 4, 1:2]).then_inc(p_scaled, 1)

                soften(qi * 8)
                soften(qi * 8 + 1)
                if qi:
                    full(act, ("po", 0, 3))
                for half_ in range(2):
                    take(("pct", qi, half_), (pcT[0:4, 4 * half_:4 * half_ + 4],
                                              ps(("pct", qi, half_))[0:4].rearrange("p (a b) -> p a b", a=4)))
                for i in range(4):
                    scale_p(qi * 8 + 2 * i)
                    scale_p(qi * 8 + 2 * i + 1)
                    if i < 3:
                        soften(qi * 8 + 2 * i + 2)
                        soften(qi * 8 + 2 * i + 3)
            full(act, ("po", 1, 3))
            freed(act, ("rowsC", 2))
            SE.activation(sig[:, 0:2], rgR[:, 0:2], ACT.Sigmoid).then_inc(ret_e, 1)
            SE.activation(sig[0:64, 2], rgR[0:64, 2], ACT.Sigmoid).then_inc(ret_e, 1)
            for m in range(3):
                root(m, rstd[0:MT[m]])
            for m in range(3):
                root(3 + m, rstd[0:MT[m], 0:1])
            for m in range(3):
                act.wait_ge(convn_in, m + 1)
                M = MT[m]
                SE.activation(sig[0:M, m], convR[0:M, m], ACT.Sigmoid).then_inc(conv_sig, 1)
            for m in range(3):
                root(6 + m, rstd2[0:MT[m]])
            for m in range(3):
                M = MT[m]
                act.wait_ge(top_ready, m + 1)
                SE.activation(g4[0:M, 0:4], top8[0:M, 0:4], ACT.Exp, bias=r1[0:M, 0:1], accum_out=r1[0:M, 1:2]).then_inc(top_exp, 1)
            for m in range(3):
                M = MT[m]
                for c in range(2):
                    job = ("plg", m, c)
                    full(act, job)
                    if m or c:
                        freed(act, ("ple", m, 0) if c else ("ple", m - 1, 1))
                    SE.activation(sg[0:M, 0:512], ps(job)[0:M], ACT.Sigmoid).then_inc(bank_free[bank(job)], 1)

            def gathered_copy(i1):
                act.wait_ge(gathered, i1)
                SE.activation(xg.rearrange("p (a k) n -> p a (k n)", a=2), psum[:, 6:8, :], ACT.Copy).then_inc(xg_ready, 1)

            gathered_copy(1)
            act.wait_ge(items_ready, 1)
            n_items = act.value_load(items_i[0:1, 0:1], min_val=NE, max_val=NI)
            with act.Fori(0, ROUNDS) as r:
                with act.If(n_items > r * NE):
                    with act.Fori(0, NE) as e:
                        i = r * NE + e
                        for n in range(4):
                            act.wait_ge(up_done, i * 4 + (n + 1))
                            SE.activation(hu[0:CAP, n * 512:n * 512 + 512], psum[0:CAP, n, :], ACT.Copy).then_inc(hu_ready, 1)
                        act.wait_ge(PG_turned, i + 1)
                        SE.activation(PGT[0:CAP, 0:NT], psum[0:CAP, 7, 0:NT], ACT.Copy).then_inc(PGT_ready, 1)
                        for half_ in range(2):
                            act.wait_ge(g_ready, i * 2 + (half_ + 1))
                            js = slice(4 * half_, 4 * half_ + 4)
                            SE.activation(act_sb[:, js], gg[:, js], ACT.Sigmoid, scale=SALPHA).then_inc(e_ready, 1)
                        gathered_copy(i + 2)
                        act.wait_ge(w_used[11], i + 1)
                        SE.activation(y[0:CAP].rearrange("p (c n) -> p c n", c=2), psum[0:CAP, 4:6, :], ACT.Copy).then_inc(y_ready, 1)

            for m in range(3):
                root(9 + m, rstd2[0:MT[m]])

        @block.vector
        def _(dve):
            seen = steps(dve, dve_step)

            def take(job, *pairs):
                full(dve, job)
                for dst, src in pairs:
                    last = VE.tensor_copy(dst, src)
                last.then_inc(bank_free[bank(job)], 1)
                freed(dve, job)

            roots = [0]

            def inverse_root(seen, out, var):
                roots[0] += 1
                VE.tensor_scalar(out, var, EPS, None, ADD).then_inc(var_ready, 1)
                dve.wait_ge(std_ready, roots[0])
                seen(VE.reciprocal(out, out))

            def normed(seen, src, dst, n, width, mvt, stt, rs):
                for k in range(n):
                    w = width // n
                    seen(VE.bn_stats(stt[:, k], src[:, k * w:(k + 1) * w]))
                seen(VE.bn_aggr(mvt, stt[:, 0:n]))
                inverse_root(seen, rs, mvt[:, 1:2])
                seen(VE.tensor_scalar(dst, src, mvt[:, 0:1], rs, SUB, MUL))

            for k in range(2):
                VE.memset(convP[:, k, 0:CK - 1], 0.0)
            seen(VE.memset(score, -1.0))
            for j in range(1, NTILE, 2):
                full(dve, ("proj", j))
                scale = 0.125 if j in (TQ, TQ + 1, TQ + 2, TQ + 3, TRK, TRK + 1) else 1.0
                VE.tensor_scalar(uT[:, j], ps(("proj", j))[:, 0:NT], scale, None, MUL).then_inc(bank_free[bank(("proj", j))], 1)
            seen(VE.memset(score[:, 0:1], 1e4))
            seen(VE.memset(score[:, 31:33], 1e4))
            dve.wait_ge(conv_e, 1)
            freed(dve, ("proj", TA))
            freed(dve, ("proj", TA + 1))
            dve.wait_ge(conv_in, 48)
            VE.tensor_tensor(convP[:, :, CK - 1:], uT[:, TA:TA + 2, 0:NPR], uT[:, TG:TG + 2, 0:NPR], MUL)
            for k in range(2):
                last = VE.tensor_tensor(convS[:, k, :, CK - 1:], uT[:, TA + k, NPR:NT].rearrange("p (b t) -> p b t", t=TS),
                                        uT[:, TG + k, NPR:NT].rearrange("p (b t) -> p b t", t=TS), MUL)
            last.then_inc(conv_ready, 1)
            for m in range(3):
                M = MT[m]
                a, c = ps(("rowsA", m)), ps(("rowsC", m))
                take(("rowsA", m), (kvR[0:M, m, 0:4], a[0:M].rearrange("p (a b) -> p a b", a=4)))
                take(("rowsC", m), (rvR[0:M, m], c[0:M, 0:256]), (rgR[0:M, m], c[0:M, 256:512]))
            for kind, t in enumerate((TCK, TCV)):
                seen(VE.tensor_reduce(cmp_p[:, kind], uT[:, t, 0:NPR].rearrange("p (n s) -> p n s", s=64), AX, ADD))
            VE.tensor_scalar(cmp_p, cmp_p, 1.0 / 64, None, MUL).then_inc(pmean_ready, 1)
            full(dve, ("rowsD", 2))
            seen(VE.memset(Qbd, 0.0))
            for g in range(2):
                gp = slice(g * 64, g * 64 + 64)
                last = VE.tensor_copy(Qbd[gp, :, g * 32:g * 32 + 32].rearrange("p b (i t) -> p b i t", t=TS),
                                      uT[gp, TQ:TQ + 4, NPR:NT].rearrange("p i (b t) -> p b i t", t=TS))
                if g == 0:
                    seen(last)
            last.then_inc(qbd_ready, 1)
            full(dve, ("gates",))
            VE.tensor_tensor(gtmp, ps(("gates",))[:, 0:96].rearrange("p (a b) -> p a b", a=4),
                             const("headmask").unsqueeze(1).to_broadcast([128, 4, 24]), MUL).then_inc(bank_free[bank(("gates",))], 1)
            freed(dve, ("gates",))
            for p in range(4):
                last = VE.tensor_reduce(gs[:, p], gtmp[:, p].rearrange("p (h c) -> p c h", c=3), AX, ADD)
            seen(last)

            for p in range(4):
                for b2 in range(2):
                    b = 2 * p + b2
                    dve.wait_ge(kv_here[b % 3], 16 * 17 * (b // 3 + 1))
                    if p:
                        full(dve, ("vc", p - 1))
                        full(dve, ("sc", p - 1))
                    for kind in range(2):
                        seen(VE.tensor_reduce(cm[:, b2, kind].rearrange("p (a b) -> p a b", b=2),
                                              kvslot[:, b % 3, :, kind].rearrange("p a (b s) -> p a b s", b=2), AX, ADD))
                VE.tensor_scalar(cm, cm, 1.0 / 64, None, MUL).then_inc(means_ready, 1)
                job = ("sc", p)
                full(dve, job)
                VE.tensor_tensor(st, ps(job)[:, 0:32], const("tabcmp"), ADD).then_inc(bank_free[bank(job)], 1)
                freed(dve, job)
                seen(VE.tensor_reduce(mx[:, 0:1], st, AX, MAXOP))
                VE.tensor_scalar(nmx[:, 0:1], mx[:, 0:1], -1e29, -1.0, MAXOP, MUL).then_inc(cmp_max, 1)
                dve.wait_ge(cmp_exp, p + 1)
                seen(VE.tensor_scalar(fac[:, 0:1], sums[:, 0:1], TINY, None, MAXOP))
                seen(VE.reciprocal(fac[:, 0:1], fac[:, 0:1]))
                VE.tensor_scalar(pcm, st, fac[:, 0:1], None, MUL).then_inc(pcm_ready, 1)
                dve.wait_ge(pcm_ready, p + 1)
                if p:
                    full(dve, ("pt", p - 1, 5))
                VE.tensor_scalar(pgc, pcm, gs[:, p, 0:1], None, MUL).then_inc(pgc_ready, 1)
                job = ("imp", p)
                full(dve, job)
                VE.tensor_copy(score[:, 1:31], ps(job)[:, 1:31]).then_inc(bank_free[bank(job)], 1)
                freed(dve, job)
                seen(VE.max(t8a, score))
                seen(VE.match_replace(score2, t8a, score, -2.0))
                seen(VE.max(t8b, score2))
                seen(VE.match_replace(score3, t8b, score2, -2.0))
                seen(VE.tensor_scalar(selb, score3[:, 0:32], -2.0, -NEG, ALU.is_equal, MUL))
                seen(VE.tensor_scalar(selb, selb, -NEG, None, SUB))
                for c in range(6):
                    job = ("sw", p, c)
                    full(dve, job)
                    if c == 0:
                        last = VE.tensor_tensor(S[:, 0:512], ps(job), const("tabwin"), ADD)
                    elif c == 1:
                        last = VE.tensor_tensor(S[:, 512:640], ps(job)[:, 0:128], const("tabnew", 4, 128)[:, p], ADD)
                    else:
                        at = 640 + 512 * (c - 2)
                        last = VE.scalar_tensor_tensor(out=S[:, at:at + 512], in0=ps(job), scalar=const("chunkbase")[:, c - 2:c - 1],
                                                       in1=const("tabsel"), op0=ADD, op1=ADD)
                    last.then_inc(bank_free[bank(job)], 1)
                    freed(dve, job)
                    if c == 1:
                        seen(VE.tensor_reduce(mx[:, 1:2], S[:, 0:576], AX, MAXOP))
                        VE.tensor_scalar(nmx[:, 1:2], mx[:, 1:2], -1.0, None, MUL).then_inc(s_max, 1)
                blocks = S[:, 640:2688].rearrange("p (n s) -> p n s", s=64)
                seen(VE.tensor_tensor(blocks, blocks, selb.unsqueeze(2).to_broadcast([128, 32, 64]), ADD))
                seen(VE.tensor_reduce(mx[:, 2:3], S[:, 576:2688], AX, MAXOP))
                VE.tensor_scalar(nmx[:, 2:3], mx[:, 2:3], -1.0, None, MUL).then_inc(s_max, 1)
                for n in range(2):
                    dve.wait_ge(s_exp, 2 * p + n + 1)
                    f = fac[:, n + 1:n + 2]
                    seen(VE.tensor_scalar(f, sums[:, n + 1:n + 2], TINY, None, MAXOP))
                    seen(VE.reciprocal(f, f))
                    VE.tensor_scalar(f, f, gs[:, p, 2 - n:3 - n], None, MUL).then_inc(s_fac, 1)
                if p:
                    full(dve, ("o", p - 1))
                for q in (1, 3):
                    take(("pt", p, q), (PT[:, 4 * q:4 * q + 4], ps(("pt", p, q)).rearrange("p (a b) -> p a b", a=4)))
                b = ps(("pt", p, 5))
                take(("pt", p, 5), (PT[:, 20], b[:, 0:128]), (PT[0:32, 21], b[0:32, 128:256]))
                src = ps(("o", p))[:, 0:128].rearrange("p (b g i t) -> p b g i t", b=2, g=2, i=4)
                cols = slice(NPR + 16 * p, NPR + 16 * p + 16)
                full(dve, ("o", p))
                for g in range(2):
                    gp = slice(g * 64, g * 64 + 64)
                    last = VE.tensor_copy(mixT[gp, 2:6, cols].rearrange("p i (b t) -> p i b t", b=2),
                                          src[gp, :, g].rearrange("p b i t -> p i b t"))
                last.then_inc(bank_free[bank(("o", p))], 1)

            def prompt_scores(n):
                qi, hh = n // 8, (n % 8) // 2 + 4 * (n % 2)
                Kq = 128 * (qi + 1)
                job = ("ps", qi, hh)
                full(dve, job)
                dist = const("distp")[:, 0:128] if qi == 0 else const("distp")[:, 128:384]
                if n >= 4:
                    m = n - 4
                    full(dve, ("ppt", m // 8, (m % 8) // 2 + 4 * (m % 2)))
                VE.scalar_tensor_tensor(out=Sp[:, n % 4, :, 0:Kq], in0=dist.unsqueeze(1).to_broadcast([128, 2, Kq]),
                                        scalar=NSLOPE[hh], in1=ps(job).rearrange("p (a b) -> p a b", a=2)[:, :, 0:Kq],
                                        op0=MUL, op1=ADD).then_inc(bank_free[bank(job)], 1)
                freed(dve, job)
                seen(VE.tensor_reduce(mxp[:, n % 4], Sp[:, n % 4, :, 0:Kq], AX, MAXOP))
                VE.tensor_scalar(nmxp[:, n % 4], mxp[:, n % 4], -1.0, None, MUL).then_inc(p_max, 2)

            def prompt_factor(n):
                qi, hh = n // 8, (n % 8) // 2 + 4 * (n % 2)
                dve.wait_ge(p_exp, 2 * n + 2)
                f = facp[:, n % 4]
                seen(VE.tensor_scalar(f, sump[:, n % 4], TINY, None, MAXOP))
                seen(VE.reciprocal(f, f))
                VE.tensor_tensor(f, f, gsig[:, qi, 3 * hh + 1:3 * hh + 3], MUL).then_inc(p_fac, 1)

            for qi in range(2):
                if qi:
                    full(dve, ("pct", 0, 1))
                for g in range(2):
                    job = ("pc", qi, g)
                    full(dve, job)
                    for i in range(4):
                        last = VE.scalar_tensor_tensor(out=pcs[:, 4 * g + i], in0=const("distcmp", 2, 4)[:, qi], scalar=NSLOPE[4 * g + i],
                                                       in1=ps(job)[:, 4 * i:4 * i + 4], op0=MUL, op1=ADD)
                    last.then_inc(bank_free[bank(job)], 1)
                    freed(dve, job)
                seen(VE.tensor_reduce(mc8, pcs, AX, MAXOP))
                seen(VE.tensor_scalar(mc8, mc8, -1e29, None, MAXOP))
                VE.tensor_tensor(pcs, pcs, mc8.unsqueeze(2).to_broadcast([128, 8, 4]), SUB).then_inc(pc_max, 1)
                prompt_scores(qi * 8)
                prompt_scores(qi * 8 + 1)
                dve.wait_ge(pc_exp, qi + 1)
                seen(VE.tensor_reduce(sc8, pcs, AX, ADD))
                seen(VE.tensor_scalar(sc8, sc8, TINY, None, MAXOP))
                seen(VE.reciprocal(sc8, sc8))
                seen(VE.tensor_tensor(sc8, sc8, gsig[:, qi].rearrange("p (h c) -> p h c", c=3)[:, :, 0], MUL))
                VE.tensor_tensor(pcs, pcs, sc8.unsqueeze(2).to_broadcast([128, 8, 4]), MUL).then_inc(pc_ready, 1)
                for i in range(4):
                    prompt_factor(qi * 8 + 2 * i)
                    prompt_factor(qi * 8 + 2 * i + 1)
                    if i < 3:
                        prompt_scores(qi * 8 + 2 * i + 2)
                        prompt_scores(qi * 8 + 2 * i + 3)
                    w = 256 * (qi + 1)
                    for g in range(2):
                        n = qi * 8 + 2 * i + g
                        if n >= 4:
                            full(dve, ("po", (n - 4) // 8, ((n - 4) % 8) // 2))
                        job = ("ppt", qi, i + 4 * g)
                        take(job, (PTp[:, n % 4].rearrange("p a b -> p (a b)")[:, 0:w], ps(job)[:, 0:w]))
                    take(("po", qi, i), (mixT[:, 2 + i, qi * 128:qi * 128 + 128], ps(("po", qi, i))[:, 0:128]))

            dve.wait_ge(late_in, 16)
            for m in range(3):
                freed(dve, ("rowsD", m))

            def heads(a):
                return a.rearrange("p (h e) -> p h e", h=RH)

            def weigh(c, decay):
                M = MT[c]
                for z in range(2):
                    job = ("att", c, z)
                    full(dve, job)
                    VE.tensor_tensor(attT[0:M, z::2, 0:M], ps(job)[0:M].rearrange("p (h e) -> p h e", h=RH)[:, z::2, 0:M],
                                     decay[0:M, z::2], MUL).then_inc(bank_free[bank(job)], 1)

            def take_ro(c):
                M = MT[c]
                for z in range(2):
                    job = ("ro", c, z)
                    take(job, (heads(retR[0:M, c])[:, z::2], heads(ps(job)[0:M, 0:256])[:, z::2]))

            for c in range(2):
                if c:
                    full(dve, ("rS", 0))
                VE.tensor_tensor(heads(kd), heads(rkR[:, c]), const("kdec").unsqueeze(2).to_broadcast([128, RH, 64]), MUL)\
                    .then_inc(kd_ready, 1)
                if c:
                    full(dve, ("ro", 0, 1))
                    VE.tensor_tensor(q_dec, uT[:, TRQ:TRQ + 2, 128:256], const("qdec", 2, 128), MUL).then_inc(qd_ready, 1)
                weigh(c, const("dmask", RH, 128))
                take_ro(c)
                job = ("rS", c)
                if c == 0:
                    take(job, (S1, ps(job)[:, 0:128].rearrange("p (h e) -> p h e", h=2)))
                else:
                    full(dve, job)
                    for hp in range(2):
                        last = VE.scalar_tensor_tensor(out=S2[:, hp], in0=S1[:, hp], scalar=const("cdec")[:, hp:hp + 1],
                                                       in1=ps(job)[:, hp * 64:hp * 64 + 64], op0=MUL, op1=ADD)
                    last.then_inc(bank_free[bank(job)], 1)
            VE.tensor_tensor(heads(kd[0:64]), heads(rkR[0:64, 2]), const("kdec_s")[0:64].unsqueeze(2).to_broadcast([64, RH, 64]), MUL)
            for hp in range(2):
                VE.tensor_tensor(q_wide[:, hp], uT[:, TRQ + hp, NPR:NT].unsqueeze(1).to_broadcast([128, NB, 64]),
                                 const("qmask", 2, NB, 64)[:, hp], MUL)
            for hh in range(RH):
                last = VE.tensor_tensor(v_wide[0:64, hh], rvR[0:64, 2, hh * 64:hh * 64 + 64].unsqueeze(1).to_broadcast([64, NB, 64]),
                                        const("bmask")[0:64].unsqueeze(2).to_broadcast([64, NB, 64]), MUL)
            last.then_inc(rets_ready, 1)
            weigh(2, const("dmask_s", RH, 64))
            take_ro(2)
            for z in range(2):
                job = ("ri", z)
                full(dve, job)
                o = heads(retR[0:64, 2])[:, z::2]
                VE.tensor_tensor(o, o, heads(ps(job)[0:64, 0:256])[:, z::2], ADD).then_inc(bank_free[bank(job)], 1)
                freed(dve, job)
            dve.wait_ge(sin_in, 16)
            for hp in range(2):
                job = ("rS_s", hp)
                full(dve, job)
                VE.scalar_tensor_tensor(out=s_in[:, hp], in0=s_in[:, hp], scalar=const("cdec_s")[:, hp:hp + 1],
                                        in1=ps(job).rearrange("p (b e) -> p b e", b=NB), op0=MUL, op1=ADD)\
                    .then_inc(bank_free[bank(job)], 1)
            dve.wait_ge(vec_in, 16)
            dve.wait_ge(ret_e, 2)
            for m in range(3):
                M = MT[m]
                seen(VE.tensor_tensor(sig[0:M, m], sig[0:M, m], rgR[0:M, m], MUL))
                for hh in range(RH):
                    seen(VE.bn_stats(stats[0:M, hh], retR[0:M, m, hh * 64:hh * 64 + 64]))
                    seen(VE.bn_aggr(mv[0:M, hh], stats[0:M, hh]))
                inverse_root(seen, rstd[0:M], mv[0:M, :, 1])
                for hh in range(RH):
                    x = retR[0:M, m, hh * 64:hh * 64 + 64]
                    last = VE.tensor_scalar(x, x, mv[0:M, hh, 0:1], rstd[0:M, hh:hh + 1], SUB, MUL)
                seen(last)
                seen(VE.tensor_tensor(retR[0:M, m], retR[0:M, m], vecs[0:M, 2], MUL))
                last = VE.tensor_tensor(retR[0:M, m], retR[0:M, m], sig[0:M, m], MUL)
                if m == 2:
                    last.then_inc(ret_done, 1)
                else:
                    seen(last)
            dve.wait_ge(ret_done, 1)
            for m in range(3):
                M = MT[m]
                take(("cv", m), (convR[0:M, m], ps(("cv", m))[0:M, 0:256]))
                normed(seen, convR[0:M, m], convR[0:M, m], 1, CC, mv[0:M, 0], stats[0:M], rstd[0:M, 0:1])
                seen(VE.tensor_tensor(convR[0:M, m], convR[0:M, m], vecs[0:M, 0], MUL))
                VE.tensor_tensor(convR[0:M, m], convR[0:M, m], vecs[0:M, 1], ADD).then_inc(convn_in, 1)
            for m in range(3):
                M = MT[m]
                dve.wait_ge(conv_sig, m + 1)
                VE.tensor_tensor(convR[0:M, m], convR[0:M, m], sig[0:M, m], MUL).then_inc(mix_ready, 1)
            for m in range(3):
                M, job = MT[m], ("mx", m)
                t = slice(m * 128, m * 128 + M)
                b = ps(job).rearrange("p (k n) -> p k n", k=4)
                take(job, (mixT[:, 0:2, t], b[:, 0:2, 0:M]), (mixT[:, 6:8, t], b[:, 2:4, 0:M]))

            dve.wait_ge(xrow_in, 32)
            dve.wait_ge(ln1_in, 16)
            dve.wait_ge(states_out, 32)
            for m in range(3):
                M = MT[m]
                for c in range(2):
                    job = ("wo", m, c)
                    full(dve, job)
                    z = acc[0:M, m, c * 512:c * 512 + 512]
                    VE.scalar_tensor_tensor(out=z, in0=z, scalar=ALPHA, in1=ps(job)[0:M], op0=MUL, op1=ADD).then_inc(bank_free[bank(job)], 1)
                    freed(dve, job)
                normed(seen, acc[0:M, m], h[0:M, m], 2, D, mv2[0:M], stats2[0:M], rstd2[0:M])
                seen(VE.tensor_tensor(h[0:M, m], h[0:M, m], ln[0:M, 0], MUL))
                VE.tensor_tensor(h[0:M, m], h[0:M, m], ln[0:M, 1], ADD).then_inc(h_ready, 1)
            dve.wait_ge(h_ready, 3)
            full(dve, ("wo", 2, 1))
            for m in range(3):
                for c in range(2):
                    job = ("hT", m, c)
                    M = MT[m]
                    take(job, (hT[:, 4 * c:4 * c + 4, m * 128:m * 128 + M], ps(job).rearrange("p (k n) -> p k n", k=4)[:, :, 0:M]))
            dve.wait_ge(moe_in, 16 * 5)
            for m in range(3):
                M, job = MT[m], ("router", m)
                full(dve, job)
                VE.tensor_tensor(lg[0:M], ps(job)[0:M, 0:NE], br[0:M], ADD).then_inc(bank_free[bank(job)], 1)
                freed(dve, job)
                seen(VE.max(top8[0:M], lg[0:M]))
                seen(VE.max_index(top_i[0:M, m, :], top8[0:M], lg[0:M]))
                seen(VE.tensor_copy(idxf[0:M], top_i[0:M, m, :]))
                VE.tensor_scalar(r1[0:M, 0:1], top8[0:M, 0:1], -1.0, None, MUL).then_inc(top_ready, 1)
                seen(VE.memset(Mk[0:M, m], 0.0))
                seen(VE.memset(G[0:M, m], 0.0))
                for k in range(TOPK):
                    last = VE.scalar_tensor_tensor(out=Mk[0:M, m], in0=const("iota")[0:M, 0:NE], scalar=idxf[0:M, k:k + 1], in1=Mk[0:M, m],
                                                   op0=ALU.is_equal, op1=ADD)
                    if k < TOPK - 1:
                        seen(last)
                last.then_inc(mask_ready, 1)
                dve.wait_ge(top_exp, m + 1)
                seen(VE.reciprocal(r1[0:M, 2:3], r1[0:M, 1:2]))
                seen(VE.tensor_scalar(g4[0:M, 0:4], g4[0:M, 0:4], r1[0:M, 2:3], None, MUL))
                for k in range(TOPK):
                    seen(VE.tensor_scalar(etmp[0:M], const("iota")[0:M, 0:NE], idxf[0:M, k:k + 1], g4[0:M, k:k + 1], ALU.is_equal, MUL))
                    seen(VE.tensor_tensor(G[0:M, m], G[0:M, m], etmp[0:M], ADD))
            for m in range(3):
                M = MT[m]
                for c in range(2):
                    cols = slice(c * 512, c * 512 + 512)
                    freed(dve, ("plg", m, c))
                    s = sg[0:M, 0:512]
                    job = ("ple", m, c)
                    full(dve, job)
                    VE.tensor_tensor(acc[0:M, m, cols], s, ps(job)[0:M], MUL).then_inc(bank_free[bank(job)], 1)
                    freed(dve, job)
                    seen(VE.scalar_tensor_tensor(out=acc[0:M, m, cols], in0=h[0:M, m, cols], scalar=ALPHA,
                                                 in1=acc[0:M, m, cols], op0=MUL, op1=ADD))
            seen(VE.memset(rank_all, -1e4))
            seen(VE.memset(gate_all, 0.0))
            for m in range(3):
                M, job = MT[m], ("rank", m)
                full(dve, job)
                VE.scalar_tensor_tensor(out=lg[0:M], in0=ps(job)[0:M, 0:NE], scalar=1e4, in1=Mk[0:M, m], op0=ADD, op1=MUL)\
                    .then_inc(bank_free[bank(job)], 1)
                freed(dve, job)
                for r in range(ROUNDS):
                    VE.tensor_scalar(rank_all[0:M, m, r * NE:(r + 1) * NE], lg[0:M], -1e4 - CAP * r, None, ADD)
                    last = VE.tensor_copy(gate_all[0:M, m, r * NE:(r + 1) * NE], G[0:M, m])
                seen(last)
            job = ("count",)
            full(dve, job)
            VE.tensor_reduce(r1[:, 3:4], ps(job)[:, 0:NE], AX, MAXOP).then_inc(bank_free[bank(job)], 1)
            freed(dve, job)
            seen(VE.tensor_scalar(lg[:, 0:ROUNDS], const("iota")[:, 0:ROUNDS], float(CAP), r1[:, 3:4], MUL, ALU.is_lt))
            seen(VE.tensor_reduce(r1[:, 4:5], lg[:, 0:ROUNDS], AX, ADD))
            seen(VE.tensor_scalar(r1[:, 4:5], r1[:, 4:5], float(NE), None, MUL))
            VE.tensor_copy(items_i[0:1, 0:1], r1[0:1, 4:5]).then_inc(items_ready, 1)
            take(("GT",), (GTs[0:NE], ps(("GT",))[0:NE, 0:NT]))
            for m in range(3):
                M = MT[m]
                for c in range(2):
                    job = ("bd", m, c)
                    full(dve, job)
                    a = acc[0:M, m, c * 512:c * 512 + 512]
                    VE.tensor_tensor(a, a, ps(job)[0:M], ADD).then_inc(bank_free[bank(job)], 1)
                    freed(dve, job)

            def choose(seen, out, i, gated):
                for m in range(3):
                    M = MT[m]
                    if gated:
                        last = VE.tensor_scalar(out[0:M, m, 0:CAP], const("iota")[0:M], rank_all[0:M, m, bass.ds(i, 1)],
                                                gate_all[0:M, m, bass.ds(i, 1)], ALU.is_equal, MUL)
                    else:
                        last = VE.tensor_scalar(out[0:M, m], const("iota")[0:M], rank_all[0:M, m, bass.ds(i, 1)],
                                                None, ALU.is_equal)
                return last

            choose(seen, P, 0, False).then_inc(P_ready, 1)
            VE.memset(y[0:CAP], 0.0).then_inc(y_ready, 1)
            VE.memset(PGT[0:CAP], 0.0).then_inc(PGT_ready, 1)
            dve.wait_ge(items_ready, 1)
            n_items = dve.value_load(items_i[0:1, 0:1], min_val=NE, max_val=NI)
            LINKS = 8

            def add_item(i, n):
                m, c = n // 2, n % 2
                dve.wait_ge(scattered, i * 6 + (n + 1))
                a = acc[0:MT[m], m, c * 512:c * 512 + 512]
                VE.tensor_tensor(a, a, psum[0:MT[m], 6 + c, :], ADD).then_inc(added, 1)

            with dve.Fori(0, ROUNDS) as r:
                with dve.If(n_items > r * NE):
                    with dve.Fori(0, NE) as e:
                        i = r * NE + e
                        lseen = steps(dve, dve_loop, i * LINKS)
                        dve.wait_ge(gathered, i + 1)
                        choose(lseen, PG, i, True).then_inc(PG_ready, 1)
                        choose(lseen, P, i + 1, False).then_inc(P_ready, 1)
                        for n in range(6):
                            add_item(i, n)
                        bias = bup[:, bass.ds(e, 1)].rearrange("p a (s j) -> p (a s) j", s=2)
                        for half_ in range(2):
                            js = slice(4 * half_, 4 * half_ + 4)
                            g_t, u_t = (psum[:, 2 * half_ + s, :].rearrange("p (j n) -> p j n", j=4) for s in range(2))
                            gate, up_, sg_ = gg[:, js], uu[:, js], act_sb[:, js]
                            dve.wait_ge(hu_turned, i * 2 + (half_ + 1))
                            lseen(VE.tensor_tensor(gate, g_t, bias[:, 0, js].unsqueeze(2).to_broadcast([128, 4, CAP]), ADD))
                            VE.tensor_scalar(gate, gate, LIMIT, None, ALU.min).then_inc(g_ready, 1)
                            lseen(VE.tensor_tensor(up_, u_t, bias[:, 1, js].unsqueeze(2).to_broadcast([128, 4, CAP]), ADD))
                            lseen(VE.tensor_scalar(up_, up_, LIMIT, -LIMIT, ALU.min, MAXOP))
                            lseen(VE.scalar_tensor_tensor(out=up_, in0=up_, scalar=1.0, in1=gate, op0=ADD, op1=MUL))
                            dve.wait_ge(e_ready, i * 2 + (half_ + 1))
                            VE.tensor_tensor(sg_, up_, sg_, MUL).then_inc(act_ready, 1)
                        assert lseen.count[0] == LINKS
            dve.wait_ge(added, n_items * 6)
            for n in range(6):
                add_item(n_items, n)
            tail = steps(dve, dve_tail)
            dve.wait_ge(added, n_items * 6 + 6)
            for m in range(3):
                M = MT[m]
                a = acc[0:M, m]
                normed(tail, a, a, 2, D, mv2[0:M], stats2[0:M], rstd2[0:M])
                tail(VE.tensor_tensor(a, a, ln[0:M, 2], MUL))
                VE.tensor_tensor(a, a, ln[0:M, 3], ADD).then_inc(y_out, 1)

        @block.gpsimd
        def _(pool):
            seen = steps(pool, pool_step)
            pool.dma_start(O["win_s"][:, 0:WIN - TS], A["cache_win"][:, TS:WIN]).then_inc(wincopy_out, 16)
            pool.wait_ge(conv_in, 48)
            pool.wait_ge(conv_ready, 1)
            full(pool, ("rowsC", 2))
            for k in range(2):
                parts = [(convY[:, k, 0:NPR], conv_t, lambda t, k=k: convP[:, k, t:t + NPR]),
                         (convY[:, k, NPR:NT].rearrange("p (b t) -> p b t", t=TS),
                          conv_t[:, 0:NSM].rearrange("p (b t) -> p b t", t=TS), lambda t, k=k: convS[:, k, :, t:t + TS])]
                for dst, tmp, src in parts:
                    seen(GE.tensor_scalar(dst, src(0), conv_w[:, k, 0:1], conv_w[:, k, CK:CK + 1], MUL, ADD))
                    for t in range(1, CK):
                        seen(GE.tensor_scalar(tmp, src(t), conv_w[:, k, t:t + 1], None, MUL))
                        seen(GE.tensor_tensor(dst, dst, tmp, ADD))
            pool.dma_start(O["conv_p"], convP[:, :, NPR:NPR + CK - 1]).then_inc(conv_out, 16)
            for k in range(2):
                pool.dma_start(O["conv_s"][:, k], convS[:, k, :, TS:TS + CK - 1]).then_inc(conv_out, 16)
            for m in range(3):
                for w in ("rowsA", "rowsB"):
                    freed(pool, (w, m))
            for m in range(2):
                pool.dma_start(O["nsa_p"][m * 128:m * 128 + 128], kvR[:, m, 0:4]).then_inc(rows_out, 16)
                pool.dma_start(O["win_p"][m * 128:m * 128 + 128], kvR[:, m, 4:6]).then_inc(rows_out, 16)
            pool.dma_start(O["nsa_s"], kvR[0:64, 2, 0:4]).then_inc(rows_out, 16)
            for b in range(NB):
                rows = kvR[b * TS:(b + 1) * TS, 2, 4:6].rearrange("p a b -> p (a b)")
                pool.dma_start(O["win_s"][b, WIN - TS:WIN], rows).then_inc(rows_out, 16)
            freed(pool, ("rS", 1))
            pool.dma_start(O["ret_p"], S2).then_inc(states_out, 16)
            freed(pool, ("rS_s", 0))
            freed(pool, ("rS_s", 1))
            pool.dma_start(O["ret_s"], s_in).then_inc(states_out, 16)
            for m in range(3):
                pool.wait_ge(y_out, m + 1)
                pool.dma_start(O["y"][m * 128:m * 128 + MT[m]], acc[0:MT[m], m]).then_inc(y_stored, 16)
            pool.wait_ge(conv_out, 48)
            pool.wait_ge(wincopy_out, 16)
            pool.wait_ge(rows_out, 16 * 13)
            pool.wait_ge(states_out, 32)
            pool.wait_ge(y_stored, 48)
    return nc


def lay_out(x):
    import numpy as np
    c = np.ascontiguousarray
    a = {k: np.asarray(v) for k, v in x.items()}
    rows = np.concatenate([a["x_prompt"].reshape(NPR, D), a["x_sample"].reshape(NSM, D)])
    pr = np.concatenate([a["p_prompt"].reshape(NPR, PLE), a["p_sample"].reshape(NSM, PLE)])
    w = a["w_in"][0]
    at = {}
    o = 0
    for name, n in (("a", 256), ("g", 256), ("q", 512), ("kv", 768), ("gate", 24), ("rq", 256), ("rk", 256), ("rv", 256), ("rg", 256)):
        at[name] = w[:, o:o + n]
        o += n
    q = at["q"].reshape(D, KV, GQ, HD)
    kv = at["kv"].reshape(D, 6, 128)
    cols = [q[:, :, i].reshape(D, 128) for i in range(4)] + [kv[:, 0], kv[:, 2], kv[:, 4]]
    cols += [at["rq"], at["rk"], at["a"], at["g"], kv[:, 1], kv[:, 3], kv[:, 5], at["gate"], np.zeros((D, 104), w.dtype), at["rv"], at["rg"]]
    cols = np.concatenate(cols, 1)
    assert cols.shape == (D, NTILE * 128)
    w_in = cols.reshape(KT, 128, NTILE, 128).transpose(2, 1, 0, 3)
    cache = a["cache_nsa_kv"][0].reshape(-1, PAGE, 4, 128)
    pages = np.stack([cache[:, :, 0].transpose(0, 2, 1), cache[:, :, 1].transpose(0, 2, 1),
                      cache[:, :, 2].transpose(0, 2, 1), cache[:, :, 3]], 2)
    wk = a["cache_win_kv"][0].reshape(NB, WIN, 2, 128)
    windows = np.stack([wk[:, :, 0].transpose(0, 2, 1),
                        wk[:, :, 1].reshape(NB, 4, 128, 128).transpose(0, 2, 1, 3).reshape(NB, 128, 512)], 2)
    wo = a["w_out"][0]
    att = wo[256:768].reshape(KV, GQ, HD, D).transpose(1, 0, 2, 3).reshape(512, D)
    wo = np.concatenate([wo[:256], att, wo[768:]])

    def ktiles(m):
        return m.reshape(-1, 128, m.shape[1]).transpose(1, 0, 2)

    def spread(v):
        return np.broadcast_to(v, (128,) + v.shape)

    early, late = constants()
    cw = np.concatenate([a["conv_w"][0], a["conv_b"][0][None]])
    out = dict(
        xT=ktiles(c(rows.T)), pT=ktiles(c(pr.T)), x_rows=rows, w_in=w_in, pages=pages.reshape(len(cache), 128, 512),
        windows=windows, cache_win=wk.reshape(NB, WIN, 256), page_table=a["page_table"].reshape(1, -1),
        w_out=ktiles(wo), w_plg=ktiles(a["w_plg"][0]), w_ple=ktiles(a["w_ple"][0]), w_router=ktiles(a["w_router"][0]),
        b_router=spread(a["b_router"][0]), b_down=a["b_down"][0], w_up=a["w_up"][0], w_down=a["w_down"][0],
        b_up=a["b_up"][0].reshape(NE, 8, 128, 2).transpose(2, 0, 3, 1).reshape(128, NE, 16),
        state_conv=a["state_conv"][0].transpose(2, 0, 1).reshape(2, 128, NB, CK - 1).transpose(1, 0, 2, 3),
        conv_w=cw.T.reshape(2, 128, CK + 1).transpose(1, 0, 2),
        state_ret=a["state_ret"][0].reshape(NB, 2, 2, 64, 64).transpose(2, 3, 1, 0, 4).reshape(128, 2, NB, 64),
        vecs=spread(np.stack([a["conv_ln_g"][0], a["conv_ln_b"][0], a["ret_norm_g"][0]])),
        ln=spread(np.stack([a["ln1_g"][0], a["ln1_b"][0], a["ln2_g"][0], a["ln2_b"][0]])),
        early=early, late=late)
    return {k: c(v) for k, v in out.items()}


OUTPUTS = dict(y=(NT, D), nsa_p=(NPR, 4, 128), nsa_s=(NSM, 4, 128), win_p=(NPR, 2, 128), win_s=(NB, WIN, 256),
               ret_p=(128, 2, 64), ret_s=(128, 2, NB, 64), conv_p=(128, 2, CK - 1), conv_s=(128, 2, NB, CK - 1))


def kernel(**inputs):
    import numpy as np
    import concourse.bacc as bacc
    from concourse import mybir
    from concourse.bass_utils import run_bass_kernel_spmd

    arrays = lay_out(inputs)
    nc = bacc.Bacc("TRN2", target_bir_lowering=False, num_devices=1)
    A = {k: nc.dram_tensor(f"in_{k}", v.shape, mybir.dt.from_np(v.dtype), kind="ExternalInput").ap() for k, v in arrays.items()}
    O = {k: nc.dram_tensor(f"out_{k}", s, mybir.dt.float32, kind="ExternalOutput").ap() for k, s in OUTPUTS.items()}
    build(nc, A, O)
    run = run_bass_kernel_spmd(nc, [{f"in_{k}": v for k, v in arrays.items()}], core_ids=[0])
    o = {k: np.asarray(run.results[0][f"out_{k}"]) for k in OUTPUTS}
    ret_s = o["ret_s"].reshape(2, 64, 2, NB, 64).transpose(3, 2, 0, 1, 4).reshape(1, NB, RH, 64, 64)
    ret_p = o["ret_p"].reshape(2, 64, 2, 64).transpose(2, 0, 1, 3).reshape(1, 1, RH, 64, 64)
    conv_p = o["conv_p"].transpose(2, 1, 0).reshape(1, 1, CK - 1, CC)
    conv_s = o["conv_s"].transpose(2, 3, 1, 0).reshape(1, NB, CK - 1, CC)
    return (o["y"][:NPR].reshape(1, NPR, D), o["y"][NPR:].reshape(NB, TS, D),
            o["nsa_p"].reshape(1, 1, NPR, 4, KV, HD), o["nsa_s"].reshape(1, NB, TS, 4, KV, HD),
            o["win_p"].reshape(1, 1, NPR, 2, KV, HD), o["win_s"].reshape(1, NB, WIN, 2, KV, HD),
            np.ascontiguousarray(ret_p), np.ascontiguousarray(ret_s), np.ascontiguousarray(conv_p), np.ascontiguousarray(conv_s))
```

```python
import math

F = 4
D, NPR, NB, TS = 1024, 256, 8, 8
NSM = NB * TS
NT = NPR + NSM
KT = D // 128
HD, HEADS, KV, GQ = 64, 8, 2, 4
PAST, PAGE = 2048, 128
NPG = PAST // PAGE
WIN = 512
RH, CC, CK = 4, 256, 31
NE, TOPK, FF, PLE = 32, 4, 1024, 256
CAP = 128
ROUNDS = -(-NT // CAP)
ALPHA = 2 ** 0.25
EPS, TINY, NEG = 1e-5, 1e-30, -1e30
LIMIT, SALPHA = 7.0, 1.702
MT = [128, 128, 64]
TQ, TCK, TSK, TWK, TRQ, TRK, TA, TG, TCV, TSV, TWV, TGATE, TRV, TRG = 0, 4, 5, 6, 7, 9, 11, 13, 15, 16, 17, 18, 19, 21
NTILE = 23


def const_layout():
    sizes = dict(ident=128, lower=128, ones=128, headsum=128, iota=128, kdec=RH, kdec_s=RH,
                 cdec=2, cdec_s=2, bmask=NB, tabwin=WIN, tabsel=WIN, chunkbase=4, tabnew=4 * 128,
                 tabcmp=32, pick=4 * 128, headmask=24)
    late = dict(distp=384, distcmp=2 * 4, dmask=RH * 128, dmask_s=RH * 64, qdec=2 * 128, qmask=2 * NB * 64)
    out, ends = {}, []
    for group in (sizes, late):
        at = 0
        for k, n in group.items():
            out[k] = (at, n)
            at += n
        ends.append(at)
    return out, ends[0], ends[1], set(late)


def constants():
    import numpy as np
    lay, n, n_late, late = const_layout()
    early, retention = np.zeros((128, n), np.float32), np.zeros((128, n_late), np.float32)

    def put(name, a):
        a = np.asarray(a, np.float64).reshape(a.shape[0], -1)
        o, w = lay[name]
        c = retention if name in late else early
        assert a.shape[1] == w, (name, a.shape, w)
        c[:a.shape[0], o:o + w] = a.astype(np.float32)

    p = np.arange(128)
    put("ident", np.eye(128))
    put("lower", (p[:, None] < p[None, :]) * 1.0)
    put("ones", np.ones((128, 128)))
    r = p
    b2, g, i, t = r // 64, r // 32 % 2, r // 8 % 4, r % 8
    put("headsum", ((b2[:, None] == b2) & (g[:, None] == g) & (t[:, None] == t)) * 1.0)
    put("iota", np.tile(np.arange(128.0), (128, 1)))
    lg = np.log1p(-np.exp2(-5.0 - np.arange(RH)))
    d = p[None, :] - p[:, None]
    put("dmask", np.stack([np.where(d >= 0, np.exp(lg[h] * np.maximum(d, 0)), 0) for h in range(RH)], 1))
    q = np.arange(64)
    ds = q[None, :] - q[:, None]
    same = (q[None, :] // 8 == q[:, None] // 8) & (ds >= 0)
    put("dmask_s", np.stack([np.where(same, np.exp(lg[h] * np.maximum(ds, 0)), 0) for h in range(RH)], 1))
    hp = p // 64
    put("qdec", np.stack([np.exp(lg[2 * k + hp][:, None] * (np.arange(128) + 1.0)) for k in range(2)], 1))
    put("kdec", np.exp(lg[None, :] * (127.0 - p[:, None])))
    put("kdec_s", np.exp(lg[None, :] * (7.0 - (q % 8)[:, None])))
    put("cdec", np.stack([np.exp(lg[2 * k + hp] * 128) for k in range(2)], 1))
    put("cdec_s", np.stack([np.exp(lg[2 * k + hp] * 8) for k in range(2)], 1))
    put("bmask", (q[:, None] // 8 == np.arange(8)) * 1.0)
    qm = np.stack([np.exp(lg[2 * k + hp][:, None] * (q % 8 + 1.0)) for k in range(2)], 1)
    put("qmask", qm[:, :, None, :] * (np.arange(8)[:, None] == q // 8)[None, None])
    slope = np.exp2(-1.0 * (g * 4 + i + 1))
    ts = PAST + t
    near = ts[:, None] - (PAST - WIN + np.arange(WIN))[None, :]
    put("tabwin", np.where(near < WIN, -slope[:, None] * near, NEG))
    put("tabsel", -slope[:, None] * near)
    put("chunkbase", slope[:, None] * 512.0 * (np.arange(4) - 3)[None, :])
    new = []
    for k in range(4):
        ok = (q[None, :] // 8 == (2 * k + b2)[:, None]) & ((q % 8)[None, :] <= t[:, None])
        new.append(np.tile(np.where(ok, -slope[:, None] * (t[:, None] - (q % 8)[None, :]), NEG), (1, 2)))
    put("tabnew", np.stack(new, 1))
    put("tabcmp", -slope[:, None] * (ts[:, None] - ((np.arange(32) + 1) * 64 - 1)[None, :]))
    put("pick", np.stack([(q[:, None] == ((2 * k + b2) * 8 + t)[None, :]) * 1.0 for k in range(4)], 1))
    put("headmask", np.repeat((np.arange(8)[None, :] == (g * 4 + i)[:, None]) * 1.0, 3, 1))
    far = 1e33
    k0, k1 = p[None, :], np.arange(256)[None, :]
    d0, d1 = p[:, None] - k0, 128 + p[:, None] - k1
    put("distp", np.concatenate([np.where(d0 >= 0, d0, far), np.where(d1 >= 0, d1, far)], 1))
    ce = (np.arange(4) + 1) * 64 - 1
    dc = np.arange(256)[:, None] - ce[None, :]
    dc = np.where(dc >= 0, dc, far)
    put("distcmp", np.stack([dc[:128], dc[128:]], 1))
    return early, retention


def jobs():
    out = [("proj", j) for j in range(NTILE)]
    out += [(w, m) for m in range(3) for w in ("rowsA", "rowsB", "rowsC", "rowsD")]
    out += [("gates",)]
    out += [("sw", 0, c) for c in range(6)] + [("sc", 0), ("imp", 0), ("vc", 0)]
    for p in range(4):
        out += [("pt", p, q) for q in range(6)]
        if p < 3:
            out += [("sw", p + 1, c) for c in range(6)] + [("sc", p + 1)]
        out += [("o", p)]
        if p < 3:
            out += [("imp", p + 1), ("vc", p + 1)]
    out += [("pcv",)] + [("pc", qi, g) for qi in range(2) for g in range(2)]
    out += [("ps", 0, 0), ("ps", 0, 4)] + [("pct", qi, g) for qi in range(2) for g in range(2)]
    for n in range(9):
        if n < 7:
            out += [("ps", (n + 1) // 4, (n + 1) % 4), ("ps", (n + 1) // 4, (n + 1) % 4 + 4)]
        if n >= 1:
            out += [("po", (n - 1) // 4, (n - 1) % 4)]
        if n < 8:
            out += [("ppt", n // 4, n % 4), ("ppt", n // 4, n % 4 + 4)]
    for c in range(3):
        out += [("att", c, 0), ("att", c, 1), ("ro", c, 0), ("ro", c, 1)]
        out += [("rS", c)] if c < 2 else [("ri", 0), ("ri", 1), ("rS_s", 0), ("rS_s", 1)]
    out += [("cv", m) for m in range(3)] + [("mx", m) for m in range(3)]
    out += [("wo", m, c) for m in range(3) for c in range(2)]
    out += [("hT", m, c) for m in range(3) for c in range(2)]
    out += [("router", m) for m in range(3)]
    out += [(w, m, c) for m in range(3) for c in range(2) for w in ("plg", "ple")]
    out += [("rank", m) for m in range(3)] + [("count",), ("GT",)]
    out += [("bd", m, c) for m in range(3) for c in range(2)]
    return {n: k for k, n in enumerate(out)}


def build(nc, A, O):
    from contextlib import ExitStack
    import concourse.bass as bass
    from concourse import mybir

    f32, f32r, i32, u32 = mybir.dt.float32, mybir.dt.float32r, mybir.dt.int32, mybir.dt.uint32
    ALU, ACT, AX = mybir.AluOpType, mybir.ActivationFunctionType, mybir.AxisListType.X
    MUL, ADD, SUB, MAXOP = ALU.mult, ALU.add, ALU.subtract, ALU.max
    JOB = jobs()
    LAY, NCONST, NLATE, LATE = const_layout()
    TE, VE, SE, GE = nc.tensor, nc.vector, nc.scalar, nc.gpsimd
    ctx = ExitStack()
    with ctx:
        def sem(name):
            return ctx.enter_context(nc.semaphore(name))

        def many(name, n):
            return [sem(f"{name}{k}") for k in range(n)]

        SLOT = 2048
        SIZE = 52960 - 8 * SLOT
        with nc.sbuf_tensor("early", [128, 8 * SLOT], f32) as early_part:
            pass
        w_hi = ctx.enter_context(nc.sbuf_tensor("w_hi", [128, 3, SLOT], f32r))
        w_lo = ctx.enter_context(nc.sbuf_tensor("w_lo", [128, 3, SLOT], f32r))
        x_split = ctx.enter_context(nc.sbuf_tensor("x_split", [128, 4, 8 * CAP], f32r))
        arena = ctx.enter_context(nc.sbuf_tensor("arena", [128, SIZE], f32))
        page_ids = ctx.enter_context(nc.sbuf_tensor("page_ids", [1, NB * NPG], i32))
        items_i = ctx.enter_context(nc.sbuf_tensor("items_i", [1, 1], i32))
        top_i = ctx.enter_context(nc.sbuf_tensor("top_i", [128, 3, 8], u32))
        conv_w = ctx.enter_context(nc.sbuf_tensor("conv_w", [128, 2, CK + 1], f32))
        psum = ctx.enter_context(nc.psum_tensor("psum", [128, 8, 512], f32))

        def split(a, dims):
            if len(dims) == 1:
                return a
            names = "abcd"[:len(dims)]
            return a.rearrange(f"p ({' '.join(names)}) -> p {' '.join(names)}",
                               **{x: d for x, d in zip(names, dims)})

        class Cut:

            def __init__(self, at, end, of=None):
                self.at, self.end, self.of = at, end, arena if of is None else of

            def take(self, *dims):
                a = self.of[:, self.at:self.at + math.prod(dims)]
                self.at += math.prod(dims)
                assert self.at <= self.end, (dims, self.at, self.end)
                return split(a, dims)

        U0 = 4 * SLOT
        C0 = U0 + NTILE * NT
        R0 = C0 + NCONST
        M0 = R0 + 3 * (768 + 24 + 768)
        X0 = M0 + KT * NT
        ec0 = Cut(0, 8 * SLOT, early_part)
        slots01, slots23 = Cut(0, U0).take(2, NPG, 2, 128), ec0.take(2, NPG, 2, 128)
        sel_slot = [slots01[:, 0], slots01[:, 1], slots23[:, 0], slots23[:, 1]]
        cmp_slot = ec0.take(2, NPG, 2, 128)
        w_out = Cut(0, U0).take(KT, D)
        w_plg = Cut(0, 4 * SLOT, early_part).take(KT, D)
        w_ple = Cut(4 * SLOT, 5 * SLOT, early_part).take(2, D)
        late_sb = early_part[:, 5 * SLOT:5 * SLOT + NLATE]
        assert NLATE <= 2 * SLOT
        retc = Cut(7 * SLOT, 8 * SLOT, early_part)
        s_in, q_wide = retc.take(2, NB, 64), retc.take(2, NB, 64)
        uT = Cut(U0, C0).take(NTILE, NT)
        early_sb = arena[:, C0:C0 + NCONST]

        def const(name, *dims):
            o, n = LAY[name]
            return split((late_sb if name in LATE else early_sb)[:, o:o + n], dims or (n,))

        ident, ones = const("ident"), const("ones")
        rc = Cut(R0, M0)
        kvR = rc.take(3, 6, 128)
        gateR = rc.take(3, 24)
        rvR, rgR, rkR = rc.take(3, 256), rc.take(3, 256), rc.take(3, 256)
        xT = Cut(M0, X0).take(KT, NT)
        mixT = Cut(M0, X0).take(KT, NT)
        hT = mixT
        xc = Cut(X0, SIZE)
        w_in = Cut(X0 + 3 * 1024, SIZE).take(4, KT, 128)
        win = xc.take(4, 2, 512)
        PT = xc.take(22, 128)
        assert xc.at <= X0 + 3072 + 4096
        xc.at = X0 + 3072 + 4096
        convP, convS, convY = xc.take(2, CK - 1 + NPR), xc.take(2, NB, CK - 1 + TS), xc.take(2, NT)
        vecs = xc.take(3, CC)
        cm, vcr = xc.take(NB, 2, 32), xc.take(2, 128)
        pc2 = Cut(X0, X0 + 3072 + 4096)
        Sp, PTp = pc2.take(4, 2, 256), pc2.take(4, 4, 128)
        pcT, vcp = pc2.take(16, 128), pc2.take(128)
        pcs = pc2.take(16, 4)
        v_wide = Cut(X0, X0 + 2048).take(RH, NB, 64)
        sm = xc
        cmp_p = sm.take(2, 4)
        pcm, pgc, score, score2, score3 = sm.take(32), sm.take(32), sm.take(40), sm.take(40), sm.take(40)
        selb, st = sm.take(32), sm.take(32)
        gsig, gs, gtmp = sm.take(3, 24), sm.take(4, 3), split(PT[:, 0, 0:96], (4, 24))
        mx, nmx, sums, fac = sm.take(4), sm.take(4), sm.take(4), sm.take(4)
        t8a, t8b = sm.take(8), sm.take(8)
        mxp, nmxp, sump, facp = sm.take(4, 2), sm.take(4, 2), sm.take(4, 2), sm.take(4, 2)
        mc8, sc8 = sm.take(16), sm.take(16)
        stats, mv, rstd = sm.take(4, 6), sm.take(4, 2), sm.take(4)
        su = Cut(U0 + 11 * NT, C0)
        S, Qbd, Vnew = su.take(2688), su.take(NB, 64), su.take(128)
        ru = Cut(U0 + 11 * NT, C0)
        attT, q_dec, kd = ru.take(RH, 128), ru.take(2, 128), ru.take(256)
        S1, S2 = ru.take(2, 64), ru.take(2, 64)
        retR, convR, sig = ru.take(3, 256), ru.take(3, 256), ru.take(3, 256)
        conv_t = Cut(C0 - NPR, C0).take(NPR)
        assert ru.at <= C0 - NPR and su.at <= C0 - NPR
        acc = Cut(U0, C0).take(3, D)
        h = Cut(U0 + 3 * D, C0).take(3, D)
        ln = Cut(R0, M0).take(4, D)
        ec = Cut(X0, SIZE)
        wr, br, pT = ec.take(KT, NE), ec.take(NE), ec.take(2, NT)
        bup = ec.take(NE, 16)
        NI = ROUNDS * NE
        rank_all, gate_all = ec.take(3, NI + 8), ec.take(3, NI + 8)
        Mk, G = ec.take(3, NE), ec.take(3, NE)
        lg, etmp, top8, idxf, g4 = ec.take(NE), ec.take(NE), ec.take(8), ec.take(8), ec.take(8)
        r1 = ec.take(8)
        stats2, mv2, rstd2 = ec.take(2, 6), ec.take(2), ec.take(1)
        P, PG, PGT = ec.take(3, CAP), ec.take(3, CAP), ec.take(384)
        hu, y = ec.take(2 * FF), ec.take(D)
        gg, uu = ec.take(8, CAP), ec.take(8, CAP)
        act_sb = Cut(U0 + 6 * D, C0).take(8, CAP)
        chunk_in = [arena[:, k * SLOT:(k + 1) * SLOT] for k in range(4)] + [arena[:, R0:R0 + SLOT], arena[:, M0:M0 + SLOT]]
        assert SLOT <= KT * NT and SLOT == 2 * D
        bdn = hu[:, 0:D]
        sg = hu[:, D:2 * D]
        GTs = y[:, 0:NT]
        assert ec.at <= SIZE
        x_hi, x_lo, act_hi, act_lo = (x_split[:, k].rearrange("p (k n) -> p k n", k=8) for k in range(4))

        bank_full, bank_free = many("bank_full", 8), many("bank_free", 8)
        const_in, late_in, x_in, ids_in = sem("const_in"), sem("late_in"), sem("x_in"), sem("ids_in")
        w_in_here, cmp_here, sel_here = many("w_in_here", 4), many("cmp_here", 2), many("sel_here", 4)
        batch_means = sem("batch_means")
        conv_in, vec_in, wout_in, plg_in, ple_in = sem("conv_in"), sem("vec_in"), sem("wout_in"), sem("plg_in"), sem("ple_in")
        sin_in, xrow_in, ln1_in, ln2_in, moe_in = sem("sin_in"), sem("xrow_in"), sem("ln1_in"), sem("ln2_in"), sem("moe_in")
        vnew_in = sem("vnew_in")
        conv_e, conv_ready = sem("conv_e"), sem("conv_ready")
        gsig_ready, qbd_ready = sem("gsig_ready"), sem("qbd_ready")
        means_ready, cmp_max, cmp_exp, pcm_ready = sem("means_ready"), sem("cmp_max"), sem("cmp_exp"), sem("pcm_ready")
        pgc_ready = sem("pgc_ready")
        s_max, s_exp, s_fac, s_scaled = sem("s_max"), sem("s_exp"), sem("s_fac"), sem("s_scaled")
        pmean_ready, pc_max, pc_exp, pc_ready = sem("pmean_ready"), sem("pc_max"), sem("pc_exp"), sem("pc_ready")
        p_max, p_exp, p_fac, p_scaled = sem("p_max"), sem("p_exp"), sem("p_fac"), sem("p_scaled")
        kd_ready, qd_ready, rets_ready = sem("kd_ready"), sem("qd_ready"), sem("rets_ready")
        ret_e, ret_done, convn_in, conv_sig, mix_ready = sem("ret_e"), sem("ret_done"), sem("convn_in"), sem("conv_sig"), sem("mix_ready")
        states_ready = sem("states_ready")
        h_ready, top_ready, top_exp, sig_e = sem("h_ready"), sem("top_ready"), sem("top_exp"), sem("sig_e")
        mask_ready, G_ready, items_ready, rank_ready = sem("mask_ready"), sem("G_ready"), sem("items_ready"), sem("rank_ready")
        w_here, hi_ready, lo_ready, lo_ready2, chunk_used = many("w_here", 6), sem("hi_ready"), sem("lo_ready"), sem("lo_ready2"), sem("chunk_used")
        xlo_ready, act_hi_ready, act_lo_ready = sem("xlo_ready"), sem("act_hi_ready"), sem("act_lo_ready")
        P_ready, PG_ready, gathered, xg_ready = sem("P_ready"), sem("PG_ready"), sem("gathered"), sem("xg_ready")
        up_done, hu_ready, PG_turned, PGT_ready = sem("up_done"), sem("hu_ready"), sem("PG_turned"), sem("PGT_ready")
        hu_turned, g_ready, e_ready, act_ready = sem("hu_turned"), sem("g_ready"), sem("e_ready"), sem("act_ready")
        y_stored, var_ready, std_ready = sem("y_stored"), sem("var_ready"), sem("std_ready")
        y_ready, scattered, added, y_out = sem("y_ready"), sem("scattered"), sem("added"), sem("y_out")
        rows_out, states_out, wincopy_out, conv_out = sem("rows_out"), sem("states_out"), sem("wincopy_out"), sem("conv_out")
        dve_step, act_step, pool_step, dve_loop, dve_tail = sem("dve_step"), sem("act_step"), sem("pool_step"), sem("dve_loop"), sem("dve_tail")

        def bank(job):
            return JOB[job] % 8

        def ps(job):
            return psum[:, bank(job), :]

        def full(eng, job):
            eng.wait_ge(bank_full[bank(job)], JOB[job] // 8 + 1)

        def freed(eng, job):
            eng.wait_ge(bank_free[bank(job)], JOB[job] // 8 + 1)

        def open_bank(pe, job):
            if JOB[job] >= 8:
                pe.wait_ge(bank_free[bank(job)], JOB[job] // 8)

        def steps(eng, s, start=0):
            n = [0]

            def seen(ins):
                n[0] += 1
                ins.then_inc(s, 1)
                eng.wait_ge(s, start + n[0])
            seen.count = n
            return seen

        DVE_COLS = 3 * SLOT // 4
        CONV_STEPS = 2 * 2 * (1 + 2 * (CK - 1))
        NSLOPE = [-(2.0 ** -(hh + 1)) for hh in range(HEADS)]
        block = ctx.enter_context(nc.Block())

        @block.sync
        def _(sp):
            sp.dma_start(page_ids[:, :], A["page_table"]).then_inc(ids_in, 16)

            page_regs = [sp.alloc_register(f"page{n}") for n in range(4)]

            def page_value(reg):
                return sp.snap(reg, min_val=0, max_val=A["pages"].shape[0] - 1)

            def page_loads(b, dst, part, here):
                with sp.Fori(0, NPG // 4) as k:
                    sp.load(page_regs, page_ids[0:1, bass.ds(k * 4 + b * NPG, 4)])
                    pages = [page_value(reg) for reg in page_regs]
                    for n, page in enumerate(pages):
                        sp.dma_start(dst[:, bass.ds(k * 1024 + n * 256, 256)],
                                     A["pages"][bass.ds(page, 1), :, part * 256:part * 256 + 256].rearrange("a p n -> (a p) n")).then_inc(here, 16)

            def cmp_load(b):
                if b >= 2:
                    sp.wait_ge(batch_means, b - 1)
                page_loads(b, cmp_slot[:, b % 2].rearrange("p a b c -> p (a b c)"), 0, cmp_here[b % 2])

            def sel_load(b):
                if b >= 4:
                    full(sp, ("o", (b - 4) // 2))
                elif b == 3:
                    full(sp, ("proj", NTILE - 1))
                page_loads(b, sel_slot[b % 4].rearrange("p a b c -> p (a b c)"), 1, sel_here[b % 4])
                sp.dma_start(win[:, b % 4], A["windows"][b]).then_inc(sel_here[b % 4], 16)

            sp.dma_start(early_sb, A["early"]).then_inc(const_in, 16)
            sp.wait_ge(ids_in, 16)
            for b in (0, 1):
                cmp_load(b)
            for b in (0, 1):
                sel_load(b)
            for b in range(2, NB):
                cmp_load(b)
            for b in (2, 3):
                sel_load(b)
            sp.wait_ge(batch_means, NB)
            sp.dma_start(late_sb, A["late"]).then_inc(late_in, 16)
            sp.dma_start(s_in, A["state_ret"]).then_inc(sin_in, 16)
            sp.dma_start(w_ple, A["w_ple"]).then_inc(ple_in, 16)
            for b in range(4, NB):
                sel_load(b)
            full(sp, ("o", 2))
            sp.dma_start(w_out, A["w_out"]).then_inc(wout_in, 16)
            full(sp, ("o", 3))
            sp.dma_start(w_plg, A["w_plg"]).then_inc(plg_in, 16)
            freed(sp, ("rS_s", 1))
            sp.dma_start(acc[:, 0:2], A["x_rows"][0:256].rearrange("(m p) d -> p m d", p=128)).then_inc(xrow_in, 16)
            sp.dma_start(acc[0:64, 2], A["x_rows"][256:320]).then_inc(xrow_in, 16)
            sp.wait_ge(rows_out, 16 * 13)
            sp.wait_ge(conv_out, 48)
            full(sp, ("mx", 2))
            sp.dma_start(ln, A["ln"]).then_inc(ln1_in, 16)
            sp.dma_start(wr, A["w_router"]).then_inc(moe_in, 16)
            sp.dma_start(br, A["b_router"]).then_inc(moe_in, 16)
            sp.dma_start(pT, A["pT"]).then_inc(moe_in, 16)
            sp.dma_start(bup, A["b_up"]).then_inc(moe_in, 16)
            sp.dma_start(bdn[0:NE, :], A["b_down"]).then_inc(moe_in, 16)

            up = A["w_up"].rearrange("e (k p) n -> e k p n", p=128)
            down = A["w_down"].rearrange("e (k a p) n -> e k p a n", p=128, a=2)

            def weights(e, c):
                if c < 8:
                    dst, src = chunk_in[c % 6], up[e, c] if isinstance(e, int) else up[bass.ds(e, 1), c].rearrange("e p n -> (e p) n")
                else:
                    dst = chunk_in[c % 6].rearrange("p (a n) -> p a n", a=2)
                    src = down[e, c - 8] if isinstance(e, int) else down[bass.ds(e, 1), c - 8].rearrange("e p a n -> (e p) a n")
                sp.dma_start(dst, src).then_inc(w_here[c % 6], 16)

            full(sp, ("wo", 2, 1))
            for c in range(4):
                weights(0, c)
            sp.wait_ge(h_ready, 3)
            weights(0, 4)
            full(sp, ("ple", 2, 1))
            weights(0, 5)

            def item_loads(i, e, e_next):
                for c in range(6, 18):
                    sp.wait_ge(lo_ready, i * 12 + (c + 1))
                    sp.wait_ge(lo_ready2, i * 12 + (c + 1))
                    weights(e if c < 12 else e_next, c % 12)

            sp.wait_ge(items_ready, 1)
            n_items = sp.value_load(items_i[0:1, 0:1], min_val=NE, max_val=NI)
            with sp.Fori(0, ROUNDS) as r:
                with sp.If(n_items > r * NE):
                    with sp.Fori(0, NE - 1) as e:
                        item_loads(r * NE + e, e, e + 1)
                    item_loads(r * NE + (NE - 1), NE - 1, 0)

        @block.tensor
        def _(pe):
            def mm(out, lhsT, rhs, start, stop):
                return TE.matmul(out, lhsT, rhs, start=start, stop=stop, skip_group_check=True)

            def turn(out, in_):
                return TE.transpose(out, in_, ident[0:in_.shape[0], 0:in_.shape[0]])

            def close(ins, job):
                ins.then_inc(bank_full[bank(job)], 1)

            def tok(m):
                return slice(m * 128, m * 128 + MT[m])

            pe.wait_ge(x_in, 16)
            for j in range(NTILE):
                job = ("proj", j)
                open_bank(pe, job)
                pe.wait_ge(w_in_here[j % 4], 16 * (j // 4 + 1))
                for k in range(KT):
                    last = mm(ps(job)[:, 0:NT], w_in[:, j % 4, k], xT[:, k], k == 0, k == KT - 1)
                close(last, job)
            pe.wait_ge(const_in, 16)
            for j in range(NTILE):
                freed(pe, ("proj", j))
            for m in range(3):
                for what, tiles in (("rowsA", (TCK, TCV, TSK, TSV)), ("rowsB", (TWK, TWV, TGATE)),
                                    ("rowsC", (TRV, TRV + 1, TRG, TRG + 1)), ("rowsD", (TRK, TRK + 1))):
                    job = (what, m)
                    open_bank(pe, job)
                    for n, t in enumerate(tiles):
                        K = 24 if t == TGATE else 128
                        last = turn(ps(job)[0:MT[m], n * 128:n * 128 + K], uT[0:K, t, tok(m)])
                    close(last, job)
            open_bank(pe, ("gates",))
            pe.wait_ge(gsig_ready, 3)
            for p in range(4):
                last = mm(ps(("gates",))[:, 24 * p:24 * p + 24], const("pick", 4, 128)[0:64, p], gsig[0:64, 2], True, True)
            close(last, ("gates",))

            pe.wait_ge(qbd_ready, 1)
            pe.wait_ge(batch_means, NB)
            half = [slice(b2 * 64, b2 * 64 + 64) for b2 in range(2)]

            def sample_cmp(p):
                job = ("sc", p)
                open_bank(pe, job)
                for b2 in range(2):
                    last = mm(ps(job)[half[b2], 0:32], Qbd[:, 2 * p + b2], cm[:, 2 * p + b2, 0], True, True)
                close(last, job)

            def sample_values(p):
                job = ("vc", p)
                open_bank(pe, job)
                for b2 in range(2):
                    last = turn(ps(job)[0:32, b2 * 128:b2 * 128 + 128], cm[:, 2 * p + b2, 1])
                close(last, job)

            def sample_importance(p):
                job = ("imp", p)
                open_bank(pe, job)
                pe.wait_ge(pcm_ready, p + 1)
                close(mm(ps(job)[:, 0:32], const("headsum"), pcm, True, True), job)

            def sample_scores(p):
                for c in range(6):
                    job = ("sw", p, c)
                    open_bank(pe, job)
                    for b2 in range(2):
                        b = 2 * p + b2
                        pe.wait_ge(sel_here[b % 4], 16 * 17 * (b // 4 + 1))
                        if c == 0:
                            last = mm(ps(job)[half[b2], :], Qbd[:, b], win[:, b % 4, 0], True, True)
                        elif c == 1:
                            mm(ps(job)[half[b2], 0:64], Qbd[:, b], uT[:, TWK, NPR:NT], True, True)
                            last = mm(ps(job)[half[b2], 64:128], Qbd[:, b], uT[:, TSK, NPR:NT], True, True)
                        else:
                            q = 4 * (c - 2)
                            last = mm(ps(job)[half[b2], :], Qbd[:, b], sel_slot[b % 4][:, q:q + 4, 0], True, True)
                    close(last, job)

            def sample_output(p, b2):
                job, cols, b = ("o", p), half[b2], 2 * p + b2
                out = ps(job)[:, cols]
                mm(out, vcr[0:32, b2], PT[0:32, 21, cols], True, False)
                for t in range(21):
                    v = (win[:, b % 4, 1, t * 128:t * 128 + 128] if t < 4 else
                         Vnew if t == 4 else sel_slot[b % 4][:, t - 5, 1])
                    last = mm(out, v, PT[:, t, cols], False, t == 20)
                return last

            sample_scores(0)
            sample_cmp(0)
            sample_importance(0)
            sample_values(0)
            for p in range(4):
                for q in range(6):
                    job = ("pt", p, q)
                    open_bank(pe, job)
                    pe.wait_ge(s_scaled, 2 * p + (1 if q == 0 else 2))
                    if q < 5:
                        for k in range(4):
                            last = turn(ps(job)[:, k * 128:k * 128 + 128], S[:, (4 * q + k) * 128:(4 * q + k) * 128 + 128])
                    else:
                        turn(ps(job)[:, 0:128], S[:, 2560:2688])
                        pe.wait_ge(pgc_ready, p + 1)
                        last = turn(ps(job)[0:32, 128:256], pgc)
                    close(last, job)
                if p < 3:
                    sample_scores(p + 1)
                    sample_cmp(p + 1)
                open_bank(pe, ("o", p))
                freed(pe, ("vc", p))
                pe.wait_ge(vnew_in, 32)
                for q in range(6):
                    freed(pe, ("pt", p, q))
                sample_output(p, 0)
                if p < 3:
                    sample_importance(p + 1)
                close(sample_output(p, 1), ("o", p))
                if p < 3:
                    sample_values(p + 1)

            job = ("pcv",)
            open_bank(pe, job)
            pe.wait_ge(pmean_ready, 1)
            close(turn(ps(job)[0:4, 0:128], cmp_p[:, 1]), job)

            def prompt_scores(qi, hh):
                i, g = hh % 4, hh // 4
                gp = slice(g * 64, g * 64 + 64)
                Kq = 128 * (qi + 1)
                job = ("ps", qi, hh)
                open_bank(pe, job)
                q = uT[gp, TQ + i, qi * 128:qi * 128 + 128]
                mm(ps(job)[:, 0:Kq], q, uT[gp, TSK, 0:Kq], True, True)
                close(mm(ps(job)[:, 256:256 + Kq], q, uT[gp, TWK, 0:Kq], True, True), job)

            for qi in range(2):
                for g in range(2):
                    job = ("pc", qi, g)
                    open_bank(pe, job)
                    gp = slice(g * 64, g * 64 + 64)
                    for i in range(4):
                        last = mm(ps(job)[:, 4 * i:4 * i + 4], uT[gp, TQ + i, qi * 128:qi * 128 + 128], cmp_p[gp, 0], True, True)
                    close(last, job)
            prompt_scores(0, 0)
            prompt_scores(0, 4)
            pe.wait_ge(pc_ready, 1)
            for qi in range(2):
                for g in range(2):
                    job = ("pct", qi, g)
                    open_bank(pe, job)
                    for k in range(4):
                        last = turn(ps(job)[0:4, k * 128:k * 128 + 128], pcs[:, 8 * qi + 4 * g + k])
                    close(last, job)

            def prompt_turn(n):
                qi, i = n // 4, n % 4
                for g in range(2):
                    m = 2 * n + g
                    job = ("ppt", qi, i + 4 * g)
                    open_bank(pe, job)
                    pe.wait_ge(p_scaled, m + 1)
                    for b2 in range(2):
                        for k in range(qi + 1):
                            c = (b2 * (qi + 1) + k) * 128
                            last = turn(ps(job)[:, c:c + 128], Sp[:, m % 4, b2, k * 128:k * 128 + 128])
                    close(last, job)

            def prompt_output(n):
                qi, i = n // 4, n % 4
                job = ("po", qi, i)
                open_bank(pe, job)
                for g in range(2):
                    m = 2 * n + g
                    gp = slice(g * 64, g * 64 + 64)
                    freed(pe, ("ppt", qi, i + 4 * g))
                    out = ps(job)[gp, 0:128]
                    mm(out, vcp[0:4, gp], pcT[0:4, 8 * qi + i + 4 * g], True, False)
                    for b2 in range(2):
                        for k in range(qi + 1):
                            last = mm(out, kvR[:, k, 3 + 2 * b2, gp], PTp[:, m % 4, b2 * (qi + 1) + k], False,
                                      b2 == 1 and k == qi)
                close(last, job)

            freed(pe, ("pcv",))
            for qi in range(2):
                for g in range(2):
                    freed(pe, ("pct", qi, g))
            for n in range(9):
                if n < 7:
                    prompt_scores((n + 1) // 4, (n + 1) % 4)
                    prompt_scores((n + 1) // 4, (n + 1) % 4 + 4)
                if n >= 1:
                    prompt_output(n - 1)
                if n < 8:
                    prompt_turn(n)

            def head(hh):
                return slice((hh % 2) * 64, (hh % 2) * 64 + 64)

            for c in range(3):
                M = MT[c]
                for z in range(2):
                    job = ("att", c, z)
                    open_bank(pe, job)
                    for hh in (z, z + 2):
                        last = mm(ps(job)[0:M, hh * 128:hh * 128 + M], uT[head(hh), TRK + hh // 2, tok(c)],
                                  uT[head(hh), TRQ + hh // 2, tok(c)], True, True)
                    close(last, job)
                if c == 1:
                    freed(pe, ("rS", 0))
                    pe.wait_ge(qd_ready, 1)
                if c == 2:
                    pe.wait_ge(rets_ready, 1)
                    pe.wait_ge(sin_in, 16)
                for z in range(2):
                    job = ("ro", c, z)
                    open_bank(pe, job)
                    freed(pe, ("att", c, z))
                    for hh in (z, z + 2):
                        out = ps(job)[0:M, hh * 64:hh * 64 + 64]
                        last = mm(out, attT[0:M, hh, 0:M], rvR[0:M, c, hh * 64:hh * 64 + 64], True, c != 1)
                        if c == 1:
                            last = mm(out, q_dec[head(hh), hh // 2], S1[head(hh), hh // 2], False, True)
                    close(last, job)
                if c < 2:
                    job = ("rS", c)
                    open_bank(pe, job)
                    pe.wait_ge(kd_ready, c + 1)
                    for hh in range(RH):
                        last = mm(ps(job)[head(hh), (hh // 2) * 64:(hh // 2) * 64 + 64], kd[:, hh * 64:hh * 64 + 64],
                                  rvR[:, c, hh * 64:hh * 64 + 64], True, True)
                    close(last, job)
            for z in range(2):
                job = ("ri", z)
                open_bank(pe, job)
                for hh in (z, z + 2):
                    for b in range(NB):
                        last = mm(ps(job)[0:64, hh * 64:hh * 64 + 64], q_wide[head(hh), hh // 2, b],
                                  s_in[head(hh), hh // 2, b], b == 0, b == NB - 1)
                close(last, job)
            for hp in range(2):
                job = ("rS_s", hp)
                open_bank(pe, job)
                for hh in (2 * hp, 2 * hp + 1):
                    last = mm(ps(job)[head(hh), :], kd[0:64, hh * 64:hh * 64 + 64], v_wide[0:64, hh], True, True)
                close(last, job)
            pe.wait_ge(pool_step, CONV_STEPS)
            for m in range(3):
                job = ("cv", m)
                open_bank(pe, job)
                for k in range(2):
                    last = turn(ps(job)[0:MT[m], k * 128:k * 128 + 128], convY[:, k, tok(m)])
                close(last, job)
            for m in range(3):
                job = ("mx", m)
                open_bank(pe, job)
                pe.wait_ge(mix_ready, m + 1)
                for k in range(4):
                    src = (convR if k < 2 else retR)[0:MT[m], m, (k % 2) * 128:(k % 2) * 128 + 128]
                    last = turn(ps(job)[:, k * 128:k * 128 + MT[m]], src)
                close(last, job)
            pe.wait_ge(wout_in, 16)
            for p in range(4):
                freed(pe, ("o", p))
            for qi in range(2):
                for i in range(4):
                    freed(pe, ("po", qi, i))
            for m in range(3):
                freed(pe, ("mx", m))
                for c in range(2):
                    job = ("wo", m, c)
                    open_bank(pe, job)
                    for k in range(KT):
                        last = mm(ps(job)[0:MT[m], :], mixT[:, k, tok(m)], w_out[:, k, c * 512:c * 512 + 512], k == 0, k == KT - 1)
                    close(last, job)
            for m in range(3):
                for c in range(2):
                    job = ("hT", m, c)
                    open_bank(pe, job)
                    pe.wait_ge(h_ready, m + 1)
                    for k in range(4):
                        d = (4 * c + k) * 128
                        last = turn(ps(job)[:, k * 128:k * 128 + MT[m]], h[0:MT[m], m, d:d + 128])
                    close(last, job)
            pe.wait_ge(moe_in, 16 * 5)
            for m in range(3):
                job = ("router", m)
                open_bank(pe, job)
                freed(pe, ("hT", m, 0))
                freed(pe, ("hT", m, 1))
                for k in range(KT):
                    last = mm(ps(job)[0:MT[m], 0:NE], hT[:, k, tok(m)], wr[:, k], k == 0, k == KT - 1)
                close(last, job)
            pe.wait_ge(plg_in, 16)
            pe.wait_ge(ple_in, 16)
            for m in range(3):
                for c in range(2):
                    for what, w, x, K in (("plg", w_plg, hT, KT), ("ple", w_ple, pT, 2)):
                        job = (what, m, c)
                        open_bank(pe, job)
                        for k in range(K):
                            last = mm(ps(job)[0:MT[m], :], x[:, k, tok(m)], w[:, k, c * 512:c * 512 + 512], k == 0, k == K - 1)
                        close(last, job)
            pe.wait_ge(mask_ready, 3)
            for m in range(3):
                job = ("rank", m)
                open_bank(pe, job)
                for j in range(m + 1):
                    w = const("lower") if j == m else ones
                    last = mm(ps(job)[0:MT[m], 0:NE], w[0:MT[j], 0:MT[m]], Mk[0:MT[j], j], j == 0, j == m)
                close(last, job)
            job = ("count",)
            open_bank(pe, job)
            for j in range(3):
                last = mm(ps(job)[:, 0:NE], ones[0:MT[j], :], Mk[0:MT[j], j], j == 0, j == 2)
            close(last, job)
            job = ("GT",)
            open_bank(pe, job)
            for m in range(3):
                last = turn(ps(job)[0:NE, tok(m)], G[0:MT[m], m])
            close(last, job)
            freed(pe, ("GT",))
            for m in range(3):
                for c in range(2):
                    job = ("bd", m, c)
                    open_bank(pe, job)
                    close(mm(ps(job)[0:MT[m], :], GTs[0:NE, tok(m)], bdn[0:NE, c * 512:c * 512 + 512], True, True), job)

            for job in list(JOB)[-8:]:
                freed(pe, job)

            def gather(i1):
                pe.wait_ge(P_ready, i1)
                for k in range(KT):
                    if k == 4:
                        pe.wait_ge(PGT_ready, i1)
                    for m in range(3):
                        last = mm(psum[:, 6 + k // 4, (k % 4) * CAP:(k % 4 + 1) * CAP], h[0:MT[m], m, k * 128:k * 128 + 128],
                                  P[0:MT[m], m], m == 0, m == 2)
                last.then_inc(gathered, 1)

            def scatter(i):
                pe.wait_ge(y_ready, i + 1)
                pe.wait_ge(PGT_ready, i + 1)
                for n in range(6):
                    m, c = n // 2, n % 2
                    if n >= 2:
                        pe.wait_ge(added, i * 6 + (n - 1))
                    mm(psum[:, 6 + c, :], PGT[0:CAP, m * 128:m * 128 + 128], y[0:CAP, c * 512:c * 512 + 512], True, True)\
                        .then_inc(scattered, 1)

            gather(1)
            n_ready = items_ready
            pe.wait_ge(n_ready, 1)
            n_items = pe.value_load(items_i[0:1, 0:1], min_val=NE, max_val=NI)
            with pe.Fori(0, ROUNDS) as r:
                with pe.If(n_items > r * NE):
                    with pe.Fori(0, NE) as e:
                        i = r * NE + e
                        pe.wait_ge(xg_ready, i + 1)
                        pe.wait_ge(xlo_ready, i + 1)
                        for k in range(KT):
                            pe.wait_ge(hi_ready, i * 12 + (k + 1))
                            for n, x in [(n, x) for x in (x_hi, x_lo) for n in range(4)]:
                                mm(psum[0:CAP, n, :], x[:, k], w_hi[:, k % 3, n * 512:n * 512 + 512], k == 0 and x is x_hi, False)
                            pe.wait_ge(lo_ready, i * 12 + (k + 7))
                            for n in range(4):
                                if n == 3:
                                    pe.wait_ge(lo_ready2, i * 12 + (k + 7))
                                last = mm(psum[0:CAP, n, :], x_hi[:, k], w_lo[:, k % 3, n * 512:n * 512 + 512], False, k == KT - 1)
                                if k == KT - 1 and n < 3:
                                    last.then_inc(up_done, 1)
                            last.then_inc(chunk_used, 1)
                        scatter(i)
                        pe.wait_ge(added, i * 6 + 6)
                        pe.wait_ge(PG_ready, i + 1)
                        for m in range(3):
                            last = turn(psum[:, 7, tok(m)], PG[0:MT[m], m])
                        last.then_inc(PG_turned, 1)
                        pe.wait_ge(hu_ready, i * 4 + 4)
                        for half_ in range(2):
                            for s in range(2):
                                for j in range(4 * half_, 4 * half_ + 4):
                                    cols = hu[:, 2 * j * 128 + s:2 * (j + 1) * 128:2]
                                    last = turn(psum[:, 2 * half_ + s, (j % 4) * CAP:(j % 4 + 1) * CAP], cols)
                            last.then_inc(hu_turned, 1)
                        gather(i + 2)
                        for q in range(4):
                            c12 = 8 + q
                            if q % 2 == 0:
                                pe.wait_ge(act_hi_ready, i * 2 + (q // 2 + 1))
                                pe.wait_ge(act_lo_ready, i * 2 + (q // 2 + 1))
                            pe.wait_ge(hi_ready, i * 12 + (c12 + 1))
                            for a, c, x in [(a, c, x) for a in range(2) for x in (act_hi, act_lo) for c in range(2)]:
                                mm(psum[0:CAP, 4 + c, :], x[:, 2 * q + a], w_hi[:, c12 % 3, a * D + c * 512:a * D + c * 512 + 512],
                                   q == 0 and a == 0 and x is act_hi, False)
                            pe.wait_ge(lo_ready, i * 12 + (c12 + 7))
                            for a, c in ((0, 0), (0, 1), (1, 0), (1, 1)):
                                if (a, c) == (1, 1):
                                    pe.wait_ge(lo_ready2, i * 12 + (c12 + 7))
                                last = mm(psum[0:CAP, 4 + c, :], act_hi[:, 2 * q + a],
                                          w_lo[:, c12 % 3, a * D + c * 512:a * D + c * 512 + 512], False, q == 3 and a == 1)
                            last.then_inc(chunk_used, 1)
            scatter(n_items)

        @block.scalar
        def _(act):
            seen = steps(act, act_step)

            def root(n, v):
                act.wait_ge(var_ready, n + 1)
                SE.activation(v, v, ACT.Sqrt).then_inc(std_ready, 1)

            def take(job, *pairs):
                full(act, job)
                for dst, src in pairs:
                    last = SE.activation(dst, src, ACT.Copy)
                last.then_inc(bank_free[bank(job)], 1)

            def tile_load(j):
                act.dma_start(w_in[:, j % 4], A["w_in"][j]).then_inc(w_in_here[j % 4], 16)

            act.dma_start(xT, A["xT"]).then_inc(x_in, 16)
            for j in range(4):
                tile_load(j)
            act.dma_start(convS[:, 0, :, 0:CK - 1], A["state_conv"][:, 0]).then_inc(conv_in, 16)
            act.dma_start(convS[:, 1, :, 0:CK - 1], A["state_conv"][:, 1]).then_inc(conv_in, 16)
            act.dma_start(conv_w[:, :, :], A["conv_w"]).then_inc(conv_in, 16)
            act.dma_start(vecs, A["vecs"]).then_inc(vec_in, 16)
            for j in range(NTILE):
                full(act, ("proj", j))
                scale = 0.125 if j in (TQ, TQ + 1, TQ + 2, TQ + 3, TRK, TRK + 1) else 1.0
                SE.activation(uT[:, j], ps(("proj", j))[:, 0:NT], ACT.Copy, scale=scale).then_inc(bank_free[bank(("proj", j))], 1)
                if j + 4 < NTILE:
                    tile_load(j + 4)
            freed(act, ("proj", TG))
            freed(act, ("proj", TG + 1))
            SE.activation(uT[:, TG:TG + 2], uT[:, TG:TG + 2], ACT.Sigmoid).then_inc(conv_e, 1)
            for m in range(3):
                M = MT[m]
                b = ps(("rowsB", m))
                take(("rowsB", m), (kvR[0:M, m, 4:6], b[0:M, 0:256].rearrange("p (a b) -> p a b", a=2)),
                     (gateR[0:M, m], b[0:M, 256:280]))
                freed(act, ("rowsB", m))
                SE.activation(gsig[0:M, m], gateR[0:M, m], ACT.Sigmoid).then_inc(gsig_ready, 1)
                take(("rowsD", m), (rkR[0:M, m], ps(("rowsD", m))[0:M, 0:256]))
            freed(act, ("rowsA", 2))
            full(act, ("rowsD", 2))
            act.wait_ge(conv_ready, 1)
            act.dma_start(Vnew[0:64], kvR[0:64, 2, 5]).then_inc(vnew_in, 16)
            act.dma_start(Vnew[64:128], kvR[0:64, 2, 3]).then_inc(vnew_in, 16)

            def exp_s(p, n):
                a, b = ((0, 576), (576, 2688))[n]
                act.wait_ge(s_max, 2 * p + n + 1)
                SE.activation(S[:, a:b], S[:, a:b], ACT.Exp, bias=nmx[:, n + 1:n + 2],
                              accum_out=sums[:, n + 1:n + 2]).then_inc(s_exp, 1)

            def scale_s(p, n):
                a, b = ((0, 576), (576, 2688))[n]
                act.wait_ge(s_fac, 2 * p + n + 1)
                SE.activation(S[:, a:b], S[:, a:b], ACT.Copy, scale=fac[:, n + 1:n + 2]).then_inc(s_scaled, 1)

            for p in range(4):
                exp_s(p, 0)
                act.wait_ge(cmp_max, p + 1)
                SE.activation(st, st, ACT.Exp, bias=nmx[:, 0:1], accum_out=sums[:, 0:1]).then_inc(cmp_exp, 1)
                scale_s(p, 0)
                exp_s(p, 1)
                scale_s(p, 1)
                if p:
                    full(act, ("o", p - 1))
                take(("vc", p), (vcr[0:32], ps(("vc", p))[0:32, 0:256].rearrange("p (a b) -> p a b", a=2)))
                for q in (0, 2, 4):
                    take(("pt", p, q), (PT[:, 4 * q:4 * q + 4], ps(("pt", p, q)).rearrange("p (a b) -> p a b", a=4)))

            full(act, ("o", 3))
            take(("pcv",), (vcp[0:4], ps(("pcv",))[0:4, 0:128]))
            act.wait_ge(pc_max, 1)
            SE.activation(pcs, pcs, ACT.Exp).then_inc(pc_exp, 1)

            def soften(m):
                Kq = 128 * (m // 8 + 1)
                for b2 in range(2):
                    act.wait_ge(p_max, 2 * m + b2 + 1)
                    SE.activation(Sp[:, m % 4, b2, 0:Kq], Sp[:, m % 4, b2, 0:Kq], ACT.Exp, bias=nmxp[:, m % 4, b2:b2 + 1],
                                  accum_out=sump[:, m % 4, b2:b2 + 1]).then_inc(p_exp, 1)

            def scale_p(m):
                act.wait_ge(p_fac, m + 1)
                Kq = 128 * (m // 8 + 1)
                for b2 in range(2):
                    last = SE.activation(Sp[:, m % 4, b2, 0:Kq], Sp[:, m % 4, b2, 0:Kq], ACT.Copy, scale=facp[:, m % 4, b2:b2 + 1])
                last.then_inc(p_scaled, 1)

            soften(0)
            soften(1)
            for qi in range(2):
                for g in range(2):
                    take(("pct", qi, g), (pcT[0:4, 8 * qi + 4 * g:8 * qi + 4 * g + 4],
                                          ps(("pct", qi, g))[0:4].rearrange("p (a b) -> p a b", a=4)))
            for n in range(8):
                scale_p(2 * n)
                scale_p(2 * n + 1)
                if n < 7:
                    soften(2 * n + 2)
                    soften(2 * n + 3)
            full(act, ("po", 1, 3))
            freed(act, ("rowsC", 2))
            SE.activation(sig[:, 0:2], rgR[:, 0:2], ACT.Sigmoid).then_inc(ret_e, 1)
            SE.activation(sig[0:64, 2], rgR[0:64, 2], ACT.Sigmoid).then_inc(ret_e, 1)
            for m in range(3):
                root(m, rstd[0:MT[m]])
            for m in range(3):
                root(3 + m, rstd[0:MT[m], 0:1])
            for m in range(3):
                act.wait_ge(convn_in, m + 1)
                M = MT[m]
                SE.activation(sig[0:M, m], convR[0:M, m], ACT.Sigmoid).then_inc(conv_sig, 1)
            for m in range(3):
                root(6 + m, rstd2[0:MT[m]])
            for m in range(3):
                M = MT[m]
                act.wait_ge(top_ready, m + 1)
                SE.activation(g4[0:M, 0:4], top8[0:M, 0:4], ACT.Exp, bias=r1[0:M, 0:1], accum_out=r1[0:M, 1:2]).then_inc(top_exp, 1)
            for m in range(3):
                M = MT[m]
                for c in range(2):
                    job = ("plg", m, c)
                    full(act, job)
                    if m or c:
                        freed(act, ("ple", m, 0) if c else ("ple", m - 1, 1))
                    SE.activation(sg[0:M, 0:512], ps(job)[0:M], ACT.Sigmoid).then_inc(bank_free[bank(job)], 1)

            def gathered_copy(i1):
                act.wait_ge(gathered, i1)
                SE.activation(x_hi.rearrange("p (a k) n -> p a (k n)", a=2), psum[:, 6:8, :], ACT.Copy).then_inc(xg_ready, 1)

            def high(i, c):
                act.wait_ge(w_here[c % 6], i * 32 + (c // 6 * 16 + 16))
                act.wait_ge(chunk_used, i * 12 + (c + 1))
                SE.activation(w_hi[:, c % 3], chunk_in[c % 6], ACT.Copy).then_inc(hi_ready, 1)

            act.wait_ge(states_out, 32)
            full(act, ("ple", 2, 1))
            for c in range(3):
                high(0, c)
            gathered_copy(1)
            act.wait_ge(items_ready, 1)
            n_items = act.value_load(items_i[0:1, 0:1], min_val=NE, max_val=NI)
            with act.Fori(0, ROUNDS) as r:
                with act.If(n_items > r * NE):
                    with act.Fori(0, NE) as e:
                        i = r * NE + e
                        for c in range(3, 10):
                            high(i, c)
                        for n in range(4):
                            if n < 3:
                                act.wait_ge(up_done, i * 3 + (n + 1))
                            else:
                                act.wait_ge(chunk_used, i * 12 + (KT + 3))
                            last = SE.activation(hu[0:CAP, n * 512:n * 512 + 512], psum[0:CAP, n, :], ACT.Copy)
                            last.then_inc(hu_ready, 1)
                        high(i, 10)
                        act.wait_ge(PG_turned, i + 1)
                        SE.activation(PGT[0:CAP, 0:NT], psum[0:CAP, 7, 0:NT], ACT.Copy).then_inc(PGT_ready, 1)
                        for half_ in range(2):
                            act.wait_ge(g_ready, i * 2 + (half_ + 1))
                            js = slice(4 * half_, 4 * half_ + 4)
                            SE.activation(act_sb[:, js], gg[:, js], ACT.Sigmoid, scale=SALPHA).then_inc(e_ready, 1)
                        for half_ in range(2):
                            act.wait_ge(act_ready, i * 2 + (half_ + 1))
                            js = slice(4 * half_, 4 * half_ + 4)
                            SE.activation(act_hi[:, js], act_sb[:, js], ACT.Copy).then_inc(act_hi_ready, 1)
                        gathered_copy(i + 2)
                        for c in range(11, 15):
                            high(i, c)
                        SE.activation(y[0:CAP].rearrange("p (c n) -> p c n", c=2), psum[0:CAP, 4:6, :], ACT.Copy).then_inc(y_ready, 1)

            for c in (3, 4, 5):
                act.wait_ge(w_here[c], n_items * 32 + 16)
            for m in range(3):
                root(9 + m, rstd2[0:MT[m]])

        @block.vector
        def _(dve):
            seen = steps(dve, dve_step)

            def take(job, *pairs):
                full(dve, job)
                for dst, src in pairs:
                    last = VE.tensor_copy(dst, src)
                last.then_inc(bank_free[bank(job)], 1)
                freed(dve, job)

            roots = [0]

            def inverse_root(seen, out, var):
                roots[0] += 1
                VE.tensor_scalar(out, var, EPS, None, ADD).then_inc(var_ready, 1)
                dve.wait_ge(std_ready, roots[0])
                seen(VE.reciprocal(out, out))

            def normed(seen, src, dst, n, width, mvt, stt, rs):
                for k in range(n):
                    w = width // n
                    seen(VE.bn_stats(stt[:, k], src[:, k * w:(k + 1) * w]))
                seen(VE.bn_aggr(mvt, stt[:, 0:n]))
                inverse_root(seen, rs, mvt[:, 1:2])
                seen(VE.tensor_scalar(dst, src, mvt[:, 0:1], rs, SUB, MUL))

            for k in range(2):
                VE.memset(convP[:, k, 0:CK - 1], 0.0)
            seen(VE.memset(score, -1.0))
            def cache_means(b):
                dve.wait_ge(cmp_here[b % 2], 16 * NPG * (b // 2 + 1))
                for kind in range(2):
                    last = VE.tensor_reduce(cm[:, b, kind].rearrange("p (a b) -> p a b", b=2),
                                            cmp_slot[:, b % 2, :, kind].rearrange("p a (b s) -> p a b s", b=2), AX, ADD)
                seen(last)
                VE.tensor_scalar(cm[:, b], cm[:, b], 1.0 / 64, None, MUL).then_inc(batch_means, 1)

            for b in range(6):
                cache_means(b)
            seen(VE.memset(score[:, 0:1], 1e4))
            seen(VE.memset(score[:, 31:33], 1e4))
            dve.wait_ge(conv_e, 1)
            freed(dve, ("proj", TA))
            freed(dve, ("proj", TA + 1))
            dve.wait_ge(conv_in, 48)
            VE.tensor_tensor(convP[:, :, CK - 1:], uT[:, TA:TA + 2, 0:NPR], uT[:, TG:TG + 2, 0:NPR], MUL)
            for k in range(2):
                last = VE.tensor_tensor(convS[:, k, :, CK - 1:], uT[:, TA + k, NPR:NT].rearrange("p (b t) -> p b t", t=TS),
                                        uT[:, TG + k, NPR:NT].rearrange("p (b t) -> p b t", t=TS), MUL)
            last.then_inc(conv_ready, 1)
            for b in range(6, NB):
                cache_means(b)
            for m in range(3):
                M = MT[m]
                a, c = ps(("rowsA", m)), ps(("rowsC", m))
                take(("rowsA", m), (kvR[0:M, m, 0:4], a[0:M].rearrange("p (a b) -> p a b", a=4)))
                take(("rowsC", m), (rvR[0:M, m], c[0:M, 0:256]), (rgR[0:M, m], c[0:M, 256:512]))
            for kind, t in enumerate((TCK, TCV)):
                seen(VE.tensor_reduce(cmp_p[:, kind], uT[:, t, 0:NPR].rearrange("p (n s) -> p n s", s=64), AX, ADD))
            VE.tensor_scalar(cmp_p, cmp_p, 1.0 / 64, None, MUL).then_inc(pmean_ready, 1)
            full(dve, ("rowsD", 2))
            seen(VE.memset(Qbd, 0.0))
            for g in range(2):
                gp = slice(g * 64, g * 64 + 64)
                last = VE.tensor_copy(Qbd[gp, :, g * 32:g * 32 + 32].rearrange("p b (i t) -> p b i t", t=TS),
                                      uT[gp, TQ:TQ + 4, NPR:NT].rearrange("p i (b t) -> p b i t", t=TS))
                if g == 0:
                    seen(last)
            last.then_inc(qbd_ready, 1)
            full(dve, ("gates",))
            VE.tensor_tensor(gtmp, ps(("gates",))[:, 0:96].rearrange("p (a b) -> p a b", a=4),
                             const("headmask").unsqueeze(1).to_broadcast([128, 4, 24]), MUL).then_inc(bank_free[bank(("gates",))], 1)
            freed(dve, ("gates",))
            for p in range(4):
                last = VE.tensor_reduce(gs[:, p], gtmp[:, p].rearrange("p (h c) -> p c h", c=3), AX, ADD)
            seen(last)

            def add_bias(p):
                if p:
                    full(dve, ("pt", p - 1, 5))
                for c in range(6):
                    job = ("sw", p, c)
                    full(dve, job)
                    if c == 0:
                        last = VE.tensor_tensor(S[:, 0:512], ps(job), const("tabwin"), ADD)
                    elif c == 1:
                        last = VE.tensor_tensor(S[:, 512:640], ps(job)[:, 0:128], const("tabnew", 4, 128)[:, p], ADD)
                    else:
                        at = 640 + 512 * (c - 2)
                        last = VE.scalar_tensor_tensor(out=S[:, at:at + 512], in0=ps(job), scalar=const("chunkbase")[:, c - 2:c - 1],
                                                       in1=const("tabsel"), op0=ADD, op1=ADD)
                    last.then_inc(bank_free[bank(job)], 1)
                    if c == 1:
                        freed(dve, job)
                        seen(VE.tensor_reduce(mx[:, 1:2], S[:, 0:576], AX, MAXOP))
                        VE.tensor_scalar(nmx[:, 1:2], mx[:, 1:2], -1.0, None, MUL).then_inc(s_max, 1)
                freed(dve, ("sw", p, 5))

            def compressed(p):
                job = ("sc", p)
                full(dve, job)
                VE.tensor_tensor(st, ps(job)[:, 0:32], const("tabcmp"), ADD).then_inc(bank_free[bank(job)], 1)
                freed(dve, job)
                seen(VE.tensor_reduce(mx[:, 0:1], st, AX, MAXOP))
                VE.tensor_scalar(nmx[:, 0:1], mx[:, 0:1], -1e29, -1.0, MAXOP, MUL).then_inc(cmp_max, 1)
                factor(p, 0)
                dve.wait_ge(cmp_exp, p + 1)
                seen(VE.tensor_scalar(fac[:, 0:1], sums[:, 0:1], TINY, None, MAXOP))
                seen(VE.reciprocal(fac[:, 0:1], fac[:, 0:1]))
                VE.tensor_scalar(pcm, st, fac[:, 0:1], None, MUL).then_inc(pcm_ready, 1)
                dve.wait_ge(pcm_ready, p + 1)
                VE.tensor_scalar(pgc, pcm, gs[:, p, 0:1], None, MUL).then_inc(pgc_ready, 1)

            def select(p):
                job = ("imp", p)
                full(dve, job)
                VE.tensor_copy(score[:, 1:31], ps(job)[:, 1:31]).then_inc(bank_free[bank(job)], 1)
                freed(dve, job)
                seen(VE.max(t8a, score))
                seen(VE.match_replace(score2, t8a, score, -2.0))
                seen(VE.max(t8b, score2))
                seen(VE.match_replace(score3, t8b, score2, -2.0))
                seen(VE.tensor_scalar(selb, score3[:, 0:32], -2.0, -NEG, ALU.is_equal, MUL))
                seen(VE.tensor_scalar(selb, selb, -NEG, None, SUB))
                blocks = S[:, 640:2688].rearrange("p (n s) -> p n s", s=64)
                seen(VE.tensor_tensor(blocks, blocks, selb.unsqueeze(2).to_broadcast([128, 32, 64]), ADD))
                seen(VE.tensor_reduce(mx[:, 2:3], S[:, 576:2688], AX, MAXOP))
                VE.tensor_scalar(nmx[:, 2:3], mx[:, 2:3], -1.0, None, MUL).then_inc(s_max, 1)

            def factor(p, n):
                dve.wait_ge(s_exp, 2 * p + n + 1)
                f = fac[:, n + 1:n + 2]
                seen(VE.tensor_scalar(f, sums[:, n + 1:n + 2], TINY, None, MAXOP))
                seen(VE.reciprocal(f, f))
                VE.tensor_scalar(f, f, gs[:, p, 2 - n:3 - n], None, MUL).then_inc(s_fac, 1)

            add_bias(0)
            compressed(0)
            select(0)
            for p in range(4):
                factor(p, 1)
                if p:
                    full(dve, ("o", p - 1))
                for q in (1, 3):
                    take(("pt", p, q), (PT[:, 4 * q:4 * q + 4], ps(("pt", p, q)).rearrange("p (a b) -> p a b", a=4)))
                b = ps(("pt", p, 5))
                take(("pt", p, 5), (PT[:, 20], b[:, 0:128]), (PT[0:32, 21], b[0:32, 128:256]))
                if p < 3:
                    add_bias(p + 1)
                    compressed(p + 1)
                    select(p + 1)
                src = ps(("o", p))[:, 0:128].rearrange("p (b g i t) -> p b g i t", b=2, g=2, i=4)
                cols = slice(NPR + 16 * p, NPR + 16 * p + 16)
                full(dve, ("o", p))
                for g in range(2):
                    gp = slice(g * 64, g * 64 + 64)
                    last = VE.tensor_copy(mixT[gp, 2:6, cols].rearrange("p i (b t) -> p i b t", b=2),
                                          src[gp, :, g].rearrange("p b i t -> p i b t"))
                last.then_inc(bank_free[bank(("o", p))], 1)

            def prompt_scores(n):
                qi, hh = n // 8, (n % 8) // 2 + 4 * (n % 2)
                Kq = 128 * (qi + 1)
                job = ("ps", qi, hh)
                full(dve, job)
                dist = const("distp")[:, 0:128] if qi == 0 else const("distp")[:, 128:384]
                if n >= 4:
                    m = n - 4
                    full(dve, ("ppt", m // 8, (m % 8) // 2 + 4 * (m % 2)))
                VE.scalar_tensor_tensor(out=Sp[:, n % 4, :, 0:Kq], in0=dist.unsqueeze(1).to_broadcast([128, 2, Kq]),
                                        scalar=NSLOPE[hh], in1=ps(job).rearrange("p (a b) -> p a b", a=2)[:, :, 0:Kq],
                                        op0=MUL, op1=ADD).then_inc(bank_free[bank(job)], 1)
                freed(dve, job)
                seen(VE.tensor_reduce(mxp[:, n % 4], Sp[:, n % 4, :, 0:Kq], AX, MAXOP))
                VE.tensor_scalar(nmxp[:, n % 4], mxp[:, n % 4], -1.0, None, MUL).then_inc(p_max, 2)

            def prompt_factor(n):
                qi, hh = n // 8, (n % 8) // 2 + 4 * (n % 2)
                dve.wait_ge(p_exp, 2 * n + 2)
                f = facp[:, n % 4]
                seen(VE.tensor_scalar(f, sump[:, n % 4], TINY, None, MAXOP))
                seen(VE.reciprocal(f, f))
                VE.tensor_tensor(f, f, gsig[:, qi, 3 * hh + 1:3 * hh + 3], MUL).then_inc(p_fac, 1)

            dve.wait_ge(late_in, 16)
            for qi in range(2):
                for g in range(2):
                    job = ("pc", qi, g)
                    full(dve, job)
                    for i in range(4):
                        last = VE.scalar_tensor_tensor(out=pcs[:, 8 * qi + 4 * g + i], in0=const("distcmp", 2, 4)[:, qi], scalar=NSLOPE[4 * g + i],
                                                       in1=ps(job)[:, 4 * i:4 * i + 4], op0=MUL, op1=ADD)
                    last.then_inc(bank_free[bank(job)], 1)
            freed(dve, ("pc", 1, 1))
            seen(VE.tensor_reduce(mc8, pcs, AX, MAXOP))
            seen(VE.tensor_scalar(mc8, mc8, -1e29, None, MAXOP))
            VE.tensor_tensor(pcs, pcs, mc8.unsqueeze(2).to_broadcast([128, 16, 4]), SUB).then_inc(pc_max, 1)
            prompt_scores(0)
            prompt_scores(1)
            dve.wait_ge(pc_exp, 1)
            seen(VE.tensor_reduce(sc8, pcs, AX, ADD))
            seen(VE.tensor_scalar(sc8, sc8, TINY, None, MAXOP))
            seen(VE.reciprocal(sc8, sc8))
            seen(VE.tensor_tensor(sc8.rearrange("p (q h) -> p q h", q=2), sc8.rearrange("p (q h) -> p q h", q=2),
                                  gsig[:, 0:2].rearrange("p q (h c) -> p q h c", c=3)[:, :, :, 0], MUL))
            VE.tensor_tensor(pcs, pcs, sc8.unsqueeze(2).to_broadcast([128, 16, 4]), MUL).then_inc(pc_ready, 1)
            for n in range(9):
                if n < 8:
                    prompt_factor(2 * n)
                    prompt_factor(2 * n + 1)
                if n < 7:
                    prompt_scores(2 * n + 2)
                    prompt_scores(2 * n + 3)
                if n >= 1:
                    qi, i = (n - 1) // 4, (n - 1) % 4
                    take(("po", qi, i), (mixT[:, 2 + i, qi * 128:qi * 128 + 128], ps(("po", qi, i))[:, 0:128]))
                if n < 8:
                    qi, i = n // 4, n % 4
                    w = 256 * (qi + 1)
                    for g in range(2):
                        if n >= 2:
                            full(dve, ("po", (n - 2) // 4, (n - 2) % 4))
                        job = ("ppt", qi, i + 4 * g)
                        take(job, (PTp[:, (2 * n + g) % 4].rearrange("p a b -> p (a b)")[:, 0:w], ps(job)[:, 0:w]))

            for m in range(3):
                freed(dve, ("rowsD", m))

            def heads(a):
                return a.rearrange("p (h e) -> p h e", h=RH)

            def weigh(c, decay):
                M = MT[c]
                for z in range(2):
                    job = ("att", c, z)
                    full(dve, job)
                    VE.tensor_tensor(attT[0:M, z::2, 0:M], ps(job)[0:M].rearrange("p (h e) -> p h e", h=RH)[:, z::2, 0:M],
                                     decay[0:M, z::2], MUL).then_inc(bank_free[bank(job)], 1)

            def take_ro(c):
                M = MT[c]
                for z in range(2):
                    job = ("ro", c, z)
                    take(job, (heads(retR[0:M, c])[:, z::2], heads(ps(job)[0:M, 0:256])[:, z::2]))

            for c in range(2):
                if c:
                    full(dve, ("rS", 0))
                VE.tensor_tensor(heads(kd), heads(rkR[:, c]), const("kdec").unsqueeze(2).to_broadcast([128, RH, 64]), MUL)\
                    .then_inc(kd_ready, 1)
                if c:
                    full(dve, ("ro", 0, 1))
                    VE.tensor_tensor(q_dec, uT[:, TRQ:TRQ + 2, 128:256], const("qdec", 2, 128), MUL).then_inc(qd_ready, 1)
                weigh(c, const("dmask", RH, 128))
                take_ro(c)
                job = ("rS", c)
                if c == 0:
                    take(job, (S1, ps(job)[:, 0:128].rearrange("p (h e) -> p h e", h=2)))
                else:
                    full(dve, job)
                    for hp in range(2):
                        last = VE.scalar_tensor_tensor(out=S2[:, hp], in0=S1[:, hp], scalar=const("cdec")[:, hp:hp + 1],
                                                       in1=ps(job)[:, hp * 64:hp * 64 + 64], op0=MUL, op1=ADD)
                    last.then_inc(bank_free[bank(job)], 1)
            VE.tensor_tensor(heads(kd[0:64]), heads(rkR[0:64, 2]), const("kdec_s")[0:64].unsqueeze(2).to_broadcast([64, RH, 64]), MUL)
            for hp in range(2):
                VE.tensor_tensor(q_wide[:, hp], uT[:, TRQ + hp, NPR:NT].unsqueeze(1).to_broadcast([128, NB, 64]),
                                 const("qmask", 2, NB, 64)[:, hp], MUL)
            for hh in range(RH):
                last = VE.tensor_tensor(v_wide[0:64, hh], rvR[0:64, 2, hh * 64:hh * 64 + 64].unsqueeze(1).to_broadcast([64, NB, 64]),
                                        const("bmask")[0:64].unsqueeze(2).to_broadcast([64, NB, 64]), MUL)
            last.then_inc(rets_ready, 1)
            weigh(2, const("dmask_s", RH, 64))
            take_ro(2)
            for z in range(2):
                job = ("ri", z)
                full(dve, job)
                o = heads(retR[0:64, 2])[:, z::2]
                VE.tensor_tensor(o, o, heads(ps(job)[0:64, 0:256])[:, z::2], ADD).then_inc(bank_free[bank(job)], 1)
                freed(dve, job)
            dve.wait_ge(sin_in, 16)
            for hp in range(2):
                job = ("rS_s", hp)
                full(dve, job)
                VE.scalar_tensor_tensor(out=s_in[:, hp], in0=s_in[:, hp], scalar=const("cdec_s")[:, hp:hp + 1],
                                        in1=ps(job).rearrange("p (b e) -> p b e", b=NB), op0=MUL, op1=ADD)\
                    .then_inc(bank_free[bank(job)], 1)
            dve.wait_ge(vec_in, 16)
            dve.wait_ge(ret_e, 2)
            for m in range(3):
                M = MT[m]
                seen(VE.tensor_tensor(sig[0:M, m], sig[0:M, m], rgR[0:M, m], MUL))
                for hh in range(RH):
                    seen(VE.bn_stats(stats[0:M, hh], retR[0:M, m, hh * 64:hh * 64 + 64]))
                    seen(VE.bn_aggr(mv[0:M, hh], stats[0:M, hh]))
                inverse_root(seen, rstd[0:M], mv[0:M, :, 1])
                for hh in range(RH):
                    x = retR[0:M, m, hh * 64:hh * 64 + 64]
                    last = VE.tensor_scalar(x, x, mv[0:M, hh, 0:1], rstd[0:M, hh:hh + 1], SUB, MUL)
                seen(last)
                seen(VE.tensor_tensor(retR[0:M, m], retR[0:M, m], vecs[0:M, 2], MUL))
                last = VE.tensor_tensor(retR[0:M, m], retR[0:M, m], sig[0:M, m], MUL)
                if m == 2:
                    last.then_inc(ret_done, 1)
                else:
                    seen(last)
            dve.wait_ge(ret_done, 1)
            for m in range(3):
                M = MT[m]
                take(("cv", m), (convR[0:M, m], ps(("cv", m))[0:M, 0:256]))
                normed(seen, convR[0:M, m], convR[0:M, m], 1, CC, mv[0:M, 0], stats[0:M], rstd[0:M, 0:1])
                seen(VE.tensor_tensor(convR[0:M, m], convR[0:M, m], vecs[0:M, 0], MUL))
                VE.tensor_tensor(convR[0:M, m], convR[0:M, m], vecs[0:M, 1], ADD).then_inc(convn_in, 1)
            for m in range(3):
                M = MT[m]
                dve.wait_ge(conv_sig, m + 1)
                VE.tensor_tensor(convR[0:M, m], convR[0:M, m], sig[0:M, m], MUL).then_inc(mix_ready, 1)
            for m in range(3):
                M, job = MT[m], ("mx", m)
                t = slice(m * 128, m * 128 + M)
                b = ps(job).rearrange("p (k n) -> p k n", k=4)
                take(job, (mixT[:, 0:2, t], b[:, 0:2, 0:M]), (mixT[:, 6:8, t], b[:, 2:4, 0:M]))

            dve.wait_ge(xrow_in, 32)
            dve.wait_ge(ln1_in, 16)
            dve.wait_ge(states_out, 32)
            for m in range(3):
                M = MT[m]
                for c in range(2):
                    job = ("wo", m, c)
                    full(dve, job)
                    z = acc[0:M, m, c * 512:c * 512 + 512]
                    VE.scalar_tensor_tensor(out=z, in0=z, scalar=ALPHA, in1=ps(job)[0:M], op0=MUL, op1=ADD).then_inc(bank_free[bank(job)], 1)
                    freed(dve, job)
                normed(seen, acc[0:M, m], h[0:M, m], 2, D, mv2[0:M], stats2[0:M], rstd2[0:M])
                seen(VE.tensor_tensor(h[0:M, m], h[0:M, m], ln[0:M, 0], MUL))
                VE.tensor_tensor(h[0:M, m], h[0:M, m], ln[0:M, 1], ADD).then_inc(h_ready, 1)
            dve.wait_ge(h_ready, 3)
            full(dve, ("wo", 2, 1))
            for m in range(3):
                for c in range(2):
                    job = ("hT", m, c)
                    M = MT[m]
                    take(job, (hT[:, 4 * c:4 * c + 4, m * 128:m * 128 + M], ps(job).rearrange("p (k n) -> p k n", k=4)[:, :, 0:M]))
            dve.wait_ge(moe_in, 16 * 5)
            for m in range(3):
                M, job = MT[m], ("router", m)
                full(dve, job)
                VE.tensor_tensor(lg[0:M], ps(job)[0:M, 0:NE], br[0:M], ADD).then_inc(bank_free[bank(job)], 1)
                freed(dve, job)
                seen(VE.max(top8[0:M], lg[0:M]))
                seen(VE.max_index(top_i[0:M, m, :], top8[0:M], lg[0:M]))
                seen(VE.tensor_copy(idxf[0:M], top_i[0:M, m, :]))
                VE.tensor_scalar(r1[0:M, 0:1], top8[0:M, 0:1], -1.0, None, MUL).then_inc(top_ready, 1)
                seen(VE.memset(Mk[0:M, m], 0.0))
                seen(VE.memset(G[0:M, m], 0.0))
                for k in range(TOPK):
                    last = VE.scalar_tensor_tensor(out=Mk[0:M, m], in0=const("iota")[0:M, 0:NE], scalar=idxf[0:M, k:k + 1], in1=Mk[0:M, m],
                                                   op0=ALU.is_equal, op1=ADD)
                    if k < TOPK - 1:
                        seen(last)
                last.then_inc(mask_ready, 1)
                dve.wait_ge(top_exp, m + 1)
                seen(VE.reciprocal(r1[0:M, 2:3], r1[0:M, 1:2]))
                seen(VE.tensor_scalar(g4[0:M, 0:4], g4[0:M, 0:4], r1[0:M, 2:3], None, MUL))
                for k in range(TOPK):
                    seen(VE.tensor_scalar(etmp[0:M], const("iota")[0:M, 0:NE], idxf[0:M, k:k + 1], g4[0:M, k:k + 1], ALU.is_equal, MUL))
                    seen(VE.tensor_tensor(G[0:M, m], G[0:M, m], etmp[0:M], ADD))
            for m in range(3):
                M = MT[m]
                for c in range(2):
                    cols = slice(c * 512, c * 512 + 512)
                    freed(dve, ("plg", m, c))
                    s = sg[0:M, 0:512]
                    job = ("ple", m, c)
                    full(dve, job)
                    VE.tensor_tensor(acc[0:M, m, cols], s, ps(job)[0:M], MUL).then_inc(bank_free[bank(job)], 1)
                    freed(dve, job)
                    seen(VE.scalar_tensor_tensor(out=acc[0:M, m, cols], in0=h[0:M, m, cols], scalar=ALPHA,
                                                 in1=acc[0:M, m, cols], op0=MUL, op1=ADD))
            seen(VE.memset(rank_all, -1e4))
            seen(VE.memset(gate_all, 0.0))
            for m in range(3):
                M, job = MT[m], ("rank", m)
                full(dve, job)
                VE.scalar_tensor_tensor(out=lg[0:M], in0=ps(job)[0:M, 0:NE], scalar=1e4, in1=Mk[0:M, m], op0=ADD, op1=MUL)\
                    .then_inc(bank_free[bank(job)], 1)
                freed(dve, job)
                for r in range(ROUNDS):
                    VE.tensor_scalar(rank_all[0:M, m, r * NE:(r + 1) * NE], lg[0:M], -1e4 - CAP * r, None, ADD)
                    last = VE.tensor_copy(gate_all[0:M, m, r * NE:(r + 1) * NE], G[0:M, m])
                seen(last)
            job = ("count",)
            full(dve, job)
            VE.tensor_reduce(r1[:, 3:4], ps(job)[:, 0:NE], AX, MAXOP).then_inc(bank_free[bank(job)], 1)
            freed(dve, job)
            seen(VE.tensor_scalar(lg[:, 0:ROUNDS], const("iota")[:, 0:ROUNDS], float(CAP), r1[:, 3:4], MUL, ALU.is_lt))
            seen(VE.tensor_reduce(r1[:, 4:5], lg[:, 0:ROUNDS], AX, ADD))
            seen(VE.tensor_scalar(r1[:, 4:5], r1[:, 4:5], float(NE), None, MUL))
            VE.tensor_copy(items_i[0:1, 0:1], r1[0:1, 4:5]).then_inc(items_ready, 1)
            take(("GT",), (GTs[0:NE], ps(("GT",))[0:NE, 0:NT]))
            for m in range(3):
                M = MT[m]
                for c in range(2):
                    job = ("bd", m, c)
                    full(dve, job)
                    a = acc[0:M, m, c * 512:c * 512 + 512]
                    VE.tensor_tensor(a, a, ps(job)[0:M], ADD).then_inc(bank_free[bank(job)], 1)
                    freed(dve, job)

            def choose(seen, out, i, gated):
                for m in range(3):
                    M = MT[m]
                    if gated:
                        last = VE.tensor_scalar(out[0:M, m, 0:CAP], const("iota")[0:M], rank_all[0:M, m, bass.ds(i, 1)],
                                                gate_all[0:M, m, bass.ds(i, 1)], ALU.is_equal, MUL)
                    else:
                        last = VE.tensor_scalar(out[0:M, m], const("iota")[0:M], rank_all[0:M, m, bass.ds(i, 1)],
                                                None, ALU.is_equal)
                return last

            choose(seen, P, 0, False).then_inc(P_ready, 1)
            VE.memset(y[0:CAP], 0.0).then_inc(y_ready, 1)
            VE.memset(PGT[0:CAP], 0.0).then_inc(PGT_ready, 1)
            VE.memset(r1[:, 6:7], 0.0).then_inc(chunk_used, 3)
            VE.memset(r1[:, 7:8], 0.0).then_inc(lo_ready, 6)

            def low(i, c):
                dve.wait_ge(hi_ready, i * 12 + (c + 1))
                VE.tensor_tensor(w_lo[:, c % 3, 0:DVE_COLS], chunk_in[c % 6][:, 0:DVE_COLS], w_hi[:, c % 3, 0:DVE_COLS].bitcast(f32), SUB)\
                    .then_inc(lo_ready, 1)

            def gathered_low(i1):
                dve.wait_ge(xg_ready, i1)
                VE.tensor_tensor(x_lo.rearrange("p (a k) n -> p a (k n)", a=2), psum[:, 6:8, :],
                                 x_hi.rearrange("p (a k) n -> p a (k n)", a=2).bitcast(f32), SUB).then_inc(xlo_ready, 1)

            for c in range(3):
                low(0, c)
            gathered_low(1)
            dve.wait_ge(items_ready, 1)
            n_items = dve.value_load(items_i[0:1, 0:1], min_val=NE, max_val=NI)
            LINKS = 8

            def add_item(i, n):
                m, c = n // 2, n % 2
                dve.wait_ge(scattered, i * 6 + (n + 1))
                a = acc[0:MT[m], m, c * 512:c * 512 + 512]
                VE.tensor_tensor(a, a, psum[0:MT[m], 6 + c, :], ADD).then_inc(added, 1)

            with dve.Fori(0, ROUNDS) as r:
                with dve.If(n_items > r * NE):
                    with dve.Fori(0, NE) as e:
                        i = r * NE + e
                        lseen = steps(dve, dve_loop, i * LINKS)
                        dve.wait_ge(gathered, i + 1)
                        choose(lseen, PG, i, True).then_inc(PG_ready, 1)
                        choose(lseen, P, i + 1, False).then_inc(P_ready, 1)
                        for c in range(3, 10):
                            low(i, c)
                        for n in range(6):
                            add_item(i, n)
                        low(i, 10)
                        bias = bup[:, bass.ds(e, 1)].rearrange("p a (s j) -> p (a s) j", s=2)
                        for half_ in range(2):
                            js = slice(4 * half_, 4 * half_ + 4)
                            g_t, u_t = (psum[:, 2 * half_ + s, :].rearrange("p (j n) -> p j n", j=4) for s in range(2))
                            gate, up_, sg_ = gg[:, js], uu[:, js], act_sb[:, js]
                            dve.wait_ge(hu_turned, i * 2 + (half_ + 1))
                            lseen(VE.tensor_tensor(gate, g_t, bias[:, 0, js].unsqueeze(2).to_broadcast([128, 4, CAP]), ADD))
                            VE.tensor_scalar(gate, gate, LIMIT, None, ALU.min).then_inc(g_ready, 1)
                            lseen(VE.tensor_tensor(up_, u_t, bias[:, 1, js].unsqueeze(2).to_broadcast([128, 4, CAP]), ADD))
                            lseen(VE.tensor_scalar(up_, up_, LIMIT, -LIMIT, ALU.min, MAXOP))
                            lseen(VE.scalar_tensor_tensor(out=up_, in0=up_, scalar=1.0, in1=gate, op0=ADD, op1=MUL))
                            dve.wait_ge(e_ready, i * 2 + (half_ + 1))
                            VE.tensor_tensor(sg_, up_, sg_, MUL).then_inc(act_ready, 1)
                        for half_ in range(2):
                            js = slice(4 * half_, 4 * half_ + 4)
                            dve.wait_ge(act_hi_ready, i * 2 + (half_ + 1))
                            VE.tensor_tensor(act_lo[:, js], act_sb[:, js], act_hi[:, js].bitcast(f32), SUB).then_inc(act_lo_ready, 1)
                        gathered_low(i + 2)
                        for c in range(11, 15):
                            low(i, c)
                        assert lseen.count[0] == LINKS
            dve.wait_ge(added, n_items * 6)
            for n in range(6):
                add_item(n_items, n)
            tail = steps(dve, dve_tail)
            dve.wait_ge(added, n_items * 6 + 6)
            for m in range(3):
                M = MT[m]
                a = acc[0:M, m]
                normed(tail, a, a, 2, D, mv2[0:M], stats2[0:M], rstd2[0:M])
                tail(VE.tensor_tensor(a, a, ln[0:M, 2], MUL))
                VE.tensor_tensor(a, a, ln[0:M, 3], ADD).then_inc(y_out, 1)

        @block.gpsimd
        def _(pool):
            seen = steps(pool, pool_step)
            pool.dma_start(O["win_s"][:, 0:WIN - TS], A["cache_win"][:, TS:WIN]).then_inc(wincopy_out, 16)
            pool.wait_ge(conv_in, 48)
            pool.wait_ge(conv_ready, 1)
            full(pool, ("rowsC", 2))
            for k in range(2):
                parts = [(convY[:, k, 0:NPR], conv_t, lambda t, k=k: convP[:, k, t:t + NPR]),
                         (convY[:, k, NPR:NT].rearrange("p (b t) -> p b t", t=TS),
                          conv_t[:, 0:NSM].rearrange("p (b t) -> p b t", t=TS), lambda t, k=k: convS[:, k, :, t:t + TS])]
                for dst, tmp, src in parts:
                    seen(GE.tensor_scalar(dst, src(0), conv_w[:, k, 0:1], conv_w[:, k, CK:CK + 1], MUL, ADD))
                    for t in range(1, CK):
                        seen(GE.tensor_scalar(tmp, src(t), conv_w[:, k, t:t + 1], None, MUL))
                        seen(GE.tensor_tensor(dst, dst, tmp, ADD))
            pool.dma_start(O["conv_p"], convP[:, :, NPR:NPR + CK - 1]).then_inc(conv_out, 16)
            for k in range(2):
                pool.dma_start(O["conv_s"][:, k], convS[:, k, :, TS:TS + CK - 1]).then_inc(conv_out, 16)
            for m in range(3):
                for w in ("rowsA", "rowsB"):
                    freed(pool, (w, m))
            for m in range(2):
                pool.dma_start(O["nsa_p"][m * 128:m * 128 + 128], kvR[:, m, 0:4]).then_inc(rows_out, 16)
                pool.dma_start(O["win_p"][m * 128:m * 128 + 128], kvR[:, m, 4:6]).then_inc(rows_out, 16)
            pool.dma_start(O["nsa_s"], kvR[0:64, 2, 0:4]).then_inc(rows_out, 16)
            for b in range(NB):
                rows = kvR[b * TS:(b + 1) * TS, 2, 4:6].rearrange("p a b -> p (a b)")
                pool.dma_start(O["win_s"][b, WIN - TS:WIN], rows).then_inc(rows_out, 16)
            freed(pool, ("rS", 1))
            pool.dma_start(O["ret_p"], S2).then_inc(states_out, 16)
            freed(pool, ("rS_s", 0))
            freed(pool, ("rS_s", 1))
            pool.dma_start(O["ret_s"], s_in).then_inc(states_out, 16)
            GE.memset(conv_t[:, NPR - 1:NPR], 0.0).then_inc(lo_ready2, 6)

            def low(i, c):
                pool.wait_ge(hi_ready, i * 12 + (c + 1))
                GE.tensor_tensor(w_lo[:, c % 3, DVE_COLS:], chunk_in[c % 6][:, DVE_COLS:], w_hi[:, c % 3, DVE_COLS:].bitcast(f32), SUB)\
                    .then_inc(lo_ready2, 1)

            for c in range(3):
                low(0, c)
            pool.wait_ge(items_ready, 1)
            n_items = pool.value_load(items_i[0:1, 0:1], min_val=NE, max_val=NI)
            with pool.Fori(0, ROUNDS) as r:
                with pool.If(n_items > r * NE):
                    with pool.Fori(0, NE) as e:
                        for c in range(3, 15):
                            low(r * NE + e, c)
            for m in range(3):
                pool.wait_ge(y_out, m + 1)
                pool.dma_start(O["y"][m * 128:m * 128 + MT[m]], acc[0:MT[m], m]).then_inc(y_stored, 16)
            pool.wait_ge(conv_out, 48)
            pool.wait_ge(wincopy_out, 16)
            pool.wait_ge(rows_out, 16 * 13)
            pool.wait_ge(states_out, 32)
            pool.wait_ge(y_stored, 48)
    return nc


def lay_out(x):
    import numpy as np
    c = np.ascontiguousarray
    a = {k: np.asarray(v) for k, v in x.items()}
    rows = np.concatenate([a["x_prompt"].reshape(NPR, D), a["x_sample"].reshape(NSM, D)])
    pr = np.concatenate([a["p_prompt"].reshape(NPR, PLE), a["p_sample"].reshape(NSM, PLE)])
    w = a["w_in"][0]
    at = {}
    o = 0
    for name, n in (("a", 256), ("g", 256), ("q", 512), ("kv", 768), ("gate", 24), ("rq", 256), ("rk", 256), ("rv", 256), ("rg", 256)):
        at[name] = w[:, o:o + n]
        o += n
    q = at["q"].reshape(D, KV, GQ, HD)
    kv = at["kv"].reshape(D, 6, 128)
    cols = [q[:, :, i].reshape(D, 128) for i in range(4)] + [kv[:, 0], kv[:, 2], kv[:, 4]]
    cols += [at["rq"], at["rk"], at["a"], at["g"], kv[:, 1], kv[:, 3], kv[:, 5], at["gate"], np.zeros((D, 104), w.dtype), at["rv"], at["rg"]]
    cols = np.concatenate(cols, 1)
    assert cols.shape == (D, NTILE * 128)
    w_in = cols.reshape(KT, 128, NTILE, 128).transpose(2, 1, 0, 3)
    cache = a["cache_nsa_kv"][0].reshape(-1, PAGE, 4, 128)
    pages = np.stack([cache[:, :, 0].transpose(0, 2, 1), cache[:, :, 1].transpose(0, 2, 1),
                      cache[:, :, 2].transpose(0, 2, 1), cache[:, :, 3]], 2)
    wk = a["cache_win_kv"][0].reshape(NB, WIN, 2, 128)
    windows = np.stack([wk[:, :, 0].transpose(0, 2, 1),
                        wk[:, :, 1].reshape(NB, 4, 128, 128).transpose(0, 2, 1, 3).reshape(NB, 128, 512)], 2)
    wo = a["w_out"][0]
    att = wo[256:768].reshape(KV, GQ, HD, D).transpose(1, 0, 2, 3).reshape(512, D)
    wo = np.concatenate([wo[:256], att, wo[768:]])

    def ktiles(m):
        return m.reshape(-1, 128, m.shape[1]).transpose(1, 0, 2)

    def spread(v):
        return np.broadcast_to(v, (128,) + v.shape)

    early, late = constants()
    cw = np.concatenate([a["conv_w"][0], a["conv_b"][0][None]])
    out = dict(
        xT=ktiles(c(rows.T)), pT=ktiles(c(pr.T)), x_rows=rows, w_in=w_in, pages=pages.reshape(len(cache), 128, 512),
        windows=windows, cache_win=wk.reshape(NB, WIN, 256), page_table=a["page_table"].reshape(1, -1),
        w_out=ktiles(wo), w_plg=ktiles(a["w_plg"][0]), w_ple=ktiles(a["w_ple"][0]), w_router=ktiles(a["w_router"][0]),
        b_router=spread(a["b_router"][0]), b_down=a["b_down"][0], w_up=a["w_up"][0], w_down=a["w_down"][0],
        b_up=a["b_up"][0].reshape(NE, 8, 128, 2).transpose(2, 0, 3, 1).reshape(128, NE, 16),
        state_conv=a["state_conv"][0].transpose(2, 0, 1).reshape(2, 128, NB, CK - 1).transpose(1, 0, 2, 3),
        conv_w=cw.T.reshape(2, 128, CK + 1).transpose(1, 0, 2),
        state_ret=a["state_ret"][0].reshape(NB, 2, 2, 64, 64).transpose(2, 3, 1, 0, 4).reshape(128, 2, NB, 64),
        vecs=spread(np.stack([a["conv_ln_g"][0], a["conv_ln_b"][0], a["ret_norm_g"][0]])),
        ln=spread(np.stack([a["ln1_g"][0], a["ln1_b"][0], a["ln2_g"][0], a["ln2_b"][0]])),
        early=early, late=late)
    return {k: c(v) for k, v in out.items()}


OUTPUTS = dict(y=(NT, D), nsa_p=(NPR, 4, 128), nsa_s=(NSM, 4, 128), win_p=(NPR, 2, 128), win_s=(NB, WIN, 256),
               ret_p=(128, 2, 64), ret_s=(128, 2, NB, 64), conv_p=(128, 2, CK - 1), conv_s=(128, 2, NB, CK - 1))


def kernel(**inputs):
    import numpy as np
    import concourse.bacc as bacc
    from concourse import mybir
    from concourse.bass_utils import run_bass_kernel_spmd

    arrays = lay_out(inputs)
    nc = bacc.Bacc("TRN2", target_bir_lowering=False, num_devices=1)
    A = {k: nc.dram_tensor(f"in_{k}", v.shape, mybir.dt.from_np(v.dtype), kind="ExternalInput").ap() for k, v in arrays.items()}
    O = {k: nc.dram_tensor(f"out_{k}", s, mybir.dt.float32, kind="ExternalOutput").ap() for k, s in OUTPUTS.items()}
    build(nc, A, O)
    run = run_bass_kernel_spmd(nc, [{f"in_{k}": v for k, v in arrays.items()}], core_ids=[0])
    o = {k: np.asarray(run.results[0][f"out_{k}"]) for k in OUTPUTS}
    ret_s = o["ret_s"].reshape(2, 64, 2, NB, 64).transpose(3, 2, 0, 1, 4).reshape(1, NB, RH, 64, 64)
    ret_p = o["ret_p"].reshape(2, 64, 2, 64).transpose(2, 0, 1, 3).reshape(1, 1, RH, 64, 64)
    conv_p = o["conv_p"].transpose(2, 1, 0).reshape(1, 1, CK - 1, CC)
    conv_s = o["conv_s"].transpose(2, 3, 1, 0).reshape(1, NB, CK - 1, CC)
    return (o["y"][:NPR].reshape(1, NPR, D), o["y"][NPR:].reshape(NB, TS, D),
            o["nsa_p"].reshape(1, 1, NPR, 4, KV, HD), o["nsa_s"].reshape(1, NB, TS, 4, KV, HD),
            o["win_p"].reshape(1, 1, NPR, 2, KV, HD), o["win_s"].reshape(1, NB, WIN, 2, KV, HD),
            np.ascontiguousarray(ret_p), np.ascontiguousarray(ret_s), np.ascontiguousarray(conv_p), np.ascontiguousarray(conv_s))
```

```python
import math

F = 4
D, NPR, NB, TS = 1024, 256, 8, 8
NSM = NB * TS
NT = NPR + NSM
KT = D // 128
HD, HEADS, KV, GQ = 64, 8, 2, 4
PAST, PAGE = 2048, 128
NPG = PAST // PAGE
WIN = 512
RH, CC, CK = 4, 256, 31
NE, TOPK, FF, PLE = 32, 4, 1024, 256
CAP = 128
ROUNDS = -(-NT // CAP)
ALPHA = 2 ** 0.25
EPS, TINY, NEG = 1e-5, 1e-30, -1e30
LIMIT, SALPHA = 7.0, 1.702
MT = [128, 128, 64]
TQ, TCK, TSK, TWK, TRQ, TRK, TA, TG, TCV, TSV, TWV, TGATE, TRV, TRG = 0, 4, 5, 6, 7, 9, 11, 13, 15, 16, 17, 18, 19, 21
NTILE = 23


def const_layout():
    sizes = dict(ident=128, lower=128, ones=128, headsum=128, iota=128, kdec=RH, kdec_s=RH,
                 cdec=2, cdec_s=2, bmask=NB, tabwin=WIN, tabsel=WIN, chunkbase=4, tabnew=4 * 128,
                 tabcmp=32, pick=4 * 128, headmask=24)
    late = dict(distp=384, distcmp=2 * 4, dmask=RH * 128, dmask_s=RH * 64, qdec=2 * 128, qmask=2 * NB * 64)
    out, ends = {}, []
    for group in (sizes, late):
        at = 0
        for k, n in group.items():
            out[k] = (at, n)
            at += n
        ends.append(at)
    return out, ends[0], ends[1], set(late)


def constants():
    import numpy as np
    lay, n, n_late, late = const_layout()
    early, retention = np.zeros((128, n), np.float32), np.zeros((128, n_late), np.float32)

    def put(name, a):
        a = np.asarray(a, np.float64).reshape(a.shape[0], -1)
        o, w = lay[name]
        c = retention if name in late else early
        assert a.shape[1] == w, (name, a.shape, w)
        c[:a.shape[0], o:o + w] = a.astype(np.float32)

    p = np.arange(128)
    put("ident", np.eye(128))
    put("lower", (p[:, None] < p[None, :]) * 1.0)
    put("ones", np.ones((128, 128)))
    r = p
    b2, g, i, t = r // 64, r // 32 % 2, r // 8 % 4, r % 8
    put("headsum", ((b2[:, None] == b2) & (g[:, None] == g) & (t[:, None] == t)) * 1.0)
    put("iota", np.tile(np.arange(128.0), (128, 1)))
    lg = np.log1p(-np.exp2(-5.0 - np.arange(RH)))
    d = p[None, :] - p[:, None]
    put("dmask", np.stack([np.where(d >= 0, np.exp(lg[h] * np.maximum(d, 0)), 0) for h in range(RH)], 1))
    q = np.arange(64)
    ds = q[None, :] - q[:, None]
    same = (q[None, :] // 8 == q[:, None] // 8) & (ds >= 0)
    put("dmask_s", np.stack([np.where(same, np.exp(lg[h] * np.maximum(ds, 0)), 0) for h in range(RH)], 1))
    hp = p // 64
    put("qdec", np.stack([np.exp(lg[2 * k + hp][:, None] * (np.arange(128) + 1.0)) for k in range(2)], 1))
    put("kdec", np.exp(lg[None, :] * (127.0 - p[:, None])))
    put("kdec_s", np.exp(lg[None, :] * (7.0 - (q % 8)[:, None])))
    put("cdec", np.stack([np.exp(lg[2 * k + hp] * 128) for k in range(2)], 1))
    put("cdec_s", np.stack([np.exp(lg[2 * k + hp] * 8) for k in range(2)], 1))
    put("bmask", (q[:, None] // 8 == np.arange(8)) * 1.0)
    qm = np.stack([np.exp(lg[2 * k + hp][:, None] * (q % 8 + 1.0)) for k in range(2)], 1)
    put("qmask", qm[:, :, None, :] * (np.arange(8)[:, None] == q // 8)[None, None])
    slope = np.exp2(-1.0 * (g * 4 + i + 1))
    ts = PAST + t
    near = ts[:, None] - (PAST - WIN + np.arange(WIN))[None, :]
    put("tabwin", np.where(near < WIN, -slope[:, None] * near, NEG))
    put("tabsel", -slope[:, None] * near)
    put("chunkbase", slope[:, None] * 512.0 * (np.arange(4) - 3)[None, :])
    new = []
    for k in range(4):
        ok = (q[None, :] // 8 == (2 * k + b2)[:, None]) & ((q % 8)[None, :] <= t[:, None])
        new.append(np.tile(np.where(ok, -slope[:, None] * (t[:, None] - (q % 8)[None, :]), NEG), (1, 2)))
    put("tabnew", np.stack(new, 1))
    put("tabcmp", -slope[:, None] * (ts[:, None] - ((np.arange(32) + 1) * 64 - 1)[None, :]))
    put("pick", np.stack([(q[:, None] == ((2 * k + b2) * 8 + t)[None, :]) * 1.0 for k in range(4)], 1))
    put("headmask", np.repeat((np.arange(8)[None, :] == (g * 4 + i)[:, None]) * 1.0, 3, 1))
    far = 1e33
    k0, k1 = p[None, :], np.arange(256)[None, :]
    d0, d1 = p[:, None] - k0, 128 + p[:, None] - k1
    put("distp", np.concatenate([np.where(d0 >= 0, d0, far), np.where(d1 >= 0, d1, far)], 1))
    ce = (np.arange(4) + 1) * 64 - 1
    dc = np.arange(256)[:, None] - ce[None, :]
    dc = np.where(dc >= 0, dc, far)
    put("distcmp", np.stack([dc[:128], dc[128:]], 1))
    return early, retention


def jobs():
    out = [("proj", j) for j in range(NTILE)]
    out += [(w, m) for m in range(3) for w in ("rowsA", "rowsB", "rowsC", "rowsD")]
    out += [("gates",)]
    out += [("sw", 0, c) for c in range(6)] + [("sc", 0), ("imp", 0), ("vc", 0)]
    for p in range(4):
        out += [("pt", p, q) for q in range(6)]
        if p < 3:
            out += [("sw", p + 1, c) for c in range(6)] + [("sc", p + 1)]
        out += [("o", p)]
        if p < 3:
            out += [("imp", p + 1), ("vc", p + 1)]
    out += [("pcv",)] + [("pc", qi, g) for qi in range(2) for g in range(2)]
    out += [("ps", 0, 0), ("ps", 0, 4)] + [("pct", qi, g) for qi in range(2) for g in range(2)]
    for n in range(9):
        if n < 7:
            out += [("ps", (n + 1) // 4, (n + 1) % 4), ("ps", (n + 1) // 4, (n + 1) % 4 + 4)]
        if n >= 1:
            out += [("po", (n - 1) // 4, (n - 1) % 4)]
        if n < 8:
            out += [("ppt", n // 4, n % 4), ("ppt", n // 4, n % 4 + 4)]
    for c in range(3):
        out += [("att", c, 0), ("att", c, 1), ("ro", c, 0), ("ro", c, 1)]
        out += [("rS", c)] if c < 2 else []
        out += [("cv", c)]
    out += [("ri", 0), ("ri", 1), ("rS_s", 0), ("rS_s", 1)] + [("mx", m) for m in range(3)]
    out += [("wo", m, c) for m in range(3) for c in range(2)]
    out += [("hT", m, c) for m in range(3) for c in range(2)]
    out += [("router", m) for m in range(3)]
    out += [(w, m, c) for m in range(3) for c in range(2) for w in ("plg", "ple")]
    out += [("rank", m) for m in range(3)] + [("count",), ("GT",)]
    out += [("bd", m, c) for m in range(3) for c in range(2)]
    return {n: k for k, n in enumerate(out)}


def build(nc, A, O):
    from contextlib import ExitStack
    import concourse.bass as bass
    from concourse import mybir

    f32, f32r, i32, u32 = mybir.dt.float32, mybir.dt.float32r, mybir.dt.int32, mybir.dt.uint32
    ALU, ACT, AX = mybir.AluOpType, mybir.ActivationFunctionType, mybir.AxisListType.X
    MUL, ADD, SUB, MAXOP = ALU.mult, ALU.add, ALU.subtract, ALU.max
    JOB = jobs()
    LAY, NCONST, NLATE, LATE = const_layout()
    TE, VE, SE, GE = nc.tensor, nc.vector, nc.scalar, nc.gpsimd
    ctx = ExitStack()
    with ctx:
        def sem(name):
            return ctx.enter_context(nc.semaphore(name))

        def many(name, n):
            return [sem(f"{name}{k}") for k in range(n)]

        SLOT = 2048
        YCOLS = 2 * D + 3 * 128
        SIZE = 52960 - 8 * SLOT - YCOLS
        with nc.sbuf_tensor("early", [128, 8 * SLOT], f32) as early_part, nc.sbuf_tensor("early_rows", [128, YCOLS], f32) as early_rows:
            pass
        w_hi = ctx.enter_context(nc.sbuf_tensor("w_hi", [128, 3, SLOT], f32r))
        w_lo = ctx.enter_context(nc.sbuf_tensor("w_lo", [128, 3, SLOT], f32r))
        x_split = ctx.enter_context(nc.sbuf_tensor("x_split", [128, 4, 8 * CAP], f32r))
        y_split = ctx.enter_context(nc.sbuf_tensor("y_split", [128, YCOLS], f32r))
        arena = ctx.enter_context(nc.sbuf_tensor("arena", [128, SIZE], f32))
        page_ids = ctx.enter_context(nc.sbuf_tensor("page_ids", [1, NB * NPG], i32))
        items_i = ctx.enter_context(nc.sbuf_tensor("items_i", [1, 1], i32))
        top_i = ctx.enter_context(nc.sbuf_tensor("top_i", [128, 3, 8], u32))
        conv_w = ctx.enter_context(nc.sbuf_tensor("conv_w", [128, 2, CK + 1], f32))
        psum = ctx.enter_context(nc.psum_tensor("psum", [128, 8, 512], f32))

        def split(a, dims):
            if len(dims) == 1:
                return a
            names = "abcd"[:len(dims)]
            return a.rearrange(f"p ({' '.join(names)}) -> p {' '.join(names)}",
                               **{x: d for x, d in zip(names, dims)})

        class Cut:

            def __init__(self, at, end, of=None):
                self.at, self.end, self.of = at, end, arena if of is None else of

            def take(self, *dims):
                a = self.of[:, self.at:self.at + math.prod(dims)]
                self.at += math.prod(dims)
                assert self.at <= self.end, (dims, self.at, self.end)
                return split(a, dims)

        U0 = 4 * SLOT
        C0 = U0 + NTILE * NT
        R0 = C0 + NCONST
        M0 = R0 + 3 * 768
        X0 = M0 + KT * NT
        ec0 = Cut(0, 8 * SLOT, early_part)
        slots01, slots23 = Cut(0, U0).take(2, NPG, 2, 128), ec0.take(2, NPG, 2, 128)
        cmp_slot = ec0.take(2, NPG, 2, 128)
        sel_slot = [slots01[:, 0], slots01[:, 1], slots23[:, 0], slots23[:, 1], cmp_slot[:, 0], cmp_slot[:, 1],
                    slots01[:, 0], slots01[:, 1]]
        w_out = Cut(0, U0).take(KT, D)
        w_plg = Cut(0, 4 * SLOT, early_part).take(KT, D)
        w_ple = Cut(4 * SLOT, 5 * SLOT, early_part).take(2, D)
        late_sb = early_part[:, 5 * SLOT:5 * SLOT + NLATE]
        assert NLATE <= 2 * SLOT
        retc = Cut(7 * SLOT, 8 * SLOT, early_part)
        s_in, q_wide = retc.take(2, NB, 64), retc.take(2, NB, 64)
        uT = Cut(U0, C0).take(NTILE, NT)
        early_sb = arena[:, C0:C0 + NCONST]

        def const(name, *dims):
            o, n = LAY[name]
            return split((late_sb if name in LATE else early_sb)[:, o:o + n], dims or (n,))

        ident, ones = const("ident"), const("ones")
        rc = Cut(R0, M0)
        er = Cut(0, YCOLS, early_rows)
        kvR, gateR = er.take(3, 6, 128), er.take(3, 24)
        rvR, rgR, rkR = rc.take(3, 256), rc.take(3, 256), rc.take(3, 256)
        xT = Cut(M0, X0).take(KT, NT)
        mixT = Cut(M0, X0).take(KT, NT)
        hT = mixT
        xc = Cut(X0, SIZE)
        w_in = Cut(X0 + 3 * 1024, SIZE).take(4, KT, 128)
        win = xc.take(4, 2, 512)
        PT = xc.take(22, 128)
        assert xc.at <= X0 + 3072 + 4096
        xc.at = X0 + 3072 + 4096
        convP, convS, convY = xc.take(2, CK - 1 + NPR), xc.take(2, NB, CK - 1 + TS), xc.take(2, NT)
        vecs = xc.take(3, CC)
        cm, vcr = xc.take(NB, 2, 32), xc.take(2, 128)
        pc2 = Cut(X0, X0 + 3072 + 4096)
        Sp, PTp = pc2.take(4, 2, 256), pc2.take(4, 4, 128)
        pcT, vcp = pc2.take(16, 128), pc2.take(128)
        pcs = pc2.take(16, 4)
        v_wide = Cut(X0, X0 + 2048).take(RH, NB, 64)
        sm = xc
        cmp_p = sm.take(2, 4)
        pcm, pgc, score, score2, score3 = sm.take(32), sm.take(32), sm.take(40), sm.take(40), sm.take(40)
        selb, st = sm.take(32), sm.take(32)
        gsig, gs, gtmp = sm.take(3, 24), sm.take(4, 3), split(PT[:, 0, 0:96], (4, 24))
        mx, nmx, sums, fac = sm.take(4), sm.take(4), sm.take(4), sm.take(4)
        t8a, t8b = sm.take(8), sm.take(8)
        mxp, nmxp, sump, facp = sm.take(4, 2), sm.take(4, 2), sm.take(4, 2), sm.take(4, 2)
        mc8, sc8 = sm.take(16), sm.take(16)
        stats, mv, rstd = er.take(4, 6), er.take(4, 2), er.take(4)
        su = Cut(U0 + 11 * NT, C0)
        S, Qbd, Vnew = su.take(2688), su.take(NB, 64), su.take(128)
        ru = Cut(U0 + 11 * NT, C0)
        attT, q_dec, kd = ru.take(RH, 128), ru.take(2, 128), ru.take(256)
        S1, S2 = ru.take(2, 64), ru.take(2, 64)
        retR, convR, sig = ru.take(3, 256), ru.take(3, 256), ru.take(3, 256)
        conv_t = Cut(C0 - NPR, C0).take(NPR)
        assert ru.at <= C0 - NPR and su.at <= C0 - NPR
        acc = Cut(U0, C0).take(3, D)
        h = Cut(U0 + 3 * D, C0).take(3, D)
        ln = Cut(R0, M0).take(2, D)
        ec = Cut(X0, SIZE)
        wr, br, pT = ec.take(KT, NE), ec.take(NE), ec.take(2, NT)
        bup = ec.take(NE, 16)
        NI = ROUNDS * NE
        rank_all, gate_all = ec.take(3, NI + 8), ec.take(3, NI + 8)
        Mk, G = ec.take(3, NE), ec.take(3, NE)
        lg, etmp, top8, idxf, g4 = ec.take(NE), ec.take(NE), ec.take(8), ec.take(8), ec.take(8)
        r1 = ec.take(8)
        stats2, mv2, rstd2 = ec.take(2, 6), ec.take(2), ec.take(1)
        slot_no, slot_fold, turner, turn_fold, few = ec.take(CAP), ec.take(CAP), ec.take(128), ec.take(128), ec.take(NI + 8)
        P, PG, PGT = ec.take(3, CAP), ec.take(3, CAP), ec.take(384)
        hu, gate_col = ec.take(2 * FF), ec.take(1)
        ln2 = split(hu, (2, D))
        gg, uu = ec.take(8, CAP), ec.take(8, CAP)
        act_sb = Cut(U0 + 6 * D, C0).take(8, CAP)
        chunk_in = [arena[:, k * SLOT:(k + 1) * SLOT] for k in range(4)] + [arena[:, R0:R0 + SLOT], arena[:, M0:M0 + SLOT]]
        assert SLOT <= KT * NT and SLOT == 2 * D
        many_i = page_ids
        bdn = hu[:, 0:D]
        sg = hu[:, D:2 * D]
        GTs = PGT[:, 0:NT]
        assert ec.at <= SIZE
        y_hi, y_lo = y_split[:, 0:D], y_split[:, D:2 * D]
        PT01 = y_split[:, 2 * D:].rearrange("p (m n) -> p m n", m=3)
        x_hi, x_lo, act_hi, act_lo = (x_split[:, k].rearrange("p (k n) -> p k n", k=8) for k in range(4))

        bank_full, bank_free = many("bank_full", 8), many("bank_free", 8)
        const_in, late_in, x_in, ids_in = sem("const_in"), sem("late_in"), sem("x_in"), sem("ids_in")
        w_in_here, cmp_here, sel_here = many("w_in_here", 4), many("cmp_here", 2), many("sel_here", NB)
        batch_means = sem("batch_means")
        conv_in, vec_in, wout_in, plg_in, ple_in = sem("conv_in"), sem("vec_in"), sem("wout_in"), sem("plg_in"), sem("ple_in")
        sin_in, xrow_in, ln1_in, ln2_in, moe_in = sem("sin_in"), sem("xrow_in"), sem("ln1_in"), sem("ln2_in"), sem("moe_in")
        vnew_in = sem("vnew_in")
        conv_e, conv_ready = sem("conv_e"), sem("conv_ready")
        gsig_ready, qbd_ready = sem("gsig_ready"), sem("qbd_ready")
        means_ready, cmp_max, cmp_exp, pcm_ready = sem("means_ready"), sem("cmp_max"), sem("cmp_exp"), sem("pcm_ready")
        pgc_ready = sem("pgc_ready")
        s_max, s_exp, s_fac, s_scaled = sem("s_max"), sem("s_exp"), sem("s_fac"), sem("s_scaled")
        pmean_ready, pc_max, pc_exp, pc_ready = sem("pmean_ready"), sem("pc_max"), sem("pc_exp"), sem("pc_ready")
        p_max, p_exp, p_fac, p_scaled = sem("p_max"), sem("p_exp"), sem("p_fac"), sem("p_scaled")
        kd_ready, qd_ready, rets_ready = sem("kd_ready"), sem("qd_ready"), sem("rets_ready")
        ret_e, ret_done, convn_in, conv_sig, mix_ready = sem("ret_e"), sem("ret_done"), sem("convn_in"), sem("conv_sig"), sem("mix_ready")
        states_ready = sem("states_ready")
        h_ready, top_ready, top_exp, sig_e = sem("h_ready"), sem("top_ready"), sem("top_exp"), sem("sig_e")
        mask_ready, G_ready, items_ready, rank_ready = sem("mask_ready"), sem("G_ready"), sem("items_ready"), sem("rank_ready")
        w_here, hi_ready, lo_ready, lo_ready2, chunk_used = many("w_here", 6), sem("hi_ready"), sem("lo_ready"), sem("lo_ready2"), sem("chunk_used")
        ylo_ready, PT_ready = sem("ylo_ready"), sem("PT_ready")
        xlo_ready, act_hi_ready, act_lo_ready = sem("xlo_ready"), sem("act_hi_ready"), sem("act_lo_ready")
        P_ready, gathered, xg_ready = sem("P_ready"), sem("gathered"), sem("xg_ready")
        up_done, hu_ready, PG_turned, PGT_ready = sem("up_done"), sem("hu_ready"), sem("PG_turned"), sem("PGT_ready")
        hu_turned, g_ready, e_ready, act_ready = sem("hu_turned"), sem("g_ready"), sem("e_ready"), sem("act_ready")
        y_stored, var_ready, std_ready = sem("y_stored"), sem("var_ready"), sem("std_ready")
        y_ready, scattered, added, y_out = sem("y_ready"), sem("scattered"), sem("added"), sem("y_out")
        rows_out, states_out, wincopy_out, conv_out = sem("rows_out"), sem("states_out"), sem("wincopy_out"), sem("conv_out")
        dve_step, act_step, pool_step, dve_loop, dve_tail = sem("dve_step"), sem("act_step"), sem("pool_step"), sem("dve_loop"), sem("dve_tail")

        def bank(job):
            return JOB[job] % 8

        def ps(job):
            return psum[:, bank(job), :]

        def full(eng, job):
            eng.wait_ge(bank_full[bank(job)], JOB[job] // 8 + 1)

        def freed(eng, job):
            eng.wait_ge(bank_free[bank(job)], JOB[job] // 8 + 1)

        def open_bank(pe, job):
            if JOB[job] >= 8:
                pe.wait_ge(bank_free[bank(job)], JOB[job] // 8)

        def steps(eng, s, start=0):
            n = [0]

            def seen(ins):
                n[0] += 1
                ins.then_inc(s, 1)
                eng.wait_ge(s, start + n[0])
            seen.count = n
            return seen

        DVE_COLS = 9 * SLOT // 16
        POOL_CHUNK = 10
        CONV_STEPS = 2 * 2 * (1 + 2 * (CK - 1))
        NSLOPE = [-(2.0 ** -(hh + 1)) for hh in range(HEADS)]
        block = ctx.enter_context(nc.Block())

        def page_loader(eng):
            regs = [eng.alloc_register(f"page{n}") for n in range(4)]

            def page_loads(b, dst, part, here):
                with eng.Fori(0, NPG // 4) as k:
                    eng.load(regs, page_ids[0:1, bass.ds(k * 4 + b * NPG, 4)])
                    pages = [eng.snap(reg, min_val=0, max_val=A["pages"].shape[0] - 1) for reg in regs]
                    for n, page in enumerate(pages):
                        eng.dma_start(dst[:, bass.ds(k * 1024 + n * 256, 256)],
                                      A["pages"][bass.ds(page, 1), :, part * 256:part * 256 + 256].rearrange("a p n -> (a p) n"))\
                            .then_inc(here, 16)
            return page_loads

        def sel_load(page_loads, b):
            page_loads(b, sel_slot[b].rearrange("p a b c -> p (a b c)"), 1, sel_here[b])

        def window_load(eng, b):
            eng.dma_start(win[:, b % 4], A["windows"][b]).then_inc(sel_here[b], 16)

        @block.sync
        def _(sp):
            sp.dma_start(page_ids[:, :], A["page_table"]).then_inc(ids_in, 16)

            page_loads = page_loader(sp)

            def cmp_load(b):
                if b >= 2:
                    sp.wait_ge(batch_means, b - 1)
                page_loads(b, cmp_slot[:, b % 2].rearrange("p a b c -> p (a b c)"), 0, cmp_here[b % 2])

            sp.wait_ge(ids_in, 16)
            sp.wait_ge(x_in, 16)
            sp.wait_ge(w_in_here[0], 16)
            sp.dma_start(early_sb, A["early"]).then_inc(const_in, 16)
            for b in range(NB):
                cmp_load(b)
            sp.wait_ge(batch_means, NB)
            sel_load(page_loads, 4)
            sel_load(page_loads, 5)
            full(sp, ("o", 0))
            window_load(sp, 4)
            window_load(sp, 5)
            sel_load(page_loads, 6)
            sel_load(page_loads, 7)
            full(sp, ("o", 1))
            window_load(sp, 6)
            window_load(sp, 7)
            sp.dma_start(w_plg, A["w_plg"]).then_inc(plg_in, 16)
            full(sp, ("o", 2))
            sp.dma_start(late_sb, A["late"]).then_inc(late_in, 16)
            sp.dma_start(s_in, A["state_ret"]).then_inc(sin_in, 16)
            sp.dma_start(w_ple, A["w_ple"]).then_inc(ple_in, 16)
            full(sp, ("o", 3))
            sp.dma_start(w_out, A["w_out"]).then_inc(wout_in, 16)
            freed(sp, ("rS_s", 1))
            sp.dma_start(acc[:, 0:2], A["x_rows"][0:256].rearrange("(m p) d -> p m d", p=128)).then_inc(xrow_in, 16)
            sp.dma_start(acc[0:64, 2], A["x_rows"][256:320]).then_inc(xrow_in, 16)
            sp.wait_ge(rows_out, 16 * 13)
            sp.wait_ge(conv_out, 48)
            full(sp, ("mx", 2))
            sp.dma_start(ln, A["ln"][:, 0:2]).then_inc(ln1_in, 16)
            sp.dma_start(wr, A["w_router"]).then_inc(moe_in, 16)
            sp.dma_start(br, A["b_router"]).then_inc(moe_in, 16)
            sp.dma_start(pT, A["pT"]).then_inc(moe_in, 16)
            sp.dma_start(bup, A["b_up"]).then_inc(moe_in, 16)
            sp.dma_start(bdn[0:NE, :], A["b_down"]).then_inc(moe_in, 16)

            up = A["w_up"].rearrange("e (k p) n -> e k p n", p=128)
            down = A["w_down"].rearrange("e (k a p) n -> e k p a n", p=128, a=2)

            def weights(e, c):
                if c < 8:
                    dst, src = chunk_in[c % 6], up[e, c] if isinstance(e, int) else up[bass.ds(e, 1), c].rearrange("e p n -> (e p) n")
                else:
                    dst = chunk_in[c % 6].rearrange("p (a n) -> p a n", a=2)
                    src = down[e, c - 8] if isinstance(e, int) else down[bass.ds(e, 1), c - 8].rearrange("e p a n -> (e p) a n")
                sp.dma_start(dst, src).then_inc(w_here[c % 6], 16)

            full(sp, ("wo", 2, 1))
            for c in range(4):
                weights(0, c)
            sp.wait_ge(h_ready, 3)
            weights(0, 4)
            full(sp, ("ple", 2, 1))
            weights(0, 5)

            def item_loads(i, e, e_next):
                for c in range(6, 18):
                    if c - 6 != POOL_CHUNK:
                        sp.wait_ge(lo_ready, i * 12 + (c - 5))
                    sp.wait_ge(lo_ready2, i * 12 + (c - 5))
                    weights(e if c < 12 else e_next, c % 12)

            sp.wait_ge(items_ready, 1)
            n_items = sp.value_load(items_i[0:1, 0:1], min_val=NE, max_val=NI)
            with sp.Fori(0, ROUNDS) as r:
                with sp.If(n_items > r * NE):
                    with sp.Fori(0, NE - 1) as e:
                        item_loads(r * NE + e, e, e + 1)
                    item_loads(r * NE + (NE - 1), NE - 1, 0)
            sp.wait_ge(hu_turned, n_items * 2)
            sp.dma_start(ln2, A["ln"][:, 2:4]).then_inc(ln2_in, 16)

        @block.tensor
        def _(pe):
            def mm(out, lhsT, rhs, start, stop):
                return TE.matmul(out, lhsT, rhs, start=start, stop=stop, skip_group_check=True)

            def turn(out, in_):
                return TE.transpose(out, in_, ident[0:in_.shape[0], 0:in_.shape[0]])

            def close(ins, job):
                ins.then_inc(bank_full[bank(job)], 1)

            def tok(m):
                return slice(m * 128, m * 128 + MT[m])

            pe.wait_ge(x_in, 16)
            for j in range(NTILE):
                job = ("proj", j)
                open_bank(pe, job)
                pe.wait_ge(w_in_here[j % 4], 16 * (j // 4 + 1))
                for k in range(KT):
                    last = mm(ps(job)[:, 0:NT], w_in[:, j % 4, k], xT[:, k], k == 0, k == KT - 1)
                close(last, job)
            pe.wait_ge(const_in, 16)
            for j in range(NTILE):
                freed(pe, ("proj", j))
            for m in range(3):
                for what, tiles in (("rowsA", (TCK, TCV, TSK, TSV)), ("rowsB", (TWK, TWV, TGATE)),
                                    ("rowsC", (TRV, TRV + 1, TRG, TRG + 1)), ("rowsD", (TRK, TRK + 1))):
                    job = (what, m)
                    open_bank(pe, job)
                    for n, t in enumerate(tiles):
                        K = 24 if t == TGATE else 128
                        last = turn(ps(job)[0:MT[m], n * 128:n * 128 + K], uT[0:K, t, tok(m)])
                    close(last, job)
            open_bank(pe, ("gates",))
            pe.wait_ge(gsig_ready, 3)
            for p in range(4):
                last = mm(ps(("gates",))[:, 24 * p:24 * p + 24], const("pick", 4, 128)[0:64, p], gsig[0:64, 2], True, True)
            close(last, ("gates",))

            pe.wait_ge(qbd_ready, 1)
            pe.wait_ge(batch_means, NB)
            half = [slice(b2 * 64, b2 * 64 + 64) for b2 in range(2)]

            def sample_cmp(p):
                job = ("sc", p)
                open_bank(pe, job)
                for b2 in range(2):
                    last = mm(ps(job)[half[b2], 0:32], Qbd[:, 2 * p + b2], cm[:, 2 * p + b2, 0], True, True)
                close(last, job)

            def sample_values(p):
                job = ("vc", p)
                open_bank(pe, job)
                for b2 in range(2):
                    last = turn(ps(job)[0:32, b2 * 128:b2 * 128 + 128], cm[:, 2 * p + b2, 1])
                close(last, job)

            def sample_importance(p):
                job = ("imp", p)
                open_bank(pe, job)
                pe.wait_ge(pcm_ready, p + 1)
                close(mm(ps(job)[:, 0:32], const("headsum"), pcm, True, True), job)

            def sample_scores(p):
                for c in range(6):
                    job = ("sw", p, c)
                    open_bank(pe, job)
                    for b2 in range(2):
                        b = 2 * p + b2
                        pe.wait_ge(sel_here[b], 16 * (NPG + 1))
                        if c == 0:
                            last = mm(ps(job)[half[b2], :], Qbd[:, b], win[:, b % 4, 0], True, True)
                        elif c == 1:
                            mm(ps(job)[half[b2], 0:64], Qbd[:, b], uT[:, TWK, NPR:NT], True, True)
                            last = mm(ps(job)[half[b2], 64:128], Qbd[:, b], uT[:, TSK, NPR:NT], True, True)
                        else:
                            q = 4 * (c - 2)
                            last = mm(ps(job)[half[b2], :], Qbd[:, b], sel_slot[b][:, q:q + 4, 0], True, True)
                    close(last, job)

            def sample_output(p, b2):
                job, cols, b = ("o", p), half[b2], 2 * p + b2
                out = ps(job)[:, cols]
                mm(out, vcr[0:32, b2], PT[0:32, 21, cols], True, False)
                for t in range(21):
                    v = (win[:, b % 4, 1, t * 128:t * 128 + 128] if t < 4 else
                         Vnew if t == 4 else sel_slot[b][:, t - 5, 1])
                    last = mm(out, v, PT[:, t, cols], False, t == 20)
                return last

            sample_scores(0)
            sample_cmp(0)
            sample_importance(0)
            sample_values(0)
            for p in range(4):
                for q in range(6):
                    job = ("pt", p, q)
                    open_bank(pe, job)
                    pe.wait_ge(s_scaled, 2 * p + (1 if q == 0 else 2))
                    if q < 5:
                        for k in range(4):
                            last = turn(ps(job)[:, k * 128:k * 128 + 128], S[:, (4 * q + k) * 128:(4 * q + k) * 128 + 128])
                    else:
                        turn(ps(job)[:, 0:128], S[:, 2560:2688])
                        pe.wait_ge(pgc_ready, p + 1)
                        last = turn(ps(job)[0:32, 128:256], pgc)
                    close(last, job)
                if p < 3:
                    sample_scores(p + 1)
                    sample_cmp(p + 1)
                open_bank(pe, ("o", p))
                freed(pe, ("vc", p))
                pe.wait_ge(vnew_in, 32)
                for q in range(6):
                    freed(pe, ("pt", p, q))
                sample_output(p, 0)
                if p < 3:
                    sample_importance(p + 1)
                close(sample_output(p, 1), ("o", p))
                if p < 3:
                    sample_values(p + 1)

            job = ("pcv",)
            open_bank(pe, job)
            pe.wait_ge(pmean_ready, 1)
            close(turn(ps(job)[0:4, 0:128], cmp_p[:, 1]), job)

            def prompt_scores(qi, hh):
                i, g = hh % 4, hh // 4
                gp = slice(g * 64, g * 64 + 64)
                Kq = 128 * (qi + 1)
                job = ("ps", qi, hh)
                open_bank(pe, job)
                q = uT[gp, TQ + i, qi * 128:qi * 128 + 128]
                mm(ps(job)[:, 0:Kq], q, uT[gp, TSK, 0:Kq], True, True)
                close(mm(ps(job)[:, 256:256 + Kq], q, uT[gp, TWK, 0:Kq], True, True), job)

            for qi in range(2):
                for g in range(2):
                    job = ("pc", qi, g)
                    open_bank(pe, job)
                    gp = slice(g * 64, g * 64 + 64)
                    for i in range(4):
                        last = mm(ps(job)[:, 4 * i:4 * i + 4], uT[gp, TQ + i, qi * 128:qi * 128 + 128], cmp_p[gp, 0], True, True)
                    close(last, job)
            prompt_scores(0, 0)
            prompt_scores(0, 4)
            pe.wait_ge(pc_ready, 1)
            for qi in range(2):
                for g in range(2):
                    job = ("pct", qi, g)
                    open_bank(pe, job)
                    for k in range(4):
                        last = turn(ps(job)[0:4, k * 128:k * 128 + 128], pcs[:, 8 * qi + 4 * g + k])
                    close(last, job)

            def prompt_turn(n):
                qi, i = n // 4, n % 4
                for g in range(2):
                    m = 2 * n + g
                    job = ("ppt", qi, i + 4 * g)
                    open_bank(pe, job)
                    pe.wait_ge(p_scaled, m + 1)
                    for b2 in range(2):
                        for k in range(qi + 1):
                            c = (b2 * (qi + 1) + k) * 128
                            last = turn(ps(job)[:, c:c + 128], Sp[:, m % 4, b2, k * 128:k * 128 + 128])
                    close(last, job)

            def prompt_output(n):
                qi, i = n // 4, n % 4
                job = ("po", qi, i)
                open_bank(pe, job)
                for g in range(2):
                    m = 2 * n + g
                    gp = slice(g * 64, g * 64 + 64)
                    freed(pe, ("ppt", qi, i + 4 * g))
                    out = ps(job)[gp, 0:128]
                    mm(out, vcp[0:4, gp], pcT[0:4, 8 * qi + i + 4 * g], True, False)
                    for b2 in range(2):
                        for k in range(qi + 1):
                            last = mm(out, kvR[:, k, 3 + 2 * b2, gp], PTp[:, m % 4, b2 * (qi + 1) + k], False,
                                      b2 == 1 and k == qi)
                close(last, job)

            freed(pe, ("pcv",))
            for qi in range(2):
                for g in range(2):
                    freed(pe, ("pct", qi, g))
            for n in range(9):
                if n < 7:
                    prompt_scores((n + 1) // 4, (n + 1) % 4)
                    prompt_scores((n + 1) // 4, (n + 1) % 4 + 4)
                if n >= 1:
                    prompt_output(n - 1)
                if n < 8:
                    prompt_turn(n)

            def head(hh):
                return slice((hh % 2) * 64, (hh % 2) * 64 + 64)

            for c in range(3):
                M = MT[c]
                for z in range(2):
                    job = ("att", c, z)
                    open_bank(pe, job)
                    for hh in (z, z + 2):
                        last = mm(ps(job)[0:M, hh * 128:hh * 128 + M], uT[head(hh), TRK + hh // 2, tok(c)],
                                  uT[head(hh), TRQ + hh // 2, tok(c)], True, True)
                    close(last, job)
                if c == 1:
                    freed(pe, ("rS", 0))
                    pe.wait_ge(qd_ready, 1)
                if c == 2:
                    pe.wait_ge(rets_ready, 1)
                    pe.wait_ge(sin_in, 16)
                for z in range(2):
                    job = ("ro", c, z)
                    open_bank(pe, job)
                    freed(pe, ("att", c, z))
                    for hh in (z, z + 2):
                        out = ps(job)[0:M, hh * 64:hh * 64 + 64]
                        last = mm(out, attT[0:M, hh, 0:M], rvR[0:M, c, hh * 64:hh * 64 + 64], True, c != 1)
                        if c == 1:
                            last = mm(out, q_dec[head(hh), hh // 2], S1[head(hh), hh // 2], False, True)
                    close(last, job)
                if c < 2:
                    job = ("rS", c)
                    open_bank(pe, job)
                    pe.wait_ge(kd_ready, c + 1)
                    for hh in range(RH):
                        last = mm(ps(job)[head(hh), (hh // 2) * 64:(hh // 2) * 64 + 64], kd[:, hh * 64:hh * 64 + 64],
                                  rvR[:, c, hh * 64:hh * 64 + 64], True, True)
                    close(last, job)
                if c == 0:
                    pe.wait_ge(pool_step, CONV_STEPS)
                job = ("cv", c)
                open_bank(pe, job)
                for k in range(2):
                    last = turn(ps(job)[0:MT[c], k * 128:k * 128 + 128], convY[:, k, tok(c)])
                close(last, job)
            for z in range(2):
                job = ("ri", z)
                open_bank(pe, job)
                for hh in (z, z + 2):
                    for b in range(NB):
                        last = mm(ps(job)[0:64, hh * 64:hh * 64 + 64], q_wide[head(hh), hh // 2, b],
                                  s_in[head(hh), hh // 2, b], b == 0, b == NB - 1)
                close(last, job)
            for hp in range(2):
                job = ("rS_s", hp)
                open_bank(pe, job)
                for hh in (2 * hp, 2 * hp + 1):
                    last = mm(ps(job)[head(hh), :], kd[0:64, hh * 64:hh * 64 + 64], v_wide[0:64, hh], True, True)
                close(last, job)
            for m in range(3):
                job = ("mx", m)
                open_bank(pe, job)
                pe.wait_ge(mix_ready, m + 1)
                for k in range(4):
                    src = (convR if k < 2 else retR)[0:MT[m], m, (k % 2) * 128:(k % 2) * 128 + 128]
                    last = turn(ps(job)[:, k * 128:k * 128 + MT[m]], src)
                close(last, job)
            pe.wait_ge(wout_in, 16)
            for p in range(4):
                freed(pe, ("o", p))
            for qi in range(2):
                for i in range(4):
                    freed(pe, ("po", qi, i))
            for m in range(3):
                freed(pe, ("mx", m))
                for c in range(2):
                    job = ("wo", m, c)
                    open_bank(pe, job)
                    for k in range(KT):
                        last = mm(ps(job)[0:MT[m], :], mixT[:, k, tok(m)], w_out[:, k, c * 512:c * 512 + 512], k == 0, k == KT - 1)
                    close(last, job)
            for m in range(3):
                for c in range(2):
                    job = ("hT", m, c)
                    open_bank(pe, job)
                    pe.wait_ge(h_ready, m + 1)
                    for k in range(4):
                        d = (4 * c + k) * 128
                        last = turn(ps(job)[:, k * 128:k * 128 + MT[m]], h[0:MT[m], m, d:d + 128])
                    close(last, job)
            pe.wait_ge(moe_in, 16 * 5)
            for m in range(3):
                job = ("router", m)
                open_bank(pe, job)
                freed(pe, ("hT", m, 0))
                freed(pe, ("hT", m, 1))
                for k in range(KT):
                    last = mm(ps(job)[0:MT[m], 0:NE], hT[:, k, tok(m)], wr[:, k], k == 0, k == KT - 1)
                close(last, job)
            pe.wait_ge(plg_in, 16)
            pe.wait_ge(ple_in, 16)
            for m in range(3):
                for c in range(2):
                    for what, w, x, K in (("plg", w_plg, hT, KT), ("ple", w_ple, pT, 2)):
                        job = (what, m, c)
                        open_bank(pe, job)
                        for k in range(K):
                            last = mm(ps(job)[0:MT[m], :], x[:, k, tok(m)], w[:, k, c * 512:c * 512 + 512], k == 0, k == K - 1)
                        close(last, job)
            pe.wait_ge(mask_ready, 3)
            for m in range(3):
                job = ("rank", m)
                open_bank(pe, job)
                for j in range(m + 1):
                    w = const("lower") if j == m else ones
                    last = mm(ps(job)[0:MT[m], 0:NE], w[0:MT[j], 0:MT[m]], Mk[0:MT[j], j], j == 0, j == m)
                close(last, job)
            job = ("count",)
            open_bank(pe, job)
            for j in range(3):
                last = mm(ps(job)[:, 0:NE], ones[0:MT[j], :], Mk[0:MT[j], j], j == 0, j == 2)
            close(last, job)
            job = ("GT",)
            open_bank(pe, job)
            for m in range(3):
                last = turn(ps(job)[0:NE, tok(m)], G[0:MT[m], m])
            close(last, job)
            freed(pe, ("GT",))
            for m in range(3):
                for c in range(2):
                    job = ("bd", m, c)
                    open_bank(pe, job)
                    close(mm(ps(job)[0:MT[m], :], GTs[0:NE, tok(m)], bdn[0:NE, c * 512:c * 512 + 512], True, True), job)

            for job in list(JOB)[-8:]:
                freed(pe, job)

            def gather(i1):
                pe.wait_ge(P_ready, i1)
                for k in range(KT):
                    for m in range(3):
                        last = mm(psum[:, 6 + k // 4, (k % 4) * CAP:(k % 4 + 1) * CAP], h[0:MT[m], m, k * 128:k * 128 + 128],
                                  P[0:MT[m], m], m == 0, m == 2)
                last.then_inc(gathered, 1)

            def scatter(i, m):
                if m == 0:
                    pe.wait_ge(y_ready, i + 1)
                    pe.wait_ge(ylo_ready, i + 1)
                    pe.wait_ge(PT_ready, i + 1)
                if m == 2:
                    pe.wait_ge(added, i * 3 + 1)
                for c in range(2):
                    out = psum[:, (6, 4, 6)[m] + c, :]
                    mm(out, PT01[:, m], y_hi[:, c * 512:c * 512 + 512], True, False)
                    last = mm(out, PT01[:, m], y_lo[:, c * 512:c * 512 + 512], False, True)
                last.then_inc(scattered, 1)

            def turn_hidden(i, half_):
                pe.wait_ge(hu_ready, i * 4 + (2 * half_ + 2))
                for s in range(2):
                    for j in range(4 * half_, 4 * half_ + 4):
                        cols = hu[:, 2 * j * 128 + s:2 * (j + 1) * 128:2]
                        last = mm(psum[:, 2 * half_ + s, (j % 4) * CAP:(j % 4 + 1) * CAP], cols, turner, True, True)
                last.then_inc(hu_turned, 1)

            def up_product(i, passes):
                pe.wait_ge(xg_ready, i + 1)
                pe.wait_ge(xlo_ready, i + 1)
                for k in range(KT):
                    pe.wait_ge(hi_ready, i * 12 + (k + 1))
                    for n_pass, (x, w) in enumerate(passes):
                        for n in range(4):
                            if w is w_lo and n == 0:
                                pe.wait_ge(lo_ready, i * 12 + (k + 1))
                            if w is w_lo and n == DVE_COLS // 512:
                                pe.wait_ge(lo_ready2, i * 12 + (k + 1))
                            final = k == KT - 1 and n_pass == len(passes) - 1
                            last = mm(psum[0:CAP, n, :], x[:, k], w[:, k % 3, n * 512:n * 512 + 512], k == 0 and n_pass == 0, final)
                            if final and n < 3:
                                last.then_inc(up_done, 1)
                    last.then_inc(chunk_used, 1)

            def down_product(i, passes):
                pe.wait_ge(PGT_ready, i + 1)
                pe.wait_ge(PT_ready, i + 2)
                for q in range(4):
                    ch = 8 + q
                    if q % 2 == 0:
                        pe.wait_ge(act_hi_ready, i * 2 + (q // 2 + 1))
                        pe.wait_ge(act_lo_ready, i * 2 + (q // 2 + 1))
                    pe.wait_ge(hi_ready, i * 12 + (ch + 1))
                    for n_pass, (x, w) in enumerate(passes):
                        for a, c in ((0, 0), (0, 1), (1, 0), (1, 1)):
                            at = a * D + c * 512
                            if w is w_lo and at == 0 and ch != POOL_CHUNK:
                                pe.wait_ge(lo_ready, i * 12 + (ch + 1))
                            if w is w_lo and at == (0 if ch == POOL_CHUNK else DVE_COLS // 512 * 512):
                                pe.wait_ge(lo_ready2, i * 12 + (ch + 1))
                            last = mm(psum[0:CAP, 4 + c, :], x[:, 2 * q + a], w[:, ch % 3, at:at + 512],
                                      q == 0 and n_pass == 0 and a == 0, q == 3 and n_pass == len(passes) - 1 and a == 1)
                    last.then_inc(chunk_used, 1)

            gather(1)
            pe.wait_ge(items_ready, 1)
            n_items = pe.value_load(items_i[0:1, 0:1], min_val=NE, max_val=NI)
            with pe.Fori(0, ROUNDS) as r:
                with pe.If(n_items > r * NE):
                    with pe.Fori(0, NE) as e:
                        i = r * NE + e
                        many_slots = pe.value_load(many_i[0:1, bass.ds(i, 1)], min_val=0, max_val=1)
                        with pe.If(many_slots > 0):
                            up_product(i, ((x_hi, w_hi), (x_lo, w_hi), (x_hi, w_lo)))
                        with pe.If(many_slots < 1):
                            up_product(i, ((x_hi, w_hi), (x_hi, w_lo)))
                        scatter(i, 0)
                        scatter(i, 1)
                        pe.wait_ge(P_ready, i + 2)
                        turn_hidden(i, 0)
                        scatter(i, 2)
                        pe.wait_ge(added, i * 3 + 2)
                        for m in range(3):
                            last = turn(psum[:, 4, tok(m)], PG[0:MT[m], m])
                        last.then_inc(PG_turned, 1)
                        turn_hidden(i, 1)
                        pe.wait_ge(added, i * 3 + 3)
                        gather(i + 2)
                        with pe.If(many_slots > 0):
                            down_product(i, ((act_hi, w_hi), (act_lo, w_hi), (act_hi, w_lo)))
                        with pe.If(many_slots < 1):
                            down_product(i, ((act_hi, w_hi), (act_hi, w_lo)))
            for m in range(3):
                scatter(n_items, m)

        @block.scalar
        def _(act):
            seen = steps(act, act_step)

            def root(n, v):
                act.wait_ge(var_ready, n + 1)
                SE.activation(v, v, ACT.Sqrt).then_inc(std_ready, 1)

            def take(job, *pairs):
                full(act, job)
                for dst, src in pairs:
                    last = SE.activation(dst, src, ACT.Copy)
                last.then_inc(bank_free[bank(job)], 1)

            def tile_load(j):
                act.dma_start(w_in[:, j % 4], A["w_in"][j]).then_inc(w_in_here[j % 4], 16)

            act.dma_start(xT, A["xT"]).then_inc(x_in, 16)
            for j in range(4):
                tile_load(j)
            act.dma_start(convS[:, 0, :, 0:CK - 1], A["state_conv"][:, 0]).then_inc(conv_in, 16)
            act.dma_start(convS[:, 1, :, 0:CK - 1], A["state_conv"][:, 1]).then_inc(conv_in, 16)
            act.dma_start(conv_w[:, :, :], A["conv_w"]).then_inc(conv_in, 16)
            act.dma_start(vecs, A["vecs"]).then_inc(vec_in, 16)
            for j in range(NTILE):
                full(act, ("proj", j))
                scale = 0.125 if j in (TQ, TQ + 1, TQ + 2, TQ + 3, TRK, TRK + 1) else 1.0
                SE.activation(uT[:, j], ps(("proj", j))[:, 0:NT], ACT.Copy, scale=scale).then_inc(bank_free[bank(("proj", j))], 1)
                if j + 4 < NTILE:
                    tile_load(j + 4)
            freed(act, ("proj", TG))
            freed(act, ("proj", TG + 1))
            SE.activation(uT[:, TG:TG + 2], uT[:, TG:TG + 2], ACT.Sigmoid).then_inc(conv_e, 1)
            for m in range(3):
                M = MT[m]
                b = ps(("rowsB", m))
                take(("rowsB", m), (kvR[0:M, m, 4:6], b[0:M, 0:256].rearrange("p (a b) -> p a b", a=2)),
                     (gateR[0:M, m], b[0:M, 256:280]))
                freed(act, ("rowsB", m))
                SE.activation(gsig[0:M, m], gateR[0:M, m], ACT.Sigmoid).then_inc(gsig_ready, 1)
                take(("rowsD", m), (rkR[0:M, m], ps(("rowsD", m))[0:M, 0:256]))
            freed(act, ("rowsA", 2))
            full(act, ("rowsD", 2))
            act.wait_ge(conv_ready, 1)
            act.dma_start(Vnew[0:64], kvR[0:64, 2, 5]).then_inc(vnew_in, 16)
            act.dma_start(Vnew[64:128], kvR[0:64, 2, 3]).then_inc(vnew_in, 16)

            def exp_s(p, n):
                a, b = ((0, 576), (576, 2688))[n]
                act.wait_ge(s_max, 2 * p + n + 1)
                SE.activation(S[:, a:b], S[:, a:b], ACT.Exp, bias=nmx[:, n + 1:n + 2],
                              accum_out=sums[:, n + 1:n + 2]).then_inc(s_exp, 1)

            def scale_s(p, n):
                a, b = ((0, 576), (576, 2688))[n]
                act.wait_ge(s_fac, 2 * p + n + 1)
                SE.activation(S[:, a:b], S[:, a:b], ACT.Copy, scale=fac[:, n + 1:n + 2]).then_inc(s_scaled, 1)

            for p in range(4):
                exp_s(p, 0)
                act.wait_ge(cmp_max, p + 1)
                SE.activation(st, st, ACT.Exp, bias=nmx[:, 0:1], accum_out=sums[:, 0:1]).then_inc(cmp_exp, 1)
                scale_s(p, 0)
                exp_s(p, 1)
                scale_s(p, 1)
                if p:
                    full(act, ("o", p - 1))
                take(("vc", p), (vcr[0:32], ps(("vc", p))[0:32, 0:256].rearrange("p (a b) -> p a b", a=2)))
                for q in (0, 2, 4):
                    take(("pt", p, q), (PT[:, 4 * q:4 * q + 4], ps(("pt", p, q)).rearrange("p (a b) -> p a b", a=4)))

            full(act, ("o", 3))
            take(("pcv",), (vcp[0:4], ps(("pcv",))[0:4, 0:128]))
            act.wait_ge(pc_max, 1)
            SE.activation(pcs, pcs, ACT.Exp).then_inc(pc_exp, 1)

            def soften(m):
                Kq = 128 * (m // 8 + 1)
                for b2 in range(2):
                    act.wait_ge(p_max, 2 * m + b2 + 1)
                    SE.activation(Sp[:, m % 4, b2, 0:Kq], Sp[:, m % 4, b2, 0:Kq], ACT.Exp, bias=nmxp[:, m % 4, b2:b2 + 1],
                                  accum_out=sump[:, m % 4, b2:b2 + 1]).then_inc(p_exp, 1)

            def scale_p(m):
                act.wait_ge(p_fac, m + 1)
                Kq = 128 * (m // 8 + 1)
                for b2 in range(2):
                    last = SE.activation(Sp[:, m % 4, b2, 0:Kq], Sp[:, m % 4, b2, 0:Kq], ACT.Copy, scale=facp[:, m % 4, b2:b2 + 1])
                last.then_inc(p_scaled, 1)

            soften(0)
            soften(1)
            for qi in range(2):
                for g in range(2):
                    take(("pct", qi, g), (pcT[0:4, 8 * qi + 4 * g:8 * qi + 4 * g + 4],
                                          ps(("pct", qi, g))[0:4].rearrange("p (a b) -> p a b", a=4)))
            for n in range(8):
                scale_p(2 * n)
                scale_p(2 * n + 1)
                if n < 7:
                    soften(2 * n + 2)
                    soften(2 * n + 3)
            full(act, ("po", 1, 3))
            freed(act, ("rowsC", 2))
            SE.activation(sig[:, 0:2], rgR[:, 0:2], ACT.Sigmoid).then_inc(ret_e, 1)
            SE.activation(sig[0:64, 2], rgR[0:64, 2], ACT.Sigmoid).then_inc(ret_e, 1)
            for m in range(3):
                root(m, rstd[0:MT[m], 0:1])
            for m in range(3):
                root(3 + m, rstd[0:MT[m]])
            for m in range(3):
                act.wait_ge(convn_in, m + 1)
                act.wait_ge(ret_done, m + 1)
                M = MT[m]
                SE.activation(sig[0:M, m], convR[0:M, m], ACT.Sigmoid).then_inc(conv_sig, 1)
            for m in range(3):
                root(6 + m, rstd2[0:MT[m]])
            for m in range(3):
                M = MT[m]
                act.wait_ge(top_ready, m + 1)
                SE.activation(g4[0:M, 0:4], top8[0:M, 0:4], ACT.Exp, bias=r1[0:M, 0:1], accum_out=r1[0:M, 1:2]).then_inc(top_exp, 1)
            for m in range(3):
                M = MT[m]
                for c in range(2):
                    job = ("plg", m, c)
                    full(act, job)
                    if m or c:
                        freed(act, ("ple", m, 0) if c else ("ple", m - 1, 1))
                    SE.activation(sg[0:M, 0:512], ps(job)[0:M], ACT.Sigmoid).then_inc(bank_free[bank(job)], 1)

            def gathered_copy(i1):
                act.wait_ge(gathered, i1)
                SE.activation(x_hi.rearrange("p (a k) n -> p a (k n)", a=2), psum[:, 6:8, :], ACT.Copy).then_inc(xg_ready, 1)

            def high(i, c):
                act.wait_ge(w_here[c % 6], i * 32 + (c // 6 * 16 + 16))
                act.wait_ge(chunk_used, i * 12 + (c + 1))
                SE.activation(w_hi[:, c % 3], chunk_in[c % 6], ACT.Copy).then_inc(hi_ready, 1)

            act.wait_ge(states_out, 32)
            act.wait_ge(rows_out, 16 * 13)
            full(act, ("ple", 2, 1))
            for c in range(3):
                high(0, c)
            gathered_copy(1)
            act.wait_ge(items_ready, 1)
            n_items = act.value_load(items_i[0:1, 0:1], min_val=NE, max_val=NI)
            with act.Fori(0, ROUNDS) as r:
                with act.If(n_items > r * NE):
                    with act.Fori(0, NE) as e:
                        i = r * NE + e
                        for c in range(3, 10):
                            high(i, c)
                        for n in range(4):
                            if n < 3:
                                act.wait_ge(up_done, i * 3 + (n + 1))
                            else:
                                act.wait_ge(chunk_used, i * 12 + (KT + 3))
                            last = SE.activation(hu[0:CAP, n * 512:n * 512 + 512], psum[0:CAP, n, :], ACT.Copy)
                            last.then_inc(hu_ready, 1)
                        high(i, 10)
                        for half_ in range(2):
                            js = slice(4 * half_, 4 * half_ + 4)
                            act.wait_ge(g_ready, i * 2 + (half_ + 1))
                            SE.activation(act_sb[:, js], gg[:, js], ACT.Sigmoid, scale=SALPHA).then_inc(e_ready, 1)
                            if half_ == 0:
                                act.wait_ge(PG_turned, i + 1)
                                SE.activation(PGT[:, 0:NT], psum[:, 4, 0:NT], ACT.Copy, accum_out=gate_col).then_inc(PGT_ready, 1)
                            act.wait_ge(act_ready, i * 2 + (half_ + 1))
                            SE.activation(act_hi[:, js], act_sb[:, js], ACT.Copy).then_inc(act_hi_ready, 1)
                        high(i, 11)
                        gathered_copy(i + 2)
                        for c in range(12, 15):
                            high(i, c)
                        act.wait_ge(PGT_ready, i + 1)
                        SE.activation(y_hi.rearrange("p (c n) -> p c n", c=2), psum[:, 4:6, :], ACT.Copy, scale=gate_col).then_inc(y_ready, 1)

            for c in (3, 4, 5):
                act.wait_ge(w_here[c], n_items * 32 + 16)
            for m in range(3):
                root(9 + m, rstd2[0:MT[m]])

        @block.vector
        def _(dve):
            seen = steps(dve, dve_step)

            def take(job, *pairs):
                full(dve, job)
                for dst, src in pairs:
                    last = VE.tensor_copy(dst, src)
                last.then_inc(bank_free[bank(job)], 1)
                freed(dve, job)

            roots = [0]

            def inverse_root(seen, out, var):
                roots[0] += 1
                VE.tensor_scalar(out, var, EPS, None, ADD).then_inc(var_ready, 1)
                dve.wait_ge(std_ready, roots[0])
                seen(VE.reciprocal(out, out))

            def normed(seen, src, dst, n, width, mvt, stt, rs):
                for k in range(n):
                    w = width // n
                    seen(VE.bn_stats(stt[:, k], src[:, k * w:(k + 1) * w]))
                seen(VE.bn_aggr(mvt, stt[:, 0:n]))
                inverse_root(seen, rs, mvt[:, 1:2])
                seen(VE.tensor_scalar(dst, src, mvt[:, 0:1], rs, SUB, MUL))

            for k in range(2):
                VE.memset(convP[:, k, 0:CK - 1], 0.0)
            seen(VE.memset(score, -1.0))
            def cache_means(b):
                dve.wait_ge(cmp_here[b % 2], 16 * NPG * (b // 2 + 1))
                for kind in range(2):
                    last = VE.tensor_reduce(cm[:, b, kind].rearrange("p (a b) -> p a b", b=2),
                                            cmp_slot[:, b % 2, :, kind].rearrange("p a (b s) -> p a b s", b=2), AX, ADD)
                seen(last)
                VE.tensor_scalar(cm[:, b], cm[:, b], 1.0 / 64, None, MUL).then_inc(batch_means, 1)

            for b in range(6):
                cache_means(b)
            seen(VE.memset(score[:, 0:1], 1e4))
            seen(VE.memset(score[:, 31:33], 1e4))
            dve.wait_ge(conv_e, 1)
            freed(dve, ("proj", TA))
            freed(dve, ("proj", TA + 1))
            dve.wait_ge(conv_in, 48)
            VE.tensor_tensor(convP[:, :, CK - 1:], uT[:, TA:TA + 2, 0:NPR], uT[:, TG:TG + 2, 0:NPR], MUL)
            for k in range(2):
                last = VE.tensor_tensor(convS[:, k, :, CK - 1:], uT[:, TA + k, NPR:NT].rearrange("p (b t) -> p b t", t=TS),
                                        uT[:, TG + k, NPR:NT].rearrange("p (b t) -> p b t", t=TS), MUL)
            last.then_inc(conv_ready, 1)
            for b in range(6, NB):
                cache_means(b)
            for m in range(3):
                M = MT[m]
                a, c = ps(("rowsA", m)), ps(("rowsC", m))
                take(("rowsA", m), (kvR[0:M, m, 0:4], a[0:M].rearrange("p (a b) -> p a b", a=4)))
                take(("rowsC", m), (rvR[0:M, m], c[0:M, 0:256]), (rgR[0:M, m], c[0:M, 256:512]))
            for kind, t in enumerate((TCK, TCV)):
                seen(VE.tensor_reduce(cmp_p[:, kind], uT[:, t, 0:NPR].rearrange("p (n s) -> p n s", s=64), AX, ADD))
            VE.tensor_scalar(cmp_p, cmp_p, 1.0 / 64, None, MUL).then_inc(pmean_ready, 1)
            full(dve, ("rowsD", 2))
            seen(VE.memset(Qbd, 0.0))
            for g in range(2):
                gp = slice(g * 64, g * 64 + 64)
                last = VE.tensor_copy(Qbd[gp, :, g * 32:g * 32 + 32].rearrange("p b (i t) -> p b i t", t=TS),
                                      uT[gp, TQ:TQ + 4, NPR:NT].rearrange("p i (b t) -> p b i t", t=TS))
                if g == 0:
                    seen(last)
            last.then_inc(qbd_ready, 1)
            full(dve, ("gates",))
            VE.tensor_tensor(gtmp, ps(("gates",))[:, 0:96].rearrange("p (a b) -> p a b", a=4),
                             const("headmask").unsqueeze(1).to_broadcast([128, 4, 24]), MUL).then_inc(bank_free[bank(("gates",))], 1)
            freed(dve, ("gates",))
            for p in range(4):
                last = VE.tensor_reduce(gs[:, p], gtmp[:, p].rearrange("p (h c) -> p c h", c=3), AX, ADD)
            seen(last)

            def add_bias(p):
                if p:
                    full(dve, ("pt", p - 1, 5))
                for c in range(6):
                    job = ("sw", p, c)
                    full(dve, job)
                    if c == 0:
                        last = VE.tensor_tensor(S[:, 0:512], ps(job), const("tabwin"), ADD)
                    elif c == 1:
                        last = VE.tensor_tensor(S[:, 512:640], ps(job)[:, 0:128], const("tabnew", 4, 128)[:, p], ADD)
                    else:
                        at = 640 + 512 * (c - 2)
                        last = VE.scalar_tensor_tensor(out=S[:, at:at + 512], in0=ps(job), scalar=const("chunkbase")[:, c - 2:c - 1],
                                                       in1=const("tabsel"), op0=ADD, op1=ADD)
                    last.then_inc(bank_free[bank(job)], 1)
                    if c == 1:
                        freed(dve, job)
                        seen(VE.tensor_reduce(mx[:, 1:2], S[:, 0:576], AX, MAXOP))
                        VE.tensor_scalar(nmx[:, 1:2], mx[:, 1:2], -1.0, None, MUL).then_inc(s_max, 1)
                freed(dve, ("sw", p, 5))

            def compressed(p):
                job = ("sc", p)
                full(dve, job)
                VE.tensor_tensor(st, ps(job)[:, 0:32], const("tabcmp"), ADD).then_inc(bank_free[bank(job)], 1)
                freed(dve, job)
                seen(VE.tensor_reduce(mx[:, 0:1], st, AX, MAXOP))
                VE.tensor_scalar(nmx[:, 0:1], mx[:, 0:1], -1e29, -1.0, MAXOP, MUL).then_inc(cmp_max, 1)
                factor(p, 0)
                dve.wait_ge(cmp_exp, p + 1)
                seen(VE.tensor_scalar(fac[:, 0:1], sums[:, 0:1], TINY, None, MAXOP))
                seen(VE.reciprocal(fac[:, 0:1], fac[:, 0:1]))
                VE.tensor_scalar(pcm, st, fac[:, 0:1], None, MUL).then_inc(pcm_ready, 1)
                dve.wait_ge(pcm_ready, p + 1)
                VE.tensor_scalar(pgc, pcm, gs[:, p, 0:1], None, MUL).then_inc(pgc_ready, 1)

            def select(p):
                job = ("imp", p)
                full(dve, job)
                VE.tensor_copy(score[:, 1:31], ps(job)[:, 1:31]).then_inc(bank_free[bank(job)], 1)
                freed(dve, job)
                seen(VE.max(t8a, score))
                seen(VE.match_replace(score2, t8a, score, -2.0))
                seen(VE.max(t8b, score2))
                seen(VE.match_replace(score3, t8b, score2, -2.0))
                seen(VE.tensor_scalar(selb, score3[:, 0:32], -2.0, -NEG, ALU.is_equal, MUL))
                seen(VE.tensor_scalar(selb, selb, -NEG, None, SUB))
                blocks = S[:, 640:2688].rearrange("p (n s) -> p n s", s=64)
                seen(VE.tensor_tensor(blocks, blocks, selb.unsqueeze(2).to_broadcast([128, 32, 64]), ADD))
                seen(VE.tensor_reduce(mx[:, 2:3], S[:, 576:2688], AX, MAXOP))
                VE.tensor_scalar(nmx[:, 2:3], mx[:, 2:3], -1.0, None, MUL).then_inc(s_max, 1)

            def factor(p, n):
                dve.wait_ge(s_exp, 2 * p + n + 1)
                f = fac[:, n + 1:n + 2]
                seen(VE.tensor_scalar(f, sums[:, n + 1:n + 2], TINY, None, MAXOP))
                seen(VE.reciprocal(f, f))
                VE.tensor_scalar(f, f, gs[:, p, 2 - n:3 - n], None, MUL).then_inc(s_fac, 1)

            add_bias(0)
            compressed(0)
            select(0)
            for p in range(4):
                factor(p, 1)
                if p:
                    full(dve, ("o", p - 1))
                for q in (1, 3):
                    take(("pt", p, q), (PT[:, 4 * q:4 * q + 4], ps(("pt", p, q)).rearrange("p (a b) -> p a b", a=4)))
                b = ps(("pt", p, 5))
                take(("pt", p, 5), (PT[:, 20], b[:, 0:128]), (PT[0:32, 21], b[0:32, 128:256]))
                if p < 3:
                    add_bias(p + 1)
                    compressed(p + 1)
                    select(p + 1)
                src = ps(("o", p))[:, 0:128].rearrange("p (b g i t) -> p b g i t", b=2, g=2, i=4)
                cols = slice(NPR + 16 * p, NPR + 16 * p + 16)
                full(dve, ("o", p))
                for g in range(2):
                    gp = slice(g * 64, g * 64 + 64)
                    last = VE.tensor_copy(mixT[gp, 2:6, cols].rearrange("p i (b t) -> p i b t", b=2),
                                          src[gp, :, g].rearrange("p b i t -> p i b t"))
                last.then_inc(bank_free[bank(("o", p))], 1)

            def prompt_scores(n):
                qi, hh = n // 8, (n % 8) // 2 + 4 * (n % 2)
                Kq = 128 * (qi + 1)
                job = ("ps", qi, hh)
                full(dve, job)
                dist = const("distp")[:, 0:128] if qi == 0 else const("distp")[:, 128:384]
                if n >= 4:
                    m = n - 4
                    full(dve, ("ppt", m // 8, (m % 8) // 2 + 4 * (m % 2)))
                VE.scalar_tensor_tensor(out=Sp[:, n % 4, :, 0:Kq], in0=dist.unsqueeze(1).to_broadcast([128, 2, Kq]),
                                        scalar=NSLOPE[hh], in1=ps(job).rearrange("p (a b) -> p a b", a=2)[:, :, 0:Kq],
                                        op0=MUL, op1=ADD).then_inc(bank_free[bank(job)], 1)
                freed(dve, job)
                seen(VE.tensor_reduce(mxp[:, n % 4], Sp[:, n % 4, :, 0:Kq], AX, MAXOP))
                VE.tensor_scalar(nmxp[:, n % 4], mxp[:, n % 4], -1.0, None, MUL).then_inc(p_max, 2)

            def prompt_factor(n):
                qi, hh = n // 8, (n % 8) // 2 + 4 * (n % 2)
                dve.wait_ge(p_exp, 2 * n + 2)
                f = facp[:, n % 4]
                seen(VE.tensor_scalar(f, sump[:, n % 4], TINY, None, MAXOP))
                seen(VE.reciprocal(f, f))
                VE.tensor_tensor(f, f, gsig[:, qi, 3 * hh + 1:3 * hh + 3], MUL).then_inc(p_fac, 1)

            dve.wait_ge(late_in, 16)
            for qi in range(2):
                for g in range(2):
                    job = ("pc", qi, g)
                    full(dve, job)
                    for i in range(4):
                        last = VE.scalar_tensor_tensor(out=pcs[:, 8 * qi + 4 * g + i], in0=const("distcmp", 2, 4)[:, qi], scalar=NSLOPE[4 * g + i],
                                                       in1=ps(job)[:, 4 * i:4 * i + 4], op0=MUL, op1=ADD)
                    last.then_inc(bank_free[bank(job)], 1)
            freed(dve, ("pc", 1, 1))
            seen(VE.tensor_reduce(mc8, pcs, AX, MAXOP))
            seen(VE.tensor_scalar(mc8, mc8, -1e29, None, MAXOP))
            VE.tensor_tensor(pcs, pcs, mc8.unsqueeze(2).to_broadcast([128, 16, 4]), SUB).then_inc(pc_max, 1)
            prompt_scores(0)
            prompt_scores(1)
            dve.wait_ge(pc_exp, 1)
            seen(VE.tensor_reduce(sc8, pcs, AX, ADD))
            seen(VE.tensor_scalar(sc8, sc8, TINY, None, MAXOP))
            seen(VE.reciprocal(sc8, sc8))
            seen(VE.tensor_tensor(sc8.rearrange("p (q h) -> p q h", q=2), sc8.rearrange("p (q h) -> p q h", q=2),
                                  gsig[:, 0:2].rearrange("p q (h c) -> p q h c", c=3)[:, :, :, 0], MUL))
            VE.tensor_tensor(pcs, pcs, sc8.unsqueeze(2).to_broadcast([128, 16, 4]), MUL).then_inc(pc_ready, 1)
            for n in range(9):
                if n < 8:
                    prompt_factor(2 * n)
                    prompt_factor(2 * n + 1)
                if n < 7:
                    prompt_scores(2 * n + 2)
                    prompt_scores(2 * n + 3)
                if n >= 1:
                    qi, i = (n - 1) // 4, (n - 1) % 4
                    take(("po", qi, i), (mixT[:, 2 + i, qi * 128:qi * 128 + 128], ps(("po", qi, i))[:, 0:128]))
                if n < 8:
                    qi, i = n // 4, n % 4
                    w = 256 * (qi + 1)
                    for g in range(2):
                        if n >= 2:
                            full(dve, ("po", (n - 2) // 4, (n - 2) % 4))
                        job = ("ppt", qi, i + 4 * g)
                        take(job, (PTp[:, (2 * n + g) % 4].rearrange("p a b -> p (a b)")[:, 0:w], ps(job)[:, 0:w]))

            for m in range(3):
                freed(dve, ("rowsD", m))

            def heads(a):
                return a.rearrange("p (h e) -> p h e", h=RH)

            def weigh(c, decay):
                M = MT[c]
                for z in range(2):
                    job = ("att", c, z)
                    full(dve, job)
                    VE.tensor_tensor(attT[0:M, z::2, 0:M], ps(job)[0:M].rearrange("p (h e) -> p h e", h=RH)[:, z::2, 0:M],
                                     decay[0:M, z::2], MUL).then_inc(bank_free[bank(job)], 1)

            def take_ro(c):
                M = MT[c]
                for z in range(2):
                    job = ("ro", c, z)
                    take(job, (heads(retR[0:M, c])[:, z::2], heads(ps(job)[0:M, 0:256])[:, z::2]))

            def conv_norm(m):
                M = MT[m]
                take(("cv", m), (convR[0:M, m], ps(("cv", m))[0:M, 0:256]))
                normed(seen, convR[0:M, m], convR[0:M, m], 1, CC, mv[0:M, 0], stats[0:M], rstd[0:M, 0:1])
                seen(VE.tensor_tensor(convR[0:M, m], convR[0:M, m], vecs[0:M, 0], MUL))
                VE.tensor_tensor(convR[0:M, m], convR[0:M, m], vecs[0:M, 1], ADD).then_inc(convn_in, 1)

            dve.wait_ge(vec_in, 16)
            for c in range(2):
                if c:
                    full(dve, ("rS", 0))
                VE.tensor_tensor(heads(kd), heads(rkR[:, c]), const("kdec").unsqueeze(2).to_broadcast([128, RH, 64]), MUL)\
                    .then_inc(kd_ready, 1)
                if c:
                    full(dve, ("ro", 0, 1))
                    VE.tensor_tensor(q_dec, uT[:, TRQ:TRQ + 2, 128:256], const("qdec", 2, 128), MUL).then_inc(qd_ready, 1)
                weigh(c, const("dmask", RH, 128))
                take_ro(c)
                job = ("rS", c)
                if c == 0:
                    take(job, (S1, ps(job)[:, 0:128].rearrange("p (h e) -> p h e", h=2)))
                else:
                    full(dve, job)
                    for hp in range(2):
                        last = VE.scalar_tensor_tensor(out=S2[:, hp], in0=S1[:, hp], scalar=const("cdec")[:, hp:hp + 1],
                                                       in1=ps(job)[:, hp * 64:hp * 64 + 64], op0=MUL, op1=ADD)
                    last.then_inc(bank_free[bank(job)], 1)
                if c == 0:
                    conv_norm(0)
            VE.tensor_tensor(heads(kd[0:64]), heads(rkR[0:64, 2]), const("kdec_s")[0:64].unsqueeze(2).to_broadcast([64, RH, 64]), MUL)
            for hp in range(2):
                VE.tensor_tensor(q_wide[:, hp], uT[:, TRQ + hp, NPR:NT].unsqueeze(1).to_broadcast([128, NB, 64]),
                                 const("qmask", 2, NB, 64)[:, hp], MUL)
            for hh in range(RH):
                last = VE.tensor_tensor(v_wide[0:64, hh], rvR[0:64, 2, hh * 64:hh * 64 + 64].unsqueeze(1).to_broadcast([64, NB, 64]),
                                        const("bmask")[0:64].unsqueeze(2).to_broadcast([64, NB, 64]), MUL)
            last.then_inc(rets_ready, 1)
            weigh(2, const("dmask_s", RH, 64))
            take_ro(2)
            conv_norm(1)
            conv_norm(2)
            for z in range(2):
                job = ("ri", z)
                full(dve, job)
                o = heads(retR[0:64, 2])[:, z::2]
                VE.tensor_tensor(o, o, heads(ps(job)[0:64, 0:256])[:, z::2], ADD).then_inc(bank_free[bank(job)], 1)
                freed(dve, job)
            dve.wait_ge(sin_in, 16)
            for hp in range(2):
                job = ("rS_s", hp)
                full(dve, job)
                VE.scalar_tensor_tensor(out=s_in[:, hp], in0=s_in[:, hp], scalar=const("cdec_s")[:, hp:hp + 1],
                                        in1=ps(job).rearrange("p (b e) -> p b e", b=NB), op0=MUL, op1=ADD)\
                    .then_inc(bank_free[bank(job)], 1)
            dve.wait_ge(ret_e, 2)
            for m in range(3):
                M = MT[m]
                seen(VE.tensor_tensor(sig[0:M, m], sig[0:M, m], rgR[0:M, m], MUL))
                for hh in range(RH):
                    last = VE.bn_stats(stats[0:M, hh], retR[0:M, m, hh * 64:hh * 64 + 64])
                seen(last)
                for hh in range(RH):
                    last = VE.bn_aggr(mv[0:M, hh], stats[0:M, hh])
                seen(last)
                inverse_root(seen, rstd[0:M], mv[0:M, :, 1])
                for hh in range(RH):
                    x = retR[0:M, m, hh * 64:hh * 64 + 64]
                    last = VE.tensor_scalar(x, x, mv[0:M, hh, 0:1], rstd[0:M, hh:hh + 1], SUB, MUL)
                seen(last)
                seen(VE.tensor_tensor(retR[0:M, m], retR[0:M, m], vecs[0:M, 2], MUL))
                last = VE.tensor_tensor(retR[0:M, m], retR[0:M, m], sig[0:M, m], MUL)
                last.then_inc(ret_done, 1)
            for m in range(3):
                M = MT[m]
                dve.wait_ge(conv_sig, m + 1)
                VE.tensor_tensor(convR[0:M, m], convR[0:M, m], sig[0:M, m], MUL).then_inc(mix_ready, 1)
            for m in range(3):
                M, job = MT[m], ("mx", m)
                t = slice(m * 128, m * 128 + M)
                b = ps(job).rearrange("p (k n) -> p k n", k=4)
                take(job, (mixT[:, 0:2, t], b[:, 0:2, 0:M]), (mixT[:, 6:8, t], b[:, 2:4, 0:M]))

            dve.wait_ge(xrow_in, 32)
            dve.wait_ge(ln1_in, 16)
            dve.wait_ge(states_out, 32)
            for m in range(3):
                M = MT[m]
                for c in range(2):
                    job = ("wo", m, c)
                    full(dve, job)
                    z = acc[0:M, m, c * 512:c * 512 + 512]
                    VE.scalar_tensor_tensor(out=z, in0=z, scalar=ALPHA, in1=ps(job)[0:M], op0=MUL, op1=ADD).then_inc(bank_free[bank(job)], 1)
                    freed(dve, job)
                normed(seen, acc[0:M, m], h[0:M, m], 2, D, mv2[0:M], stats2[0:M], rstd2[0:M])
                seen(VE.tensor_tensor(h[0:M, m], h[0:M, m], ln[0:M, 0], MUL))
                VE.tensor_tensor(h[0:M, m], h[0:M, m], ln[0:M, 1], ADD).then_inc(h_ready, 1)
            dve.wait_ge(h_ready, 3)
            full(dve, ("wo", 2, 1))
            for m in range(3):
                for c in range(2):
                    job = ("hT", m, c)
                    M = MT[m]
                    take(job, (hT[:, 4 * c:4 * c + 4, m * 128:m * 128 + M], ps(job).rearrange("p (k n) -> p k n", k=4)[:, :, 0:M]))
            dve.wait_ge(moe_in, 16 * 5)
            for m in range(3):
                M, job = MT[m], ("router", m)
                full(dve, job)
                VE.tensor_tensor(lg[0:M], ps(job)[0:M, 0:NE], br[0:M], ADD).then_inc(bank_free[bank(job)], 1)
                freed(dve, job)
                seen(VE.max(top8[0:M], lg[0:M]))
                seen(VE.max_index(top_i[0:M, m, :], top8[0:M], lg[0:M]))
                seen(VE.tensor_copy(idxf[0:M], top_i[0:M, m, :]))
                VE.tensor_scalar(r1[0:M, 0:1], top8[0:M, 0:1], -1.0, None, MUL).then_inc(top_ready, 1)
                seen(VE.memset(Mk[0:M, m], 0.0))
                seen(VE.memset(G[0:M, m], 0.0))
                for k in range(TOPK):
                    last = VE.scalar_tensor_tensor(out=Mk[0:M, m], in0=const("iota")[0:M, 0:NE], scalar=idxf[0:M, k:k + 1], in1=Mk[0:M, m],
                                                   op0=ALU.is_equal, op1=ADD)
                    if k < TOPK - 1:
                        seen(last)
                last.then_inc(mask_ready, 1)
                dve.wait_ge(top_exp, m + 1)
                seen(VE.reciprocal(r1[0:M, 2:3], r1[0:M, 1:2]))
                seen(VE.tensor_scalar(g4[0:M, 0:4], g4[0:M, 0:4], r1[0:M, 2:3], None, MUL))
                for k in range(TOPK):
                    seen(VE.tensor_scalar(etmp[0:M], const("iota")[0:M, 0:NE], idxf[0:M, k:k + 1], g4[0:M, k:k + 1], ALU.is_equal, MUL))
                    seen(VE.tensor_tensor(G[0:M, m], G[0:M, m], etmp[0:M], ADD))
            for m in range(3):
                M = MT[m]
                for c in range(2):
                    cols = slice(c * 512, c * 512 + 512)
                    freed(dve, ("plg", m, c))
                    s = sg[0:M, 0:512]
                    job = ("ple", m, c)
                    full(dve, job)
                    VE.tensor_tensor(acc[0:M, m, cols], s, ps(job)[0:M], MUL).then_inc(bank_free[bank(job)], 1)
                    freed(dve, job)
                    seen(VE.scalar_tensor_tensor(out=acc[0:M, m, cols], in0=h[0:M, m, cols], scalar=ALPHA,
                                                 in1=acc[0:M, m, cols], op0=MUL, op1=ADD))
            seen(VE.memset(rank_all, -1e4))
            seen(VE.memset(gate_all, 0.0))
            for m in range(3):
                M, job = MT[m], ("rank", m)
                full(dve, job)
                VE.scalar_tensor_tensor(out=lg[0:M], in0=ps(job)[0:M, 0:NE], scalar=1e4, in1=Mk[0:M, m], op0=ADD, op1=MUL)\
                    .then_inc(bank_free[bank(job)], 1)
                freed(dve, job)
                for r in range(ROUNDS):
                    VE.tensor_scalar(rank_all[0:M, m, r * NE:(r + 1) * NE], lg[0:M], -1e4 - CAP * r, None, ADD)
                    last = VE.tensor_copy(gate_all[0:M, m, r * NE:(r + 1) * NE], G[0:M, m])
                seen(last)
            job = ("count",)
            full(dve, job)
            seen(VE.memset(few, 0.0))
            for n in range(ROUNDS):
                last = VE.tensor_scalar(few[:, n * NE:(n + 1) * NE], ps(job)[:, 0:NE], float(CAP * n + CAP // 2), -1.0, ALU.is_gt, ADD)
            seen(last)
            seen(VE.tensor_scalar(slot_no[:, 0:NI + 8], few, 1.0, None, ADD))
            seen(VE.tensor_copy(many_i[0:1, 0:NI + 8], slot_no[0:1, 0:NI + 8]))
            VE.memset(slot_fold[:, 0:64], 0.0)
            VE.memset(slot_fold[:, 64:128], 64.0)
            VE.tensor_scalar(turn_fold[:, 0:64], ident[:, 64:128], -1.0, None, MUL)
            seen(VE.tensor_scalar(turn_fold[:, 64:128], ident[:, 0:64], -1.0, None, MUL))
            VE.tensor_reduce(r1[:, 3:4], ps(job)[:, 0:NE], AX, MAXOP).then_inc(bank_free[bank(job)], 1)
            freed(dve, job)
            seen(VE.tensor_scalar(lg[:, 0:ROUNDS], const("iota")[:, 0:ROUNDS], float(CAP), r1[:, 3:4], MUL, ALU.is_lt))
            seen(VE.tensor_reduce(r1[:, 4:5], lg[:, 0:ROUNDS], AX, ADD))
            seen(VE.tensor_scalar(r1[:, 4:5], r1[:, 4:5], float(NE), None, MUL))
            VE.tensor_copy(items_i[0:1, 0:1], r1[0:1, 4:5]).then_inc(items_ready, 1)
            take(("GT",), (GTs[0:NE], ps(("GT",))[0:NE, 0:NT]))
            for m in range(3):
                M = MT[m]
                for c in range(2):
                    job = ("bd", m, c)
                    full(dve, job)
                    a = acc[0:M, m, c * 512:c * 512 + 512]
                    VE.tensor_tensor(a, a, ps(job)[0:M], ADD).then_inc(bank_free[bank(job)], 1)
                    freed(dve, job)

            def choose(out, i, gated, m):
                M = MT[m]
                rank = rank_all[0:M, m, bass.ds(i, 1)]
                if gated:
                    return VE.tensor_scalar(out[0:M, m], slot_no[0:M], rank, gate_all[0:M, m, bass.ds(i, 1)], ALU.is_equal, MUL)
                return VE.tensor_scalar(out[0:M, m], slot_no[0:M], rank, None, ALU.is_equal)

            def number_slots(seen, i):
                seen(VE.scalar_tensor_tensor(out=slot_no, in0=slot_fold, scalar=few[:, bass.ds(i, 1)], in1=const("iota"), op0=MUL, op1=ADD))

            number_slots(seen, 0)
            for m in range(3):
                last = choose(P, 0, False, m)
            last.then_inc(P_ready, 1)
            dve.wait_ge(rows_out, 16 * 13)
            VE.memset(gate_col, 0.0)
            VE.memset(y_hi.bitcast(f32), 0.0).then_inc(y_ready, 1)
            VE.memset(PT01.bitcast(f32), 0.0).then_inc(PT_ready, 1)
            VE.memset(r1[:, 6:7], 0.0).then_inc(chunk_used, 3)

            def low(i, c):
                dve.wait_ge(hi_ready, i * 12 + (c + 1))
                VE.tensor_tensor(w_lo[:, c % 3, 0:DVE_COLS], chunk_in[c % 6][:, 0:DVE_COLS], w_hi[:, c % 3, 0:DVE_COLS].bitcast(f32), SUB)\
                    .then_inc(lo_ready, 2 if c == POOL_CHUNK + 1 else 1)

            def low_parts(x, hi, lo, many_slots, hi_there, count, ready):
                with dve.If(many_slots > 0):
                    dve.wait_ge(hi_there, count)
                    VE.tensor_tensor(lo, x, hi.bitcast(f32), SUB).then_inc(ready, 1)
                with dve.If(many_slots < 1):
                    dve.wait_ge(hi_there, count)
                    VE.tensor_tensor(hi[:, :, CAP // 2:], x[:, :, CAP // 2:], hi[:, :, CAP // 2:].bitcast(f32), SUB).then_inc(ready, 1)

            def gathered_low(i1, many_slots):
                low_parts(psum[:, 6:8, :].rearrange("p a (k n) -> p (a k) n", n=CAP), x_hi, x_lo, many_slots,
                          xg_ready, i1, xlo_ready)

            def weighted_low(i):
                dve.wait_ge(y_ready, i + 1)
                VE.scalar_tensor_tensor(out=y_lo.rearrange("p (c n) -> p c n", c=2), in0=psum[:, 4:6, :], scalar=gate_col,
                                        in1=y_hi.rearrange("p (c n) -> p c n", c=2).bitcast(f32), op0=MUL, op1=SUB).then_inc(ylo_ready, 1)

            for c in range(3):
                low(0, c)
            dve.wait_ge(items_ready, 1)
            gathered_low(1, dve.value_load(many_i[0:1, 0:1], min_val=0, max_val=1))
            n_items = dve.value_load(items_i[0:1, 0:1], min_val=NE, max_val=NI)
            LINKS = 10

            def add_item(i, m):
                dve.wait_ge(scattered, i * 3 + (m + 1))
                a = acc[0:MT[m], m].rearrange("p (c n) -> p c n", c=2)
                at = (6, 4, 6)[m]
                VE.tensor_tensor(a, a, psum[0:MT[m], at:at + 2, :], ADD).then_inc(added, 1)

            with dve.Fori(0, ROUNDS) as r:
                with dve.If(n_items > r * NE):
                    with dve.Fori(0, NE) as e:
                        i = r * NE + e
                        lseen = steps(dve, dve_loop, i * LINKS)
                        many_here = dve.value_load(many_i[0:1, bass.ds(i, 1)], min_val=0, max_val=1)
                        many_next = dve.value_load(many_i[0:1, bass.ds(i + 1, 1)], min_val=0, max_val=1)
                        low(i, 3)
                        VE.scalar_tensor_tensor(out=turner, in0=turn_fold, scalar=few[:, bass.ds(i, 1)], in1=ident, op0=MUL, op1=ADD)
                        choose(PG, i, True, 0)
                        low(i, 4)
                        choose(PG, i, True, 1)
                        lseen(choose(PG, i, True, 2))
                        low(i, 5)
                        number_slots(lseen, i + 1)
                        dve.wait_ge(gathered, i + 1)
                        choose(P, i + 1, False, 0)
                        low(i, 6)
                        choose(P, i + 1, False, 1)
                        choose(P, i + 1, False, 2).then_inc(P_ready, 1)
                        low(i, 7)
                        weighted_low(i)
                        low(i, 8)
                        low(i, 9)
                        add_item(i, 0)
                        add_item(i, 1)
                        bias = bup[:, bass.ds(e, 1)].rearrange("p a (s j) -> p (a s) j", s=2)

                        def gate_part(half_):
                            js = slice(4 * half_, 4 * half_ + 4)
                            dve.wait_ge(hu_turned, i * 2 + (half_ + 1))
                            lseen(VE.tensor_tensor(gg[:, js], psum[:, 2 * half_, :].rearrange("p (j n) -> p j n", j=4),
                                                   bias[:, 0, js].unsqueeze(2).to_broadcast([128, 4, CAP]), ADD))
                            VE.tensor_scalar(gg[:, js], gg[:, js], LIMIT, None, ALU.min).then_inc(g_ready, 1)

                        def up_part(half_):
                            js = slice(4 * half_, 4 * half_ + 4)
                            lseen(VE.tensor_tensor(uu[:, js], psum[:, 2 * half_ + 1, :].rearrange("p (j n) -> p j n", j=4),
                                                   bias[:, 1, js].unsqueeze(2).to_broadcast([128, 4, CAP]), ADD))
                            lseen(VE.tensor_scalar(uu[:, js], uu[:, js], LIMIT, -LIMIT, ALU.min, MAXOP))
                            lseen(VE.scalar_tensor_tensor(out=uu[:, js], in0=uu[:, js], scalar=1.0, in1=gg[:, js], op0=ADD, op1=MUL))
                            dve.wait_ge(e_ready, i * 2 + (half_ + 1))
                            VE.tensor_tensor(act_sb[:, js], uu[:, js], act_sb[:, js], MUL).then_inc(act_ready, 1)

                        def hidden_low(half_):
                            js = slice(4 * half_, 4 * half_ + 4)
                            low_parts(act_sb[:, js], act_hi[:, js], act_lo[:, js], many_here,
                                      act_hi_ready, i * 2 + (half_ + 1), act_lo_ready)

                        gate_part(0)
                        add_item(i, 2)
                        up_part(0)
                        dve.wait_ge(PGT_ready, i + 1)
                        VE.tensor_scalar(PT01.rearrange("p m n -> p (m n)")[:, 0:NT], PGT[:, 0:NT], 0.0, None, ALU.is_gt)\
                            .then_inc(PT_ready, 1)
                        gate_part(1)
                        hidden_low(0)
                        up_part(1)
                        hidden_low(1)
                        low(i, 11)
                        gathered_low(i + 2, many_next)
                        for c in range(12, 15):
                            low(i, c)
                        assert lseen.count[0] == LINKS
            weighted_low(n_items)
            for m in range(3):
                add_item(n_items, m)
            tail = steps(dve, dve_tail)
            dve.wait_ge(added, n_items * 3 + 3)
            dve.wait_ge(ln2_in, 16)
            for m in range(3):
                M = MT[m]
                a = acc[0:M, m]
                normed(tail, a, a, 2, D, mv2[0:M], stats2[0:M], rstd2[0:M])
                tail(VE.tensor_tensor(a, a, ln2[0:M, 0], MUL))
                VE.tensor_tensor(a, a, ln2[0:M, 1], ADD).then_inc(y_out, 1)

        @block.gpsimd
        def _(pool):
            seen = steps(pool, pool_step)
            pool.wait_ge(ids_in, 16)
            pool.wait_ge(x_in, 16)
            page_loads = page_loader(pool)
            for b in range(4):
                sel_load(page_loads, b)
                if b == 3:
                    full(pool, ("proj", NTILE - 1))
                window_load(pool, b)
            pool.wait_ge(conv_in, 48)
            pool.wait_ge(conv_ready, 1)
            full(pool, ("rowsC", 2))
            for k in range(2):
                parts = [(convY[:, k, 0:NPR], conv_t, lambda t, k=k: convP[:, k, t:t + NPR]),
                         (convY[:, k, NPR:NT].rearrange("p (b t) -> p b t", t=TS),
                          conv_t[:, 0:NSM].rearrange("p (b t) -> p b t", t=TS), lambda t, k=k: convS[:, k, :, t:t + TS])]
                for dst, tmp, src in parts:
                    seen(GE.tensor_scalar(dst, src(0), conv_w[:, k, 0:1], conv_w[:, k, CK:CK + 1], MUL, ADD))
                    for t in range(1, CK):
                        seen(GE.tensor_scalar(tmp, src(t), conv_w[:, k, t:t + 1], None, MUL))
                        seen(GE.tensor_tensor(dst, dst, tmp, ADD))
            pool.dma_start(O["conv_p"], convP[:, :, NPR:NPR + CK - 1]).then_inc(conv_out, 16)
            for k in range(2):
                pool.dma_start(O["conv_s"][:, k], convS[:, k, :, TS:TS + CK - 1]).then_inc(conv_out, 16)
            pool.dma_start(O["win_s"][:, 0:WIN - TS], A["cache_win"][:, TS:WIN]).then_inc(wincopy_out, 16)
            for m in range(3):
                for w in ("rowsA", "rowsB"):
                    freed(pool, (w, m))
            for m in range(2):
                pool.dma_start(O["nsa_p"][m * 128:m * 128 + 128], kvR[:, m, 0:4]).then_inc(rows_out, 16)
                pool.dma_start(O["win_p"][m * 128:m * 128 + 128], kvR[:, m, 4:6]).then_inc(rows_out, 16)
            pool.dma_start(O["nsa_s"], kvR[0:64, 2, 0:4]).then_inc(rows_out, 16)
            for b in range(NB):
                rows = kvR[b * TS:(b + 1) * TS, 2, 4:6].rearrange("p a b -> p (a b)")
                pool.dma_start(O["win_s"][b, WIN - TS:WIN], rows).then_inc(rows_out, 16)
            freed(pool, ("rS", 1))
            pool.dma_start(O["ret_p"], S2).then_inc(states_out, 16)
            freed(pool, ("rS_s", 0))
            freed(pool, ("rS_s", 1))
            pool.dma_start(O["ret_s"], s_in).then_inc(states_out, 16)
            def low(i, c, start=DVE_COLS):
                pool.wait_ge(hi_ready, i * 12 + (c + 1))
                GE.tensor_tensor(w_lo[:, c % 3, start:], chunk_in[c % 6][:, start:], w_hi[:, c % 3, start:].bitcast(f32), SUB)\
                    .then_inc(lo_ready2, 1)

            for c in range(3):
                low(0, c)
            pool.wait_ge(items_ready, 1)
            n_items = pool.value_load(items_i[0:1, 0:1], min_val=NE, max_val=NI)
            with pool.Fori(0, ROUNDS) as r:
                with pool.If(n_items > r * NE):
                    with pool.Fori(0, NE) as e:
                        i = r * NE + e
                        for c in range(3, 10):
                            low(i, c)
                        low(i, POOL_CHUNK, 0)
                        for c in range(11, 15):
                            low(i, c)
            for m in range(3):
                pool.wait_ge(y_out, m + 1)
                pool.dma_start(O["y"][m * 128:m * 128 + MT[m]], acc[0:MT[m], m]).then_inc(y_stored, 16)
            pool.wait_ge(conv_out, 48)
            pool.wait_ge(wincopy_out, 16)
            pool.wait_ge(rows_out, 16 * 13)
            pool.wait_ge(states_out, 32)
            pool.wait_ge(y_stored, 48)
    return nc


def lay_out(x):
    import numpy as np
    c = np.ascontiguousarray
    a = {k: np.asarray(v) for k, v in x.items()}
    rows = np.concatenate([a["x_prompt"].reshape(NPR, D), a["x_sample"].reshape(NSM, D)])
    pr = np.concatenate([a["p_prompt"].reshape(NPR, PLE), a["p_sample"].reshape(NSM, PLE)])
    w = a["w_in"][0]
    at = {}
    o = 0
    for name, n in (("a", 256), ("g", 256), ("q", 512), ("kv", 768), ("gate", 24), ("rq", 256), ("rk", 256), ("rv", 256), ("rg", 256)):
        at[name] = w[:, o:o + n]
        o += n
    q = at["q"].reshape(D, KV, GQ, HD)
    kv = at["kv"].reshape(D, 6, 128)
    cols = [q[:, :, i].reshape(D, 128) for i in range(4)] + [kv[:, 0], kv[:, 2], kv[:, 4]]
    cols += [at["rq"], at["rk"], at["a"], at["g"], kv[:, 1], kv[:, 3], kv[:, 5], at["gate"], np.zeros((D, 104), w.dtype), at["rv"], at["rg"]]
    cols = np.concatenate(cols, 1)
    assert cols.shape == (D, NTILE * 128)
    w_in = cols.reshape(KT, 128, NTILE, 128).transpose(2, 1, 0, 3)
    cache = a["cache_nsa_kv"][0].reshape(-1, PAGE, 4, 128)
    pages = np.stack([cache[:, :, 0].transpose(0, 2, 1), cache[:, :, 1].transpose(0, 2, 1),
                      cache[:, :, 2].transpose(0, 2, 1), cache[:, :, 3]], 2)
    wk = a["cache_win_kv"][0].reshape(NB, WIN, 2, 128)
    windows = np.stack([wk[:, :, 0].transpose(0, 2, 1),
                        wk[:, :, 1].reshape(NB, 4, 128, 128).transpose(0, 2, 1, 3).reshape(NB, 128, 512)], 2)
    wo = a["w_out"][0]
    att = wo[256:768].reshape(KV, GQ, HD, D).transpose(1, 0, 2, 3).reshape(512, D)
    wo = np.concatenate([wo[:256], att, wo[768:]])

    def ktiles(m):
        return m.reshape(-1, 128, m.shape[1]).transpose(1, 0, 2)

    def spread(v):
        return np.broadcast_to(v, (128,) + v.shape)

    early, late = constants()
    cw = np.concatenate([a["conv_w"][0], a["conv_b"][0][None]])
    out = dict(
        xT=ktiles(c(rows.T)), pT=ktiles(c(pr.T)), x_rows=rows, w_in=w_in, pages=pages.reshape(len(cache), 128, 512),
        windows=windows, cache_win=wk.reshape(NB, WIN, 256), page_table=a["page_table"].reshape(1, -1),
        w_out=ktiles(wo), w_plg=ktiles(a["w_plg"][0]), w_ple=ktiles(a["w_ple"][0]), w_router=ktiles(a["w_router"][0]),
        b_router=spread(a["b_router"][0]), b_down=a["b_down"][0], w_up=a["w_up"][0], w_down=a["w_down"][0],
        b_up=a["b_up"][0].reshape(NE, 8, 128, 2).transpose(2, 0, 3, 1).reshape(128, NE, 16),
        state_conv=a["state_conv"][0].transpose(2, 0, 1).reshape(2, 128, NB, CK - 1).transpose(1, 0, 2, 3),
        conv_w=cw.T.reshape(2, 128, CK + 1).transpose(1, 0, 2),
        state_ret=a["state_ret"][0].reshape(NB, 2, 2, 64, 64).transpose(2, 3, 1, 0, 4).reshape(128, 2, NB, 64),
        vecs=spread(np.stack([a["conv_ln_g"][0], a["conv_ln_b"][0], a["ret_norm_g"][0]])),
        ln=spread(np.stack([a["ln1_g"][0], a["ln1_b"][0], a["ln2_g"][0], a["ln2_b"][0]])),
        early=early, late=late)
    return {k: c(v) for k, v in out.items()}


OUTPUTS = dict(y=(NT, D), nsa_p=(NPR, 4, 128), nsa_s=(NSM, 4, 128), win_p=(NPR, 2, 128), win_s=(NB, WIN, 256),
               ret_p=(128, 2, 64), ret_s=(128, 2, NB, 64), conv_p=(128, 2, CK - 1), conv_s=(128, 2, NB, CK - 1))


def kernel(**inputs):
    import numpy as np
    import concourse.bacc as bacc
    from concourse import mybir
    from concourse.bass_utils import run_bass_kernel_spmd

    arrays = lay_out(inputs)
    nc = bacc.Bacc("TRN2", target_bir_lowering=False, num_devices=1)
    A = {k: nc.dram_tensor(f"in_{k}", v.shape, mybir.dt.from_np(v.dtype), kind="ExternalInput").ap() for k, v in arrays.items()}
    O = {k: nc.dram_tensor(f"out_{k}", s, mybir.dt.float32, kind="ExternalOutput").ap() for k, s in OUTPUTS.items()}
    build(nc, A, O)
    run = run_bass_kernel_spmd(nc, [{f"in_{k}": v for k, v in arrays.items()}], core_ids=[0])
    o = {k: np.asarray(run.results[0][f"out_{k}"]) for k in OUTPUTS}
    ret_s = o["ret_s"].reshape(2, 64, 2, NB, 64).transpose(3, 2, 0, 1, 4).reshape(1, NB, RH, 64, 64)
    ret_p = o["ret_p"].reshape(2, 64, 2, 64).transpose(2, 0, 1, 3).reshape(1, 1, RH, 64, 64)
    conv_p = o["conv_p"].transpose(2, 1, 0).reshape(1, 1, CK - 1, CC)
    conv_s = o["conv_s"].transpose(2, 3, 1, 0).reshape(1, NB, CK - 1, CC)
    return (o["y"][:NPR].reshape(1, NPR, D), o["y"][NPR:].reshape(NB, TS, D),
            o["nsa_p"].reshape(1, 1, NPR, 4, KV, HD), o["nsa_s"].reshape(1, NB, TS, 4, KV, HD),
            o["win_p"].reshape(1, 1, NPR, 2, KV, HD), o["win_s"].reshape(1, NB, WIN, 2, KV, HD),
            np.ascontiguousarray(ret_p), np.ascontiguousarray(ret_s), np.ascontiguousarray(conv_p), np.ascontiguousarray(conv_s))
```
